# Optimizing a Trainium2 kernel written in Bass

```python
import math
import jax, jax.numpy as jnp
from jax import lax
import numpy as np

D_MODEL = 1024
BATCH = 1
SEQ = 256
DEPTH = 2

HEAD_DIM = 64
NSA_HEADS = 8
NSA_GROUPS = 2
NSA_HPG = NSA_HEADS // NSA_GROUPS
CMP_LEN = 32
CMP_STRIDE = 16
CMP_HIDDEN = 256
SEL_BLK = 64
N_SEL = 16
WINDOW = 512
DSA_HEADS = 8
DSA_KV_RANK = 128
IDX_HEADS = 8
IDX_DIM = 64
DSA_TOPK = 256
DIFF_HEADS = 8
DIFF_DIM = 64
D_FF = 4 * D_MODEL
NUM_BUCKETS = 32
MAX_DISTANCE = 128
REL_HEADS = NSA_HEADS + DSA_HEADS
QBLK = 128
N_EVEN = (DEPTH + 1) // 2
N_ODD = DEPTH // 2
ALPHA = (2 * DEPTH) ** 0.25
BETA = (8 * DEPTH) ** -0.25
NEG_INF = -1e30
BIG = 1e9
EPS = 1e-5
NSA_Q = NSA_HEADS * HEAD_DIM
NSA_KV = 2 * NSA_GROUPS * HEAD_DIM
NSA_GATE = NSA_HEADS * 3
DSA_Q = DSA_HEADS * HEAD_DIM
EVEN_SIZES = (NSA_Q, NSA_KV, NSA_KV, NSA_KV, NSA_GATE, DSA_Q, DSA_KV_RANK, IDX_HEADS * IDX_DIM, IDX_DIM, IDX_HEADS)
EVEN_IN = sum(EVEN_SIZES)
EVEN_OUT = NSA_Q + DSA_HEADS * HEAD_DIM
ODD_IN = 3 * DIFF_HEADS * 2 * DIFF_DIM
ODD_OUT = DIFF_HEADS * 2 * DIFF_DIM


def _split(x, sizes):
    offs = np.cumsum(sizes)[:-1].tolist()
    return jnp.split(x, offs, axis=-1)

def layer_norm(x, g, b):
    xf = x.astype(jnp.float32)
    mu = jnp.mean(xf, axis=-1, keepdims=True)
    var = jnp.mean(jnp.square(xf - mu), axis=-1, keepdims=True)
    return ((xf - mu) * lax.rsqrt(var + EPS) * g + b).astype(x.dtype)

def rms_norm(x, g):
    xf = x.astype(jnp.float32)
    return (xf * lax.rsqrt(jnp.mean(jnp.square(xf), axis=-1, keepdims=True) + EPS) * g).astype(x.dtype)

def masked_softmax(logits, mask):
    z = jnp.where(mask, logits.astype(jnp.float32), NEG_INF)
    z = z - jnp.max(z, axis=-1, keepdims=True)
    e = jnp.where(mask, jnp.exp(z), 0.0)
    return e / jnp.maximum(jnp.sum(e, axis=-1, keepdims=True), 1e-30)

def t5_bucket(dist):
    n = jnp.maximum(dist, 0)
    exact = NUM_BUCKETS // 2
    nf = jnp.maximum(n, 1).astype(jnp.float32)
    large = exact + (jnp.log(nf / exact) / math.log(MAX_DISTANCE / exact) * (NUM_BUCKETS - exact)).astype(jnp.int32)
    return jnp.where(n < exact, n, jnp.minimum(large, NUM_BUCKETS - 1))

def sweep_query_blocks(fn, B, S):
    out = lax.map(fn, jnp.arange(S // QBLK))
    return jnp.moveaxis(out, 0, 1).reshape(B, S, -1)

def nsa_compress(k_raw, pe, w1, w2):
    B, S, G, Dh = k_raw.shape
    nc = (S - CMP_LEN) // CMP_STRIDE + 1
    idx = np.arange(nc)[:, None] * CMP_STRIDE + np.arange(CMP_LEN)[None, :]
    blk = k_raw[:, idx] + pe[:, None, :]
    blk = blk.transpose(0, 1, 3, 2, 4).reshape(B, nc, G, CMP_LEN * Dh)
    return jax.nn.gelu(blk @ w1) @ w2

def nsa_attention(q, kvc, kvs, kvw, gate_logits, pe_k, pe_v, w1_k, w2_k, w1_v, w2_v, bias_tab):
    B, S = q.shape[:2]
    G, HPG, Dh = NSA_GROUPS, NSA_HPG, HEAD_DIM
    q = q.reshape(B, S, G, HPG, Dh)
    kc_raw, vc_raw = [a.reshape(B, S, G, Dh) for a in jnp.split(kvc, 2, axis=-1)]
    kc = nsa_compress(kc_raw, pe_k, w1_k, w2_k)
    vc = nsa_compress(vc_raw, pe_v, w1_v, w2_v)
    ks, vs = [a.reshape(B, S, G, Dh).transpose(0, 2, 1, 3) for a in jnp.split(kvs, 2, axis=-1)]
    kw, vw = [jnp.pad(a.reshape(B, S, G, Dh), ((0, 0), (WINDOW, 0), (0, 0), (0, 0))) for a in jnp.split(kvw, 2, axis=-1)]
    gates = jax.nn.sigmoid(gate_logits.astype(jnp.float32)).astype(q.dtype).reshape(B, S, G, HPG, 3)
    nc = kc.shape[1]
    nb = S // SEL_BLK
    n_sel = min(N_SEL, nb)
    cs = np.arange(nc) * CMP_STRIDE
    ss = np.arange(nb) * SEL_BLK
    overlap = np.clip(np.minimum(cs[:, None] + CMP_LEN, ss[None, :] + SEL_BLK) - np.maximum(cs[:, None], ss[None, :]), 0, None)
    imp = jnp.asarray(overlap / CMP_STRIDE, dtype=jnp.float32)
    cmp_end = jnp.asarray(cs + CMP_LEN - 1, dtype=jnp.int32)
    tab = bias_tab.reshape(NUM_BUCKETS, G, HPG)
    scale = Dh ** -0.5
    bi = jnp.arange(B)[:, None, None, None]
    gi = jnp.arange(G)[None, :, None, None]
    jblk = jnp.arange(nb)

    def block(qb):
        q0 = qb * QBLK
        t = q0 + jnp.arange(QBLK)
        qq = lax.dynamic_slice_in_dim(q, q0, QBLK, axis=1)
        gg = lax.dynamic_slice_in_dim(gates, q0, QBLK, axis=1)
        dc = t[:, None] - cmp_end[None, :]
        bias_c = tab[t5_bucket(dc)].transpose(2, 3, 0, 1)
        lc = jnp.einsum('bqghd,bngd->bghqn', qq, kc) * scale + bias_c
        pc = masked_softmax(lc, dc >= 0)
        oc = jnp.einsum('bghqn,bngd->bqghd', pc.astype(vc.dtype), vc)
        score = jnp.einsum('bghqn,nj->bgqj', pc, imp)
        cb = (t // SEL_BLK)[:, None]
        allowed = jblk[None, :] * SEL_BLK <= t[:, None]
        forced = (jblk[None, :] == 0) | (jblk[None, :] == cb) | (jblk[None, :] == cb - 1)
        score = jnp.where(forced, BIG, jnp.where(allowed, score, -BIG))
        _, sel = lax.top_k(score, n_sel)
        tok = (sel[..., None] * SEL_BLK + jnp.arange(SEL_BLK)).reshape(B, G, QBLK, n_sel * SEL_BLK)
        k_sel = ks[bi, gi, tok]
        v_sel = vs[bi, gi, tok]
        dist = t[None, None, :, None] - tok
        bias_s = tab[t5_bucket(dist), gi].transpose(0, 1, 4, 2, 3)
        ls = jnp.einsum('bqghd,bgqtd->bghqt', qq, k_sel) * scale + bias_s
        ps = masked_softmax(ls, (dist >= 0)[:, :, None])
        o_s = jnp.einsum('bghqt,bgqtd->bqghd', ps.astype(v_sel.dtype), v_sel)
        kwb = lax.dynamic_slice_in_dim(kw, q0, WINDOW + QBLK, axis=1)
        vwb = lax.dynamic_slice_in_dim(vw, q0, WINDOW + QBLK, axis=1)
        s = q0 - WINDOW + jnp.arange(WINDOW + QBLK)
        dw = t[:, None] - s[None, :]
        mask_w = (dw >= 0) & (dw < WINDOW) & (s[None, :] >= 0)
        bias_w = tab[t5_bucket(dw)].transpose(2, 3, 0, 1)
        lw = jnp.einsum('bqghd,bsgd->bghqs', qq, kwb) * scale + bias_w
        pw = masked_softmax(lw, mask_w)
        o_w = jnp.einsum('bghqs,bsgd->bqghd', pw.astype(vwb.dtype), vwb)
        out = gg[..., 0:1] * oc + gg[..., 1:2] * o_s + gg[..., 2:3] * o_w
        return out.reshape(B, QBLK, G * HPG * Dh)

    return sweep_query_blocks(block, B, S)

def dsa_attention(q, kv_lat, iq, ik, iw, kv_norm, w_uk, w_uv, bias_tab):
    B, S = q.shape[:2]
    ckv = rms_norm(kv_lat, kv_norm)
    q_lat = jnp.einsum('bshd,rhd->bshr', q, w_uk)
    iq = iq.reshape(B, S, IDX_HEADS, IDX_DIM)
    iw = iw * (IDX_HEADS ** -0.5 * IDX_DIM ** -0.5)
    topk = min(DSA_TOPK, S // 4)
    scale = HEAD_DIM ** -0.5
    bi = jnp.arange(B)[:, None, None]
    spos = jnp.arange(S)

    def block(qb):
        q0 = qb * QBLK
        t = q0 + jnp.arange(QBLK)
        iqb = lax.dynamic_slice_in_dim(iq, q0, QBLK, axis=1)
        iwb = lax.dynamic_slice_in_dim(iw, q0, QBLK, axis=1)
        qlb = lax.dynamic_slice_in_dim(q_lat, q0, QBLK, axis=1)
        rel = jax.nn.relu(jnp.einsum('bqjd,bsd->bqjs', iqb, ik))
        isc = jnp.einsum('bqj,bqjs->bqs', iwb, rel).astype(jnp.float32)
        isc = jnp.where(spos[None, None, :] <= t[None, :, None], isc, NEG_INF)
        _, idx = lax.top_k(isc, topk)
        c_sel = ckv[bi, idx]
        dist = t[None, :, None] - idx
        bias = bias_tab[t5_bucket(dist)].transpose(0, 3, 1, 2)
        logits = jnp.einsum('bqhr,bqkr->bhqk', qlb, c_sel) * scale + bias
        p = masked_softmax(logits, (dist >= 0)[:, None])
        o_lat = jnp.einsum('bhqk,bqkr->bqhr', p.astype(c_sel.dtype), c_sel)
        o = jnp.einsum('bqhr,rhd->bqhd', o_lat, w_uv)
        return o.reshape(B, QBLK, DSA_HEADS * HEAD_DIM)

    return sweep_query_blocks(block, B, S)

def even_mixer(h, w_in, w_out, pe_k, pe_v, w1_k, w2_k, w1_v, w2_v, kv_norm, w_uk, w_uv, rel_bias):
    B, S, _ = h.shape
    nsa_q, kvc, kvs, kvw, gate, dsa_q, dsa_kv, idx_q, idx_k, idx_w = _split(h @ w_in, EVEN_SIZES)
    o_a = nsa_attention(nsa_q, kvc, kvs, kvw, gate, pe_k, pe_v, w1_k, w2_k, w1_v, w2_v, rel_bias[:, :NSA_HEADS])
    o_b = dsa_attention(dsa_q.reshape(B, S, DSA_HEADS, HEAD_DIM), dsa_kv, idx_q, idx_k, idx_w, kv_norm, w_uk, w_uv, rel_bias[:, NSA_HEADS:])
    return jnp.concatenate([o_a, o_b], axis=-1) @ w_out

def diff_mixer(h, w_in, w_out, lam, subln, rel_bias, lambda_init):
    B, S, _ = h.shape
    q, k, v = jnp.split(h @ w_in, 3, axis=-1)
    q = q.reshape(B, S, DIFF_HEADS, 2, DIFF_DIM)
    k = k.reshape(B, S, DIFF_HEADS, 2, DIFF_DIM)
    v = v.reshape(B, S, DIFF_HEADS, 2 * DIFF_DIM)
    lamf = lam.astype(jnp.float32)
    lam_full = jnp.exp(jnp.sum(lamf[0] * lamf[1])) - jnp.exp(jnp.sum(lamf[2] * lamf[3])) + lambda_init
    tab = rel_bias.reshape(NUM_BUCKETS, DIFF_HEADS, 2)
    scale = DIFF_DIM ** -0.5
    spos = jnp.arange(S)

    def block(qb):
        q0 = qb * QBLK
        t = q0 + jnp.arange(QBLK)
        qq = lax.dynamic_slice_in_dim(q, q0, QBLK, axis=1)
        dist = t[:, None] - spos[None, :]
        bias = tab[t5_bucket(dist)].transpose(2, 3, 0, 1)
        logits = jnp.einsum('bqhmd,bshmd->bhmqs', qq, k) * scale + bias
        p = masked_softmax(logits, dist >= 0)
        pd = p[:, :, 0] - lam_full * p[:, :, 1]
        o = jnp.einsum('bhqs,bshe->bqhe', pd.astype(v.dtype), v)
        o = rms_norm(o, subln) * (1.0 - lambda_init)
        return o.reshape(B, QBLK, DIFF_HEADS * 2 * DIFF_DIM)

    return sweep_query_blocks(block, B, S) @ w_out

def sq_relu_mlp(h, w1, w2):
    return jnp.square(jax.nn.relu(h @ w1)) @ w2

def modulate(x, shift, scale):
    return x * (1.0 + scale[:, None, :]) + shift[:, None, :]

def first_inputs(seed: int = 0) -> dict:
    key = jax.random.key(seed)
    ks = jax.random.split(key, 26)
    f32 = jnp.float32

    def nrm(k, shape, fan_in, s=1.0):
        return jax.random.normal(k, shape, f32) * (s * fan_in ** -0.5)

    D = D_MODEL
    return {
        "x": jax.random.normal(ks[0], (BATCH, SEQ, D), f32),
        "c": jax.random.normal(ks[1], (BATCH, D), f32),
        "rel_bias": 0.5 * jax.random.normal(ks[2], (NUM_BUCKETS, REL_HEADS), f32),
        "ada_w": nrm(ks[3], (DEPTH, D, 6 * D), D, 0.2),
        "ada_b": 0.01 * jax.random.normal(ks[4], (DEPTH, 6 * D), f32),
        "ln_g": 1.0 + 0.02 * jax.random.normal(ks[5], (DEPTH, 2, D), f32),
        "ln_b": 0.02 * jax.random.normal(ks[6], (DEPTH, 2, D), f32),
        "ev_w_in": nrm(ks[7], (N_EVEN, D, EVEN_IN), D),
        "ev_w_out": nrm(ks[8], (N_EVEN, EVEN_OUT, D), EVEN_OUT, BETA),
        "nsa_pe_k": 0.5 * jax.random.normal(ks[9], (N_EVEN, CMP_LEN, HEAD_DIM), f32),
        "nsa_pe_v": 0.5 * jax.random.normal(ks[10], (N_EVEN, CMP_LEN, HEAD_DIM), f32),
        "nsa_w1_k": nrm(ks[11], (N_EVEN, CMP_LEN * HEAD_DIM, CMP_HIDDEN), CMP_LEN * HEAD_DIM),
        "nsa_w2_k": nrm(ks[12], (N_EVEN, CMP_HIDDEN, HEAD_DIM), CMP_HIDDEN),
        "nsa_w1_v": nrm(ks[13], (N_EVEN, CMP_LEN * HEAD_DIM, CMP_HIDDEN), CMP_LEN * HEAD_DIM),
        "nsa_w2_v": nrm(ks[14], (N_EVEN, CMP_HIDDEN, HEAD_DIM), CMP_HIDDEN),
        "dsa_kv_norm": 1.0 + 0.02 * jax.random.normal(ks[15], (N_EVEN, DSA_KV_RANK), f32),
        "dsa_w_uk": nrm(ks[16], (N_EVEN, DSA_KV_RANK, DSA_HEADS, HEAD_DIM), DSA_KV_RANK),
        "dsa_w_uv": nrm(ks[17], (N_EVEN, DSA_KV_RANK, DSA_HEADS, HEAD_DIM), DSA_KV_RANK),
        "od_w_in": nrm(ks[18], (N_ODD, D, ODD_IN), D),
        "od_w_out": nrm(ks[19], (N_ODD, ODD_OUT, D), ODD_OUT, BETA),
        "diff_lam": 0.1 * jax.random.normal(ks[20], (N_ODD, 4, DIFF_DIM), f32),
        "diff_subln": 1.0 + 0.02 * jax.random.normal(ks[21], (N_ODD, 2 * DIFF_DIM), f32),
        "mlp_w1": nrm(ks[22], (DEPTH, D, D_FF), D),
        "mlp_w2": nrm(ks[23], (DEPTH, D_FF, D), D_FF, BETA),
    }

def first_block(x, c, rel_bias, ada_w, ada_b, ln_g, ln_b, ev_w_in, ev_w_out, nsa_pe_k, nsa_pe_v, nsa_w1_k, nsa_w2_k, nsa_w1_v, nsa_w2_v, dsa_kv_norm, dsa_w_uk, dsa_w_uv, od_w_in, od_w_out, diff_lam, diff_subln, mlp_w1, mlp_w2):
    c_act = jax.nn.silu(c)
    for l in range(DEPTH):
        ada = c_act @ ada_w[l] + ada_b[l]
        sh1, sc1, g1, sh2, sc2, g2 = jnp.split(ada, 6, axis=-1)
        h = modulate(x, sh1, sc1)
        i = l // 2
        if l % 2 == 0:
            y = even_mixer(h, ev_w_in[i], ev_w_out[i], nsa_pe_k[i], nsa_pe_v[i], nsa_w1_k[i], nsa_w2_k[i], nsa_w1_v[i], nsa_w2_v[i], dsa_kv_norm[i], dsa_w_uk[i], dsa_w_uv[i], rel_bias)
        else:
            lambda_init = 0.8 - 0.6 * math.exp(-0.3 * l)
            y = diff_mixer(h, od_w_in[i], od_w_out[i], diff_lam[i], diff_subln[i], rel_bias, lambda_init)
        x = layer_norm(ALPHA * x + (1.0 + g1[:, None, :]) * y, ln_g[l, 0], ln_b[l, 0])
        h = modulate(x, sh2, sc2)
        y = sq_relu_mlp(h, mlp_w1[l], mlp_w2[l])
        x = layer_norm(ALPHA * x + (1.0 + g2[:, None, :]) * y, ln_g[l, 1], ln_b[l, 1])
    return x


DEPTH_2 = 1

N_META = 16
GRID_W = 64
DN_HEADS = 4
DN_HEAD_DIM = 128
DN_WIDTH = DN_HEADS * DN_HEAD_DIM
DN_CHUNK = 64
CONV_W = 5
AT_Q_HEADS = 8
AT_KV_HEADS = 2
AT_HEAD_DIM = 64
AT_WIDTH = AT_Q_HEADS * AT_HEAD_DIM
AT_KV_WIDTH = AT_KV_HEADS * AT_HEAD_DIM
Q_BLOCK = 128
ROPE_THETA = 10000.0
ROPE_AXIS_DIM = AT_HEAD_DIM // 2
D_FF_2 = 4 * D_MODEL
EPS_2 = 1e-6
MIX_WIDTH = DN_WIDTH + AT_WIDTH
IN_SIZES = (DN_WIDTH, DN_WIDTH, DN_WIDTH, DN_WIDTH, 2 * DN_HEADS, 2 * DN_HEADS, AT_WIDTH, AT_KV_WIDTH, AT_KV_WIDTH)
IN_COLS = 4 * DN_WIDTH + 4 * DN_HEADS + AT_WIDTH + 2 * AT_KV_WIDTH


def rms_norm_2(x, w):
    xf = x.astype(jnp.float32)
    y = xf * lax.rsqrt(jnp.mean(xf * xf, axis=-1, keepdims=True) + EPS_2)
    return (y * w.astype(jnp.float32)).astype(x.dtype)

def l2_norm(x):
    xf = x.astype(jnp.float32)
    return xf * lax.rsqrt(jnp.sum(xf * xf, axis=-1, keepdims=True) + EPS_2)

def short_conv_silu(x, w):
    C = x.shape[-1]
    y = lax.conv_general_dilated(
        x, w[:, None, :].astype(x.dtype), window_strides=(1,),
        padding=[(CONV_W // 2, CONV_W // 2)],
        dimension_numbers=('NWC', 'WIO', 'NWC'), feature_group_count=C)
    return jax.nn.silu(y)

def to_scan_order(a_fwd, a_bwd):
    pad = jnp.zeros((a_fwd.shape[0], DN_CHUNK - N_META) + a_fwd.shape[2:], a_fwd.dtype)
    fwd = jnp.concatenate([pad, a_fwd], axis=1)
    bwd = jnp.concatenate([pad, a_bwd[:, :N_META], jnp.flip(a_bwd[:, N_META:], axis=1)], axis=1)
    return jnp.concatenate([fwd, bwd], axis=0)

def chunk_gated_delta_rule(q, k, v, g, beta):
    N, T, H, K = q.shape
    V = v.shape[-1]
    C = DN_CHUNK
    n = T // C

    def chunks(a):
        return jnp.moveaxis(a.reshape((N, n, C, H) + a.shape[3:]), 3, 2)

    q, k, v, g, beta = chunks(q), chunks(k), chunks(v), chunks(g), chunks(beta)
    gc = jnp.cumsum(g, axis=-1)
    incl = jnp.tril(jnp.ones((C, C), dtype=bool))
    strict = jnp.tril(jnp.ones((C, C), dtype=bool), -1)
    decay = jnp.exp(jnp.where(incl, gc[..., :, None] - gc[..., None, :], -jnp.inf))
    kk = jnp.einsum('bnhik,bnhjk->bnhij', k, k)
    a_low = jnp.where(strict, kk * decay * beta[..., :, None], 0.0)
    rhs = jnp.concatenate([v * beta[..., None], k * (beta * jnp.exp(gc))[..., None]], axis=-1)
    uw = lax.linalg.triangular_solve(a_low + jnp.eye(C, dtype=a_low.dtype), rhs,
                                     left_side=True, lower=True, unit_diagonal=True)
    u, w = uw[..., :V], uw[..., V:]
    qk = jnp.einsum('bnhik,bnhjk->bnhij', q, k) * decay
    q_dec = q * jnp.exp(gc)[..., None]
    k_dec = k * jnp.exp(gc[..., -1:] - gc)[..., None]
    g_last = jnp.exp(gc[..., -1])

    def step(S, xs):
        q_i, k_i, u_i, w_i, qk_i, gl_i = xs
        v_new = u_i - jnp.einsum('bhck,bhkv->bhcv', w_i, S)
        o_i = jnp.einsum('bhck,bhkv->bhcv', q_i, S) + jnp.einsum('bhij,bhjv->bhiv', qk_i, v_new)
        S = S * gl_i[..., None, None] + jnp.einsum('bhck,bhcv->bhkv', k_i, v_new)
        return S, o_i

    xs = tuple(jnp.moveaxis(a, 1, 0) for a in (q_dec, k_dec, u, w, qk, g_last))
    S0 = jnp.zeros((N, H, K, V), jnp.float32)
    _, o = lax.scan(step, S0, xs)
    o = jnp.moveaxis(o, 0, 1)
    return jnp.moveaxis(o, 3, 2).reshape(N, T, H, V)

def gated_deltanet_group(q, k, v, z, b, a, conv_w, a_log, dt_bias, o_norm_w):
    B, L, _ = q.shape
    out_dtype = q.dtype
    qkv = short_conv_silu(jnp.concatenate([q, k, v], axis=-1), conv_w)
    q, k, v = jnp.split(qkv, 3, axis=-1)
    heads = lambda t: t.reshape(B, L, DN_HEADS, DN_HEAD_DIM)
    q = l2_norm(heads(q)) * (DN_HEAD_DIM ** -0.5)
    k = l2_norm(heads(k))
    v = heads(v).astype(jnp.float32)
    beta = jax.nn.sigmoid(b.astype(jnp.float32)).reshape(B, L, 2, DN_HEADS)
    g = -jnp.exp(a_log.astype(jnp.float32)) * jax.nn.softplus(
        a.astype(jnp.float32).reshape(B, L, 2, DN_HEADS) + dt_bias.astype(jnp.float32))
    o = chunk_gated_delta_rule(
        to_scan_order(q, q), to_scan_order(k, k), to_scan_order(v, v),
        to_scan_order(g[:, :, 0], g[:, :, 1]), to_scan_order(beta[:, :, 0], beta[:, :, 1]))
    pad = DN_CHUNK - N_META
    o_f = o[:B, pad:]
    o_b = o[B:, pad:]
    o_b = jnp.concatenate([o_b[:, :N_META], jnp.flip(o_b[:, N_META:], axis=1)], axis=1)
    o = o_f + o_b
    o = rms_norm_2(o, o_norm_w) * jax.nn.silu(heads(z).astype(jnp.float32))
    return o.reshape(B, L, DN_WIDTH).astype(out_dtype)

def axial_rope_angles(n_real):
    rows = n_real // GRID_W
    r, c = jnp.meshgrid(jnp.arange(rows), jnp.arange(GRID_W), indexing='ij')
    r = r.reshape(-1).astype(jnp.float32)
    c = c.reshape(-1).astype(jnp.float32)
    F = ROPE_AXIS_DIM // 2
    freqs = ROPE_THETA ** (-jnp.arange(F, dtype=jnp.float32) / F)
    ang = jnp.concatenate([r[:, None] * freqs, c[:, None] * freqs], axis=-1)
    return jnp.concatenate([jnp.zeros((N_META, 2 * F), jnp.float32), ang], axis=0)

def apply_axial_rope(x, ang):
    B, L, H, D = x.shape
    F = ROPE_AXIS_DIM // 2
    xr = x.astype(jnp.float32).reshape(B, L, H, 2, 2, F)
    x1, x2 = xr[..., 0, :], xr[..., 1, :]
    an = ang.reshape(L, 1, 2, F)
    cos, sin = jnp.cos(an), jnp.sin(an)
    out = jnp.stack([x1 * cos - x2 * sin, x2 * cos + x1 * sin], axis=-2)
    return out.reshape(B, L, H, D).astype(x.dtype)

def axial_gqa_group(q, k, v, q_norm_w, k_norm_w):
    B, L, _ = q.shape
    G = AT_Q_HEADS // AT_KV_HEADS
    n_real = L - N_META
    q = rms_norm_2(q.reshape(B, L, AT_Q_HEADS, AT_HEAD_DIM), q_norm_w)
    k = rms_norm_2(k.reshape(B, L, AT_KV_HEADS, AT_HEAD_DIM), k_norm_w)
    v = v.reshape(B, L, AT_KV_HEADS, AT_HEAD_DIM)
    ang = axial_rope_angles(n_real)
    q = apply_axial_rope(q, ang) * (AT_HEAD_DIM ** -0.5)
    k = apply_axial_rope(k, ang)
    q = q.reshape(B, L, AT_KV_HEADS, G, AT_HEAD_DIM)

    def attend(qb):
        s = jnp.einsum('bqhgd,bkhd->bhgqk', qb, k, preferred_element_type=jnp.float32)
        p = jax.nn.softmax(s, axis=-1).astype(v.dtype)
        return jnp.einsum('bhgqk,bkhd->bqhgd', p, v)

    o_meta = attend(q[:, :N_META]).reshape(B, N_META, AT_WIDTH)
    nb = n_real // Q_BLOCK
    qr = q[:, N_META:].reshape(B, nb, Q_BLOCK, AT_KV_HEADS, G, AT_HEAD_DIM)
    o_real = lax.map(attend, jnp.moveaxis(qr, 1, 0))
    o_real = jnp.moveaxis(o_real, 0, 1).reshape(B, n_real, AT_WIDTH)
    return jnp.concatenate([o_meta, o_real], axis=1)

def second_inputs(seed: int = 0) -> dict:
    key = jax.random.key(seed)
    ks = jax.random.split(key, 20)
    f32 = jnp.float32
    nrm = lambda k_, shape, scale: jax.random.normal(k_, shape, f32) * scale
    gain = lambda k_, shape: 1.0 + 0.02 * jax.random.normal(k_, shape, f32)
    x = jax.random.normal(ks[0], (BATCH, SEQ, D_MODEL), f32)
    meta_tokens = nrm(ks[1], (N_META, D_MODEL), 1.0)
    w_in = nrm(ks[2], (DEPTH_2, D_MODEL, IN_COLS), D_MODEL ** -0.5)
    conv_w = nrm(ks[3], (DEPTH_2, CONV_W, 3 * DN_WIDTH), CONV_W ** -0.5)
    a_log = jnp.log(jax.random.uniform(ks[4], (DEPTH_2, 2, DN_HEADS), f32, 1.0, 16.0))
    dt = jnp.exp(jax.random.uniform(ks[5], (DEPTH_2, 2, DN_HEADS), f32, np.log(1e-3), np.log(1e-1)))
    dt_bias = dt + jnp.log(-jnp.expm1(-dt))
    dn_out_norm = gain(ks[6], (DEPTH_2, DN_HEAD_DIM))
    q_norm = gain(ks[7], (DEPTH_2, AT_HEAD_DIM))
    k_norm = gain(ks[8], (DEPTH_2, AT_HEAD_DIM))
    w_out = nrm(ks[9], (DEPTH_2, MIX_WIDTH, D_MODEL), MIX_WIDTH ** -0.5)
    norm_mix_pre = gain(ks[10], (DEPTH_2, D_MODEL))
    norm_mix_post = gain(ks[11], (DEPTH_2, D_MODEL))
    w_up = nrm(ks[12], (DEPTH_2, D_MODEL, D_FF_2), D_MODEL ** -0.5)
    w_down = nrm(ks[13], (DEPTH_2, D_FF_2, D_MODEL), D_FF_2 ** -0.5)
    norm_mlp_pre = gain(ks[14], (DEPTH_2, D_MODEL))
    norm_mlp_post = gain(ks[15], (DEPTH_2, D_MODEL))
    return {"x": x, "meta_tokens": meta_tokens, "w_in": w_in, "conv_w": conv_w,
            "a_log": a_log, "dt_bias": dt_bias, "dn_out_norm": dn_out_norm,
            "q_norm": q_norm, "k_norm": k_norm, "w_out": w_out,
            "norm_mix_pre": norm_mix_pre, "norm_mix_post": norm_mix_post,
            "w_up": w_up, "w_down": w_down,
            "norm_mlp_pre": norm_mlp_pre, "norm_mlp_post": norm_mlp_post}

def second_block(x, meta_tokens, w_in, conv_w, a_log, dt_bias, dn_out_norm, q_norm, k_norm, w_out,
              norm_mix_pre, norm_mix_post, w_up, w_down, norm_mlp_pre, norm_mlp_post):
    B = x.shape[0]
    split_points = [int(s) for s in np.cumsum(IN_SIZES)[:-1]]
    meta = jnp.broadcast_to(meta_tokens[None].astype(x.dtype), (B, N_META, D_MODEL))
    h = jnp.concatenate([meta, x], axis=1)
    for l in range(DEPTH_2):
        u = rms_norm_2(h, norm_mix_pre[l])
        proj = u @ w_in[l]
        dq, dk, dv, dz, db, da, aq, ak, av = jnp.split(proj, split_points, axis=-1)
        o_dn = gated_deltanet_group(dq, dk, dv, dz, db, da, conv_w[l], a_log[l], dt_bias[l], dn_out_norm[l])
        o_at = axial_gqa_group(aq, ak, av, q_norm[l], k_norm[l])
        mix = jnp.concatenate([o_dn, o_at.astype(o_dn.dtype)], axis=-1) @ w_out[l]
        h = h + rms_norm_2(mix, norm_mix_post[l])
        u = rms_norm_2(h, norm_mlp_pre[l])
        f = jnp.square(jax.nn.relu(u @ w_up[l])) @ w_down[l]
        h = h + rms_norm_2(f, norm_mlp_post[l])
    return h[:, N_META:]


def setup_inputs(seed=0):
    out = dict(first_inputs(seed))
    for name, value in second_inputs(seed + 1).items():
        if name != "x":
            out[name + "_2"] = value
    return out


def reference(
    x, c, rel_bias, ada_w, ada_b, ln_g, ln_b, ev_w_in, ev_w_out, nsa_pe_k, nsa_pe_v, nsa_w1_k,
    nsa_w2_k, nsa_w1_v, nsa_w2_v, dsa_kv_norm, dsa_w_uk, dsa_w_uv, od_w_in, od_w_out, diff_lam,
    diff_subln, mlp_w1, mlp_w2, meta_tokens_2, w_in_2, conv_w_2, a_log_2, dt_bias_2,
    dn_out_norm_2, q_norm_2, k_norm_2, w_out_2, norm_mix_pre_2, norm_mix_post_2, w_up_2,
    w_down_2, norm_mlp_pre_2, norm_mlp_post_2,
):
    x = first_block(
        x, c, rel_bias, ada_w, ada_b, ln_g, ln_b, ev_w_in, ev_w_out, nsa_pe_k, nsa_pe_v,
        nsa_w1_k, nsa_w2_k, nsa_w1_v, nsa_w2_v, dsa_kv_norm, dsa_w_uk, dsa_w_uv, od_w_in,
        od_w_out, diff_lam, diff_subln, mlp_w1, mlp_w2,
    )
    return second_block(
        x, meta_tokens_2, w_in_2, conv_w_2, a_log_2, dt_bias_2, dn_out_norm_2, q_norm_2,
        k_norm_2, w_out_2, norm_mix_pre_2, norm_mix_post_2, w_up_2, w_down_2, norm_mlp_pre_2,
        norm_mlp_post_2,
    )


_drawn_inputs = setup_inputs


def setup_inputs(seed=0):
    import zlib

    import numpy as np

    out = dict(_drawn_inputs(seed))
    spreads = {}
    factors = {'nsa_pe_k': 19.988,
     'dsa_kv_norm': 8.0,
     'diff_subln': 8.0,
     'dn_out_norm_2': 11.687,
     'q_norm_2': 27.356,
     'k_norm_2': 27.284,
     'norm_mix_post_2': 3.6,
     'norm_mlp_pre_2': 13.642,
     'norm_mlp_post_2': 51.804}
    for name, (base, spread) in spreads.items():
        noise = np.random.default_rng([zlib.crc32(name.encode()), seed]).standard_normal(out[name].shape)
        drawn = base * np.exp(spread * noise) if base else spread * noise
        out[name] = __import__('jax').numpy.asarray(drawn.astype(out[name].dtype))
    for name, factor in factors.items():
        out[name] = (out[name] * factor).astype(out[name].dtype)
    return out
```

```python
import math
from contextlib import ExitStack

import numpy as np

import concourse.bass as bass
from concourse import mybir

F32 = mybir.dt.float32
ALU = mybir.AluOpType
ACT = mybir.ActivationFunctionType
AX_X = mybir.AxisListType.X

P = 128
D = 1024
KT = D // P
SEQ = 256
QT = SEQ // P
DFF = 4 * D
META = 16
L2 = META + SEQ
ALPHA = (2 * 2) ** 0.25
NEG = -1e30
CLAMP = -1e29
REPLACED = -3e38
LAMBDA_INIT = 0.8 - 0.6 * math.exp(-0.3)
TOPK = 64
NUM_BUCKETS = 32
CMP_LEN, CMP_STRIDE = 32, 16
NCMP = (SEQ - CMP_LEN) // CMP_STRIDE + 1
SCALE = 64 ** -0.5
EXP_MAX = 80.0
SLOT = 4096
SLOTS = 5
LEVELS = 7


def t5_bucket(dist):
    n = np.maximum(dist, 0)
    exact = NUM_BUCKETS // 2
    nf = np.maximum(n, 1).astype(np.float32)
    large = exact + (np.log(nf / exact) / math.log(128 / exact) * (NUM_BUCKETS - exact)).astype(np.int32)
    return np.where(n < exact, n, np.minimum(large, NUM_BUCKETS - 1))


def bucket_windows():
    dist = np.arange(3 * P) - (P - 1)
    hot = np.zeros((NUM_BUCKETS + 1, 3 * P), np.float32)
    hot[t5_bucket(dist), np.arange(3 * P)] = dist >= 0
    hot[NUM_BUCKETS] = dist < 0
    return hot


def square_masks():
    i, j = np.arange(P)[:, None], np.arange(P)[None, :]
    blocks = [i == j, i <= j, i >= j, i > j, i < j]
    for back in (0, 1):
        for level in range(LEVELS):
            b = 1 << level
            joined = (i // (2 * b) == j // (2 * b)) & (i // b % 2 == 0) & (j // b % 2 == 1)
            blocks.append(joined.T if back else joined)
    return np.concatenate(blocks, 1).astype(np.float32)


def rope_tables():
    grid, f = 64, 16
    t = np.arange(SEQ)
    freqs = np.float32(10000.0) ** (-np.arange(f, dtype=np.float32) / np.float32(f))
    ang = np.concatenate([(t // grid).astype(np.float32)[:, None] * freqs,
                          (t % grid).astype(np.float32)[:, None] * freqs], 1)
    ang = np.concatenate([ang, np.zeros((META, 2 * f), np.float32)], 0)
    return np.concatenate([np.cos(ang), np.sin(ang)], 1).astype(np.float32)


class Queues:

    def __init__(self, nc, ctx):
        self.nc, self.ctx = nc, ctx
        self.names = ("tensor", "vector", "scalar", "gpsimd", "sync")
        self.items = {n: [] for n in self.names}
        self.sem = {n: ctx.enter_context(nc.semaphore(f"done_{n}")) for n in self.names[:4]}
        self.count = dict.fromkeys(self.names, 0)
        self.stores = []

    def put(self, engine, emit, *after, loose=False):
        waits = [s for s in after if s is not None and not (engine == "tensor" and s[0] == "tensor")]
        if engine != "tensor" and not loose and self.count[engine]:
            waits.append((engine, self.sem[engine], self.count[engine]))
        self.count[engine] += 1
        self.items[engine].append((waits, emit, self.sem[engine], 1))
        return (engine, self.sem[engine], self.count[engine])

    def dma(self, emit, sem, total, *after, engine="sync"):
        waits = [s for s in after if s is not None]
        self.items[engine].append((waits, emit, sem, 16))
        return (sem.name, sem, total)

    def load(self, name, dst, src, *after, engine="sync"):
        sem = self.ctx.enter_context(self.nc.semaphore(f"in_{name}"))
        return self.dma(lambda e: e.dma_start(dst, src), sem, 16, *after, engine=engine)

    def emit(self, engine, eng):
        seen = {}
        for waits, emit, sem, by in self.items[engine]:
            for name, s, value in waits:
                if seen.get(name, 0) < value:
                    eng.wait_ge(s, value)
                    seen[name] = value
            emit(eng).then_inc(sem, by)


class Bank:
    def __init__(self, tensor):
        self.t, self.after = tensor, []


class Banks:

    def __init__(self, nc, ctx):
        self.free = [Bank(ctx.enter_context(nc.psum_tensor(f"bank{i}", [P, 512], F32))) for i in range(8)]

    def take(self):
        return self.free.pop(0)

    def give(self, bank, *readers):
        bank.after = list(readers)
        self.free.append(bank)


class Ring:

    def __init__(self, q, nc, ctx):
        self.q = q
        self.slots = [ctx.enter_context(nc.sbuf_tensor(f"ring{i}", [P, SLOT], F32)) for i in range(SLOTS)]
        self.sems = [ctx.enter_context(nc.semaphore(f"ring_in{i}")) for i in range(SLOTS)]
        self.uses = [0] * SLOTS
        self.reader = [None] * SLOTS
        self.n = 0

    def load(self, src):
        s = self.n % SLOTS
        self.n += 1
        cols = int(np.prod(src.shape[1:]))
        rows = src.shape[0]
        view = self.slots[s][0:rows, 0:cols]
        if len(src.shape) == 3:
            view = view.rearrange("p (a b) -> p a b", a=src.shape[1])
        self.uses[s] += 1
        assert self.uses[s] == 1 or self.reader[s] is not None
        landed = self.q.dma(lambda e: e.dma_start(view, src), self.sems[s], 16 * self.uses[s], self.reader[s])
        self.reader[s] = None
        return view, landed, s

    def done(self, slot, reader):
        self.reader[slot] = reader


class Arena:

    def __init__(self, nc, ctx, cols):
        self.t = ctx.enter_context(nc.sbuf_tensor("arena", [P, cols], F32))
        self.cols, self.at, self.top = cols, 0, 0

    def over(self, start, cols):
        a = object.__new__(Arena)
        a.t, a.cols, a.at, a.top = self.t, start + cols, start, 0
        return a

    def take(self, *shape, rows=P):
        n = int(np.prod(shape))
        assert self.at + n <= self.cols, f"arena: {self.at} + {n} of {self.cols}"
        a = self.t[0:rows, self.at:self.at + n]
        self.at += n
        self.top = max(self.top, self.at)
        if len(shape) == 2:
            return a.rearrange("p (a b) -> p a b", a=shape[0])
        if len(shape) == 3:
            return a.rearrange("p (a b c) -> p a b c", a=shape[0], b=shape[1])
        return a


def program(nc, I, out):
    ctx = ExitStack()
    with ctx:
        q = Queues(nc, ctx)
        banks = Banks(nc, ctx)
        ring = Ring(q, nc, ctx)
        ar = Arena(nc, ctx, 32200)

        def PE(emit, *after):
            return q.put("tensor", emit, *after)

        def V(emit, *after, **k):
            return q.put("vector", emit, *after, **k)

        def S(emit, *after, **k):
            return q.put("scalar", emit, *after, **k)

        def G(emit, *after, **k):
            return q.put("gpsimd", emit, *after, **k)

        def mm(out_, lhsT, rhs, *after, start=True, stop=True):
            return PE(lambda e: e.matmul(out_, lhsT, rhs, start=start, stop=stop), *after)

        def copy(engine, dst, src, *after, **k):
            if engine == "scalar":
                return S(lambda e: e.activation(dst, src, ACT.Copy), *after, **k)
            return q.put(engine, lambda e: e.tensor_copy(dst, src), *after, **k)

        def tt(engine, dst, a, b, op, *after, **k):
            return q.put(engine, lambda e: e.tensor_tensor(dst, a, b, op), *after, **k)

        def ts(engine, dst, a, s1, s2, op0, op1, *after, **k):
            return q.put(engine, lambda e: e.tensor_scalar(dst, a, s1, s2, op0, op1) if s2 is not None
                         else e.tensor_scalar(dst, a, s1, None, op0), *after, **k)

        def stt(dst, a, s, b, op0, op1, *after, **k):
            return V(lambda e: e.scalar_tensor_tensor(out=dst, in0=a, scalar=s, in1=b, op0=op0, op1=op1),
                     *after, **k)

        def act(dst, src, func, *after, bias=None, scale=1.0, accum=None, **k):
            kw = {"scale": scale}
            if bias is not None:
                kw["bias"] = bias
            if accum is not None:
                kw["accum_out"] = accum
            return S(lambda e: e.activation(dst, src, func, **kw), *after, **k)

        def memset(engine, dst, value, *after):
            return q.put(engine, lambda e: e.memset(dst, value), *after)

        def turned(out_, in_, ident_, *after):
            return PE(lambda e: e.transpose(out_, in_, ident_), *after)

        def recip(dst, src, *after, **k):
            return V(lambda e: e.reciprocal(dst, src), *after, **k)

        def reduce_(dst, src, op, *after, negate=False, **k):
            return V(lambda e: e.tensor_reduce(dst, src, AX_X, op, negate=True) if negate
                     else e.tensor_reduce(dst, src, AX_X, op), *after, **k)

        ident = ar.take(P)
        in_ident = q.load("ident", ident, I["square_masks"][:, 0:P])
        hot = ar.take(3 * P, rows=NUM_BUCKETS + 1)
        in_hot = q.load("hot", hot, I["bucket_windows"][:, :])
        tab = ar.take(16, rows=NUM_BUCKETS + 1)
        in_tab = q.load("tab", tab[0:NUM_BUCKETS, :], I["rel_bias"][:, :])
        ones = ar.take(P)
        m_ones = memset("vector", ones, 1.0)
        eps5 = ar.take(1)
        memset("vector", eps5, 1e-5)
        eps6 = ar.take(1)
        m_eps = memset("vector", eps6, 1e-6)
        m_tab = memset("vector", tab[NUM_BUCKETS:NUM_BUCKETS + 1, :], NEG)

        rows_a = ar.take(P, rows=96)
        rows_b = ar.take(P, rows=96)
        col_at = {}
        n_rows = {0: 0, 1: 0}
        in_rows = {0: [], 1: []}

        def as_rows(which, name, src, n):
            r0 = n_rows[which]
            tile = (rows_a, rows_b)[which]
            in_rows[which].append(q.load(name, tile[r0:r0 + n, :], src))
            col_at[name] = (which, r0)
            n_rows[which] += n

        as_rows(0, "c", I["c"].rearrange("a (k p) -> (a k) p", p=P), KT)
        as_rows(0, "ln_g", I["ln_g"].rearrange("l s (k p) -> (l s k) p", p=P), 4 * KT)
        as_rows(0, "ln_b", I["ln_b"].rearrange("l s (k p) -> (l s k) p", p=P), 4 * KT)
        as_rows(0, "mix_pre", I["norm_mix_pre_2"].rearrange("a (k p) -> (a k) p", p=P), KT)
        as_rows(0, "mlp_pre", I["norm_mlp_pre_2"].rearrange("a (k p) -> (a k) p", p=P), KT)
        as_rows(0, "subln", I["diff_subln"], 1)
        as_rows(0, "dn_norm", I["dn_out_norm_2"], 1)
        as_rows(1, "conv", I["conv_w_2"].rearrange("a w (k p) -> (a w k) p", p=P), 60)
        as_rows(1, "pe_k", I["nsa_pe_k"].rearrange("a (l j) d -> (a l) (j d)", j=2), 16)
        as_rows(1, "pe_v", I["nsa_pe_v"].rearrange("a (l j) d -> (a l) (j d)", j=2), 16)
        cols = ar.take(2, 96)

        def transpose_rows(which, tile):
            n = n_rows[which]
            b = banks.take()
            t = turned(b.t[:, 0:n], tile[0:n, :], ident[0:n, 0:n],
                   in_ident, *in_rows[which], *b.after)
            c = copy("vector", cols[:, which, 0:n], b.t[:, 0:n], t)
            banks.give(b, c)
            return c

        def col(name, i=0, n=1):
            which, r0 = col_at[name]
            return cols[:, which, r0 + i:r0 + i + n]

        t_cols = transpose_rows(0, rows_a)
        t_cols_b = transpose_rows(1, rows_b)

        c_act = ar.take(KT)
        c_exp = ar.take(KT)
        v1 = ts("vector", c_exp, col("c", 0, KT), -EXP_MAX, None, ALU.max, None, t_cols)
        s1 = act(c_exp, c_exp, ACT.Exp, v1, scale=-1.0)
        v1 = ts("vector", c_exp, c_exp, 1.0, None, ALU.add, None, s1)
        recip(c_exp, c_exp)
        t_cact = tt("vector", c_act, c_exp, col("c", 0, KT), ALU.mult)

        x_tok = ar.take(QT, D)
        in_x = [q.load(f"x{t}", x_tok[:, t, :], I["x"][0, t * P:(t + 1) * P, :]) for t in range(QT)]
        oT = ar.take(KT, SEQ)
        after_cols = ar.at
        spare_at = ar.at
        n_tok = ar.take(QT, D)
        y_tmp = ar.take(QT, D)
        hT_at = ar.at
        hT = ar.take(KT, SEQ)
        bias = ar.take(16, SEQ)
        gate_at = ar.at
        gate_rows = ar.take(2, D)
        ln_rows = ar.take(2, D)
        ada_cols = ar.take(4, KT)
        mod_cols = ar.take(2, KT)
        ada_acc = ar.take(2, 512)
        ada_b_row = ar.take(2, 512, rows=1)
        stats = ar.take(QT, 24)
        phase_base = ar.at

        acc_reader = [None, None]
        ada_n = [0]
        ada_sem = [ctx.enter_context(nc.semaphore(f"ada_b_in{i}")) for i in range(2)]
        gate_reader = [None, None]
        col_reader = [None] * 4
        t_gate = [None, None]
        t_adac = [None] * 4

        def ada_chunk(layer, j):
            part, half = j // 2, j % 2
            s = ada_n[0] % 2
            ada_n[0] += 1
            w, landed, slot = ring.load(I["ada_w"][layer].rearrange("(k p) n -> p k n", p=P)[:, :, j * 512:(j + 1) * 512])
            brow = ada_b_row[:, s, :]
            b_in = q.dma(lambda e: e.dma_start(brow, I["ada_b"][layer:layer + 1, j * 512:(j + 1) * 512]),
                         ada_sem[s], 16 * ((ada_n[0] + 1) // 2), acc_reader[s])
            acc = ada_acc[:, s, :]
            v = ts("vector", acc, w[:, 0, :], c_act[:, 0:1], None, ALU.mult, None, landed, t_cact, acc_reader[s])
            for k in range(1, KT):
                v = stt(acc, w[:, k, :], c_act[:, k:k + 1], acc, ALU.mult, ALU.add)
            ring.done(slot, v)
            b = banks.take()
            if part in (2, 5):
                g = part // 3
                mm(b.t[:, :], ones, acc, v, m_ones, *b.after, stop=False)
                m = mm(b.t[:, :], ones[0:1, :], brow, b_in, start=False)
                c = ts("vector", gate_rows[:, g, half * 512:(half + 1) * 512], b.t[:, :], 1.0, None,
                       ALU.add, None, m, gate_reader[g])
                t_gate[g] = c
            else:
                for i in range(4):
                    mm(b.t[:, i:i + 1], acc[:, i * P:(i + 1) * P], ones[:, 0:1], v, m_ones, *b.after, stop=False)
                    m = mm(b.t[:, i:i + 1], brow[:, i * P:(i + 1) * P], ones[0:1, 0:1], b_in, start=False)
                which = {0: 0, 1: 1, 3: 2, 4: 3}[part]
                c = copy("vector", ada_cols[:, which, half * 4:half * 4 + 4], b.t[:, 0:4], m, col_reader[which])
                t_adac[which] = c
            banks.give(b, c)
            acc_reader[s] = m

        def feature_product(w, c0, m, src, toks, out_, *after):
            n = w.shape[1]
            for k in range(n):
                last = mm(out_, w[:, k, c0:c0 + m], src[:, k, toks], *(after if k == 0 else ()),
                          start=k == 0, stop=k == n - 1)
            return last

        def token_product(w, c0, n_cols, src, toks, out_, *after):
            n = w.shape[1]
            for k in range(n):
                last = mm(out_, src[:, k, toks], w[:, k, c0:c0 + n_cols], *(after if k == 0 else ()),
                          start=k == 0, stop=k == n - 1)
            return last

        def rsqrt_col(dst, var, tmp, eps, *after):
            a = ts("vector", tmp, var, eps, None, ALU.add, None, *after)
            s = act(dst, tmp, ACT.Ln, a)
            s = act(dst, dst, ACT.Exp, s, scale=-0.5)
            tmp2 = var
            tt("vector", tmp2, dst, dst, ALU.mult, s)
            tt("vector", tmp2, tmp2, tmp, ALU.mult)
            ts("vector", tmp2, tmp2, -0.5, 1.5, ALU.mult, ALU.add)
            return tt("vector", dst, dst, tmp2, ALU.mult)

        def to_features(src_tok, t_src, dst, scale_cols, shift_cols, t_coef, t_free, t, toks=P, at=None):
            at = t * P if at is None else at
            done = []
            for k0 in range(0, KT, 4):
                b = banks.take()
                for k in range(k0, k0 + 4):
                    m = turned(
                        b.t[:, (k - k0) * P:(k - k0) * P + toks], src_tok[:, k * P:(k + 1) * P],
                        ident[0:toks, 0:toks], t_src, in_ident, *b.after)
                for k in range(k0, k0 + 4):
                    o, i_ = dst[:, k, at:at + toks], b.t[:, (k - k0) * P:(k - k0) * P + toks]
                    if (k0 // 4 + t) % 2:
                        if shift_cols is None:
                            c = act(o, i_, ACT.Copy, m, t_coef, *t_free, scale=scale_cols[:, k:k + 1], loose=True)
                        else:
                            c = act(o, i_, ACT.Identity, m, t_coef, *t_free, scale=scale_cols[:, k:k + 1],
                                    bias=shift_cols[:, k:k + 1], loose=True)
                    elif shift_cols is None:
                        c = ts("vector", o, i_, scale_cols[:, k:k + 1], None, ALU.mult, None, m, t_coef, *t_free, loose=True)
                    else:
                        c = ts("vector", o, i_, scale_cols[:, k:k + 1], shift_cols[:, k:k + 1], ALU.mult, ALU.add,
                               m, t_coef, *t_free, loose=True)
                banks.give(b, c)
                done.append(c)
            return done

        t_bias = None
        for c0 in range(0, SEQ, 32):
            b = banks.take()
            for c in range(c0, c0 + 32):
                x0 = 255 - c
                m = mm(b.t[:, (c - c0) * 16:(c - c0) * 16 + 16], hot[:, x0:x0 + P], tab, in_hot, in_tab, m_tab,
                       *b.after)
            t_bias = copy("scalar", bias[:, :, c0:c0 + 32],
                          b.t[:, :].rearrange("p (c h) -> p h c", h=16), m)
            banks.give(b, t_bias)

        for j in range(4):
            ada_chunk(0, j)

        def modulation(sub, ln=None):
            sh, sc = ada_cols[:, 2 * sub, :], ada_cols[:, 2 * sub + 1, :]
            after = (t_adac[2 * sub], t_adac[2 * sub + 1])
            a = ts("vector", mod_cols[:, 0, :], sc, 1.0, None, ALU.add, None, *after)
            if ln is None:
                a = copy("vector", mod_cols[:, 1, :], sh)
            else:
                tt("vector", mod_cols[:, 1, :], mod_cols[:, 0, :], col("ln_b", ln * KT, KT), ALU.mult)
                tt("vector", mod_cols[:, 1, :], mod_cols[:, 1, :], sh, ALU.add)
                a = tt("vector", mod_cols[:, 0, :], mod_cols[:, 0, :], col("ln_g", ln * KT, KT), ALU.mult)
            col_reader[2 * sub] = col_reader[2 * sub + 1] = a
            return a

        t_mod = modulation(0)
        t_h = []
        for t in range(QT):
            t_h += to_features(x_tok[:, t, :], in_x[t], hT, mod_cols[:, 0, :], mod_cols[:, 1, :], t_mod, (), t)

        all_toks = slice(0, SEQ)
        HALF = 64
        wk = ar.at
        spare = ar.over(spare_at, 2 * QT * D)
        qT = ar.take(4, SEQ)
        dqT = ar.take(4, SEQ)
        iqT = ar.take(4, SEQ)
        k_sel = ar.take(2, SEQ)
        k_win = ar.take(2, SEQ)
        ikT = ar.take(SEQ)
        v_sw = ar.take(QT, SEQ)
        gates = ar.take(QT, 24)
        ckv = ar.take(QT, P)
        ckvT = ar.take(SEQ)
        iw = ar.take(QT, 8)
        qlatT = ar.take(8, SEQ)
        raw = ar.take(4, SEQ)
        over_hT = ar.over(hT_at, KT * SEQ)
        over_gates = ar.over(gate_at, 2 * D)
        blk = over_hT.take(2, 16, 30)
        w_ev = I["ev_w_in"][0].rearrange("(k p) n -> p k n", p=P)

        w, landed, slot = ring.load(w_ev[:, :, 0:512])
        for i in range(4):
            b = banks.take()
            m = feature_product(w, i * P, P, hT, all_toks, b.t[:, 0:SEQ], landed, *t_h, *b.after)
            t_q = copy("scalar", qT[:, i, :], b.t[:, 0:SEQ], m)
            banks.give(b, t_q)
        ring.done(slot, m)

        def both_halves(src, dst_of, m, engine):
            for g in range(2):
                for half in range(2):
                    c = copy(engine, dst_of(g)[half * HALF:(half + 1) * HALF, :], src[g * HALF:(g + 1) * HALF, :], m)
            return (c,)

        w, landed, slot = ring.load(w_ev[:, :, 512:1024])
        t_raw = []
        for kv in range(2):
            b = banks.take()
            m = feature_product(w, kv * P, P, hT, all_toks, b.t[:, 0:SEQ], landed, *b.after)
            for g in range(2):
                s_ = b.t[g * HALF:(g + 1) * HALF, :]
                copy("vector" if kv else "scalar", raw[0:HALF, 2 * kv + g, :], s_[:, 0:SEQ], m)
                c2 = copy("vector" if kv else "scalar", raw[HALF:P, 2 * kv + g, 0:SEQ - 1], s_[:, 1:SEQ], m)
            t_raw.append(c2)
            banks.give(b, c2)
        b = banks.take()
        m = feature_product(w, 256, P, hT, all_toks, b.t[:, 0:SEQ], *b.after)
        t_ks = both_halves(b.t[:, 0:SEQ], lambda g: k_sel[:, g, :], m, "vector")
        banks.give(b, *t_ks)
        b = banks.take()
        for t in range(QT):
            m = token_product(w, 384, P, hT, slice(t * P, (t + 1) * P), b.t[:, t * P:(t + 1) * P], *b.after)
        t_vs = copy("scalar", v_sw[:, :, 0:P], b.t[:, 0:SEQ].rearrange("p (t n) -> p t n", t=QT), m)
        banks.give(b, t_vs)
        ring.done(slot, m)

        w, landed, slot = ring.load(w_ev[:, :, 1024:1304])
        b = banks.take()
        m = feature_product(w, 0, P, hT, all_toks, b.t[:, 0:SEQ], landed, *b.after)
        t_kw = both_halves(b.t[:, 0:SEQ], lambda g: k_win[:, g, :], m, "scalar")
        banks.give(b, *t_kw)
        b = banks.take()
        for t in range(QT):
            m = token_product(w, P, P + 24, hT, slice(t * P, (t + 1) * P), b.t[:, t * 160:t * 160 + P + 24], *b.after)
        vg = b.t[:, 0:320].rearrange("p (t n) -> p t n", t=QT)
        t_vw = copy("scalar", v_sw[:, :, P:2 * P], vg[:, :, 0:P], m)
        v1 = ts("vector", gates, vg[:, :, P:P + 24], -EXP_MAX, None, ALU.max, None, t_vw)
        banks.give(b, v1)
        s1 = act(gates, gates, ACT.Exp, v1, scale=-1.0)
        ring.done(slot, m)
        ts("vector", gates, gates, 1.0, None, ALU.add, None, s1)
        t_gates = recip(gates, gates)

        w, landed, slot = ring.load(w_ev[:, :, 1304:1816])
        for i in range(4):
            b = banks.take()
            m = feature_product(w, i * P, P, hT, all_toks, b.t[:, 0:SEQ], landed, *b.after)
            t_dq = copy("scalar", dqT[:, i, :], b.t[:, 0:SEQ], m)
            banks.give(b, t_dq)
        ring.done(slot, m)

        kvn_row = ar.take(P)
        in_kvn = q.load("kvn", kvn_row, I["dsa_kv_norm"][0].partition_broadcast(P))
        sq = spare.take(QT, P)
        w, landed, slot = ring.load(w_ev[:, :, 1816:2328])
        b = banks.take()
        for t in range(QT):
            m = token_product(w, 0, P, hT, slice(t * P, (t + 1) * P), b.t[:, t * P:(t + 1) * P], landed, *b.after)
        for t in range(QT):
            s0 = act(sq[:, t, :], b.t[:, t * P:(t + 1) * P], ACT.Square, m, accum=stats[:, t, 0:1])
        for t in range(QT):
            ts("vector", stats[:, t, 1:2], stats[:, t, 0:1], 1.0 / P, None, ALU.mult, None, s0)
            v1 = rsqrt_col(stats[:, t, 2:3], stats[:, t, 1:2], stats[:, t, 3:4], 1e-5)
            t_ckv = stt(ckv[:, t, :], b.t[:, t * P:(t + 1) * P], stats[:, t, 2:3], kvn_row, ALU.mult, ALU.mult,
                        in_kvn)
        banks.give(b, t_ckv)
        b = banks.take()
        for t in range(QT):
            m2 = turned(b.t[:, t * P:(t + 1) * P], ckv[:, t, :], ident, t_ckv, *b.after)
        t_ckvT = copy("scalar", ckvT, b.t[:, 0:SEQ], m2)
        banks.give(b, t_ckvT)
        for i in range(4):
            if i == 3:
                ring.done(slot, m)
                w, landed, slot = ring.load(w_ev[:, :, 2328:2528])
            b = banks.take()
            m = feature_product(w, (1 + i) * P if i < 3 else 0, P, hT, all_toks, b.t[:, 0:SEQ], landed, *b.after)
            t_iq = copy("scalar", iqT[:, i, :], b.t[:, 0:SEQ], m)
            banks.give(b, t_iq)
        b = banks.take()
        m = feature_product(w, P, HALF, hT, all_toks, b.t[0:HALF, 0:SEQ], *b.after)
        copy("scalar", ikT[0:HALF, :], b.t[0:HALF, 0:SEQ], m)
        c2 = copy("scalar", ikT[HALF:P, :], b.t[0:HALF, 0:SEQ], m)
        t_ik = (c2,)
        banks.give(b, c2)
        b = banks.take()
        for t in range(QT):
            m = token_product(w, P + HALF, 8, hT, slice(t * P, (t + 1) * P), b.t[:, t * 8:(t + 1) * 8], *b.after)
        t_iw = ts("vector", iw, b.t[:, 0:16].rearrange("p (t n) -> p t n", t=QT), 8 ** -0.5 * 64 ** -0.5, None,
                  ALU.mult, None, m)
        banks.give(b, t_iw)
        ring.done(slot, m)

        w, landed, slot = ring.load(I["dsa_w_uk"][0].rearrange("r h d -> r (h d)"))
        ukT = spare.take(4, P)
        b = banks.take()
        for i in range(4):
            m = turned(b.t[:, i * P:(i + 1) * P], w[:, i * P:(i + 1) * P], ident,
                   landed, *b.after)
        t_uk = copy("vector", ukT.rearrange("p a b -> p (a b)"), b.t[:, :], m)
        banks.give(b, t_uk)
        ring.done(slot, m)
        for h in range(8):
            b = banks.take()
            lo = h % 2 * HALF
            m = mm(b.t[:, 0:SEQ], ukT[lo:lo + HALF, h // 2, :], dqT[lo:lo + HALF, h // 2, :], t_uk, t_dq, *b.after)
            t_ql = copy("scalar" if h % 2 else "vector", qlatT[:, h, :], b.t[:, 0:SEQ], m)
            if h == 6:
                t_ql6 = t_ql
            banks.give(b, t_ql)
        t_qlat = (t_ql6, t_ql)

        for kv in range(2):
            pe = col("pe_v" if kv else "pe_k", 0, 16)
            for g in range(2):
                lo = raw[:, 2 * kv + g, :].rearrange("p (n l j) -> p l n j", l=8, j=2)[:, :, :, 0]
                for hi in range(2):
                    t_blk = tt("vector", blk[:, kv, 8 * hi:8 * hi + 8, g * NCMP:(g + 1) * NCMP],
                               lo[:, :, hi:hi + NCMP],
                               pe[:, 8 * hi:8 * hi + 8].unsqueeze(2).broadcast_to([P, 8, NCMP]), ALU.add,
                               *t_raw, t_cols_b)
        hidden = ar.take(2, 2, 30)
        gel = ar.take(2, 2, 30)
        kcT = ar.take(2, NCMP)
        v_cmp = ar.take(2, HALF)
        for kv in range(2):
            w, landed, slot = ring.load(I["nsa_w1_v" if kv else "nsa_w1_k"][0].rearrange("(l p) n -> p l n", p=P))
            b = banks.take()
            for i in range(2):
                for l in range(16):
                    m = mm(b.t[:, i * 30:(i + 1) * 30], w[:, l, i * P:(i + 1) * P], blk[:, kv, l, :],
                           landed, t_blk, *b.after, start=l == 0, stop=l == 15)
            h_ = hidden[:, kv, :, :].rearrange("p a b -> p (a b)")
            g_ = gel[:, kv, :, :].rearrange("p a b -> p (a b)")
            v1 = copy("vector", h_, b.t[:, 0:60], m)
            banks.give(b, v1)
            ring.done(slot, m)
            tt("vector", g_, h_, h_, ALU.mult)
            ts("vector", g_, g_, 0.044715, 1.0, ALU.mult, ALU.add)
            tt("vector", g_, g_, h_, ALU.mult)
            v1 = ts("vector", g_, g_, -EXP_MAX / 2, None, ALU.max, None)
            s1 = act(g_, g_, ACT.Exp, v1, scale=-2.0 * math.sqrt(2.0 / math.pi))
            ts("vector", g_, g_, 1.0, None, ALU.add, None, s1)
            recip(g_, g_)
            t_gel = tt("vector", g_, g_, h_, ALU.mult)
            w, landed, slot = ring.load(I["nsa_w2_v" if kv else "nsa_w2_k"][0].rearrange("(l p) n -> p l n", p=P))
            b = banks.take()
            if kv == 0:
                for i in range(2):
                    m = mm(b.t[0:HALF, 0:30], w[:, i, :], gel[:, 0, i, :], landed, t_gel, *b.after,
                           start=i == 0, stop=i == 1)
                for half in range(2):
                    t_kc = copy("vector", kcT[half * HALF:(half + 1) * HALF, :, :],
                                b.t[0:HALF, 0:30].rearrange("p (g n) -> p g n", g=2), m)
                banks.give(b, t_kc)
            else:
                for g in range(2):
                    for i in range(2):
                        m = mm(b.t[0:NCMP, g * HALF:(g + 1) * HALF], gel[:, 1, i, g * NCMP:(g + 1) * NCMP],
                               w[:, i, :], landed, t_gel, *b.after, start=i == 0, stop=i == 1)
                for base in range(0, P, 32):
                    t_vc = copy("vector", v_cmp[base:base + NCMP, :, :],
                                b.t[0:NCMP, 0:2 * HALF].rearrange("p (g n) -> p g n", g=2), m)
                banks.give(b, t_vc)
            ring.done(slot, m)
        assert ring.n

        pc = over_hT.take(QT * 8, 32)
        bc = ar.take(QT * 8, NCMP)
        m1 = memset("gpsimd", pc, 0.0, m)
        m2 = memset("gpsimd", bc, NEG)
        first = (2 * P - 1 - (P + CMP_LEN - 1)) // CMP_STRIDE + 1
        copy("gpsimd", bc[:, 0:8, 0:first], bias[:, 0:8, P + CMP_LEN - 1::CMP_STRIDE], m2, t_bias)
        t_bc = copy("gpsimd", bc[:, 8:16, :], bias[:, 0:8, CMP_LEN - 1::CMP_STRIDE][:, :, 0:NCMP])
        z = pc[:, :, 0:NCMP]
        for par in range(2):
            b = banks.take()
            lo = par * HALF
            for t in range(QT):
                for h2 in range(4):
                    o = (t * 4 + h2) * 32
                    m = mm(b.t[:, o:o + NCMP], qT[lo:lo + HALF, h2, t * P:(t + 1) * P],
                           kcT[lo:lo + HALF, h2 // 2, :], t_q, t_kc, *b.after)
            v1 = stt(pc[:, par::2, 0:NCMP], b.t[:, 0:SEQ].rearrange("p (a n) -> p a n", n=32)[:, :, 0:NCMP],
                     SCALE, bc[:, par::2, :], ALU.mult, ALU.add, m, m1, t_bc)
            banks.give(b, v1)
        cst = ar.take(4, QT * 8)
        reduce_(cst[:, 0, :], z, ALU.max)
        ts("vector", cst[:, 0, :], cst[:, 0, :], CLAMP, None, ALU.max, None)
        v1 = tt("vector", z, z, cst[:, 0, :].unsqueeze(2).broadcast_to([P, QT * 8, NCMP]), ALU.subtract)
        s1 = act(z, z, ACT.Exp, v1)
        reduce_(cst[:, 1, :], z, ALU.add, s1)
        ts("vector", cst[:, 1, :], cst[:, 1, :], 1e-30, None, ALU.max, None)
        recip(cst[:, 2, :], cst[:, 1, :])
        tt("vector", cst[:, 3, :].rearrange("p (t h) -> p t h", t=QT), cst[:, 2, :].rearrange("p (t h) -> p t h", t=QT),
           gates[:, :, 0::3], ALU.mult)
        t_pc = tt("vector", z, z, cst[:, 3, :].unsqueeze(2).broadcast_to([P, QT * 8, NCMP]), ALU.mult)
        pcT = over_hT.take(2, SEQ)
        b = banks.take()
        for g in range(2):
            for t in range(QT):
                m = turned(
                    b.t[:, g * SEQ + t * P:g * SEQ + (t + 1) * P],
                    pc[:, t * 8 + g * 4:t * 8 + g * 4 + 4, :].rearrange("p a b -> p (a b)"), ident, t_pc, *b.after)
        t_pcT = copy("vector", pcT.rearrange("p a b -> p (a b)"), b.t[:, :], m)
        banks.give(b, t_pcT)

        UC = 3 * P
        NB = 4
        zb = spare.take(NB, UC)
        pT = spare.take(NB, UC)
        ust = ar.take(NB, 8)
        z_reader = [None] * NB
        pT_reader = [None] * NB
        unit_n = [0]

        def unit_logits(u, lhs_of, rhs_of, scale, bias_of, after, coef):
            s = u["s"] = unit_n[0] % NB
            unit_n[0] += 1
            b = banks.take()
            mm(b.t[:, 0:P], lhs_of(0), rhs_of(slice(0, P)), *after, *b.after)
            m = mm(b.t[:, P:UC], lhs_of(1), rhs_of(slice(0, SEQ)))
            z, st = zb[:, s, :], ust[:, s, :]
            bias_ap, t_b = bias_of()
            stt(z[:, 0:P], b.t[:, 0:P], scale, bias_ap[0], ALU.mult, ALU.add, m, t_b, *(z_reader[s] or ()))
            v = stt(z[:, P:UC], b.t[:, P:UC], scale, bias_ap[1], ALU.mult, ALU.add, loose=True)
            banks.give(b, v)
            reduce_(st[:, 0:1], z[:, 0:P], ALU.max, negate=True)
            v = reduce_(st[:, 1:2], z[:, P:UC], ALU.max, negate=True, loose=True)
            act(z[:, 0:P], z[:, 0:P], ACT.Exp, v, bias=st[:, 0:1], accum=st[:, 2:3], loose=True)
            a = act(z[:, P:UC], z[:, P:UC], ACT.Exp, bias=st[:, 1:2], accum=st[:, 3:4], loose=True)
            v = recip(st[:, 4:6], st[:, 2:4], a)
            if coef is not None:
                v = coef(st, v)
            u["z"], u["st"], u["v"] = z, st, v

        def unit_scale(u):
            z, st = u["z"], u["st"]
            ts("gpsimd", z[:, 0:P], z[:, 0:P], st[:, 4:5], None, ALU.mult, None, u["v"], loose=True)
            u["p"] = ts("gpsimd", z[:, P:UC], z[:, P:UC], st[:, 5:6], None, ALU.mult, None, loose=True)

        def unit_transpose(u):
            s, z = u["s"], u["z"]
            b = banks.take()
            turned(b.t[:, 0:P], z[:, 0:P], ident, u["p"], *b.after)
            turned(b.t[:, P:2 * P], z[:, P:2 * P], ident)
            m = turned(b.t[:, 2 * P:UC], z[:, 2 * P:UC], ident)
            z_reader[s] = (m,)
            c = copy("scalar", pT[:, s, :], b.t[:, 0:UC], m, *(pT_reader[s] or ()), loose=True)
            banks.give(b, c)
            u["pT"] = c

        def run_units(units, lags=(0, 2, 3)):
            for step in range(len(units) + lags[-1]):
                for stage, lag in reversed(list(enumerate(lags))):
                    if 0 <= step - lag < len(units):
                        units[step - lag][stage]()

        bias_pair = lambda h: ((bias[:, h, P:SEQ], bias[:, h, :]), t_bias)
        head_bank = {}

        def nsa_unit(h, branch):
            u = {}
            lo, g = h % 2 * HALF, h // 4
            kk, col0, ready = ((k_sel, 0, t_ks), (k_win, P, t_kw))[branch]

            def coef(st, v):
                for t in range(QT):
                    v = tt("vector", st[:, 4 + t:5 + t], st[:, 4 + t:5 + t], gates[:, t, 3 * h + 1 + branch:3 * h + 2 + branch],
                           ALU.mult, t_gates, loose=t > 0)
                return v

            def logits():
                unit_logits(u, lambda t: qT[lo:lo + HALF, h // 2, t * P:(t + 1) * P],
                            lambda k: kk[lo:lo + HALF, g, k], SCALE, lambda: bias_pair(h), (t_q, *ready), coef)
                unit_scale(u)

            def values():
                pair = h // 2
                if branch == 0:
                    if h % 2 == 0:
                        head_bank[pair] = banks.take()
                    b = head_bank[pair]
                    o = b.t[lo:lo + HALF, 0:SEQ]
                    base = 32 * (h % 4)
                    mm(o, v_cmp[base:base + NCMP, g, :], pcT[base:base + NCMP, g, :], t_vc, t_pcT, *b.after, stop=False)
                b = head_bank[pair]
                p_ = pT[:, u["s"], :]
                mm(b.t[lo:lo + HALF, 0:SEQ], v_sw[:, 0, col0 + g * HALF:col0 + (g + 1) * HALF], p_[:, 0:SEQ],
                   u["pT"], t_vs, t_vw, start=False, stop=False)
                m = mm(b.t[lo:lo + HALF, P:SEQ], v_sw[:, 1, col0 + g * HALF:col0 + (g + 1) * HALF], p_[:, SEQ:UC],
                       start=False, stop=branch == 1)
                pT_reader[u["s"]] = (m,)
                if h % 2 and branch:
                    c = copy("vector", oT[:, pair, :], b.t[:, 0:SEQ], m)
                    banks.give(b, c)
                    t_oT.append(c)
            return [logits, lambda: unit_transpose(u), values]

        t_oT = []
        run_units([nsa_unit(h, br) for h in range(8) for br in range(2)])

        isc = over_gates.take(UC)
        taken = over_gates.take(UC)
        relu = over_gates.take(2, UC)
        top8 = ar.take(QT, 8)
        r_reader = [None, None]
        for j in range(8):
            lo = j % 2 * HALF
            b = banks.take()
            mm(b.t[:, 0:P], iqT[lo:lo + HALF, j // 2, 0:P], ikT[lo:lo + HALF, 0:P], t_iq, *t_ik, *b.after)
            m = mm(b.t[:, P:UC], iqT[lo:lo + HALF, j // 2, P:SEQ], ikT[lo:lo + HALF, :])
            r = relu[:, j % 2, :]
            s1 = act(r, b.t[:, 0:UC], ACT.Relu, m, r_reader[j % 2], loose=True)
            banks.give(b, s1)
            for t, c in ((0, slice(0, P)), (1, slice(P, UC))):
                if j == 0:
                    v1 = ts("vector", isc[:, c], r[:, c], iw[:, t, 0:1], None, ALU.mult, None, s1, t_iw)
                else:
                    v1 = stt(isc[:, c], r[:, c], iw[:, t, j:j + 1], isc[:, c], ALU.mult, ALU.add, s1)
            r_reader[j % 2] = v1
        for c in (slice(0, P), slice(2 * P, UC)):
            t_isc = G(lambda e, c=c: e.affine_select(out=isc[:, c], in_=isc[:, c], compare_op=ALU.is_ge, fill=NEG,
                                                     base=0, pattern=[[-1, P]], channel_multiplier=1), v1)
        v1 = copy("vector", taken, isc, t_isc)
        for r in range(TOPK // 8):
            for t, c in ((0, slice(0, P)), (1, slice(P, UC))):
                V(lambda e, t=t, c=c: e.max(top8[:, t, :], taken[:, c]))
                V(lambda e, t=t, c=c: e.match_replace(taken[:, c], top8[:, t, :], taken[:, c], REPLACED))
        ts("vector", taken, taken, -1e38, 1.0, ALU.is_le, ALU.subtract)
        t_sel = ts("vector", taken, taken, -NEG, None, ALU.mult, None)

        w_uv, in_uv, uv_slot = ring.load(I["dsa_w_uv"][0].rearrange("r h d -> r (h d)"))
        dbias = ar.take(2, UC)
        db_reader = [None, None]
        olat = over_gates.take(2, SEQ)
        olat_reader = [None, None]

        def dsa_unit(h):
            u = {}

            def logits():
                s = h % 2
                tt("gpsimd", dbias[:, s, 0:P], bias[:, 8 + h, P:SEQ], taken[:, 0:P], ALU.add, t_sel, db_reader[s])
                g_ = tt("gpsimd", dbias[:, s, P:UC], bias[:, 8 + h, :], taken[:, P:UC], ALU.add)
                unit_logits(u, lambda t: qlatT[:, h, t * P:(t + 1) * P], lambda k: ckvT[:, k], SCALE,
                            lambda: ((dbias[:, s, 0:P], dbias[:, s, P:UC]), g_), (*t_qlat, t_ckvT), None)
                db_reader[s] = u["v"]
                unit_scale(u)

            def values():
                s = h % 2
                b = banks.take()
                p_ = pT[:, u["s"], :]
                mm(b.t[:, 0:SEQ], ckv[:, 0, :], p_[:, 0:SEQ], u["pT"], t_ckv, *b.after, stop=False)
                m = mm(b.t[:, P:SEQ], ckv[:, 1, :], p_[:, SEQ:UC], start=False)
                pT_reader[u["s"]] = (m,)
                c = copy("vector", olat[:, s, :], b.t[:, 0:SEQ], m, olat_reader[s])
                banks.give(b, c)
                u["olat"] = c

            def project():
                s, lo, pair = h % 2, h % 2 * HALF, h // 2
                if h % 2 == 0:
                    head_bank[pair] = banks.take()
                b = head_bank[pair]
                m = mm(b.t[lo:lo + HALF, 0:SEQ], w_uv[:, h * HALF:(h + 1) * HALF], olat[:, s, :], in_uv, u["olat"], *b.after)
                olat_reader[s] = m
                if h % 2:
                    c = copy("vector", oT[:, 4 + pair, :], b.t[:, 0:SEQ], m)
                    banks.give(b, c)
                    t_oT.append(c)
                u["m"] = m
                return m
            return [logits, lambda: unit_transpose(u), values, project], u

        dsa = [dsa_unit(h) for h in range(8)]
        run_units([d[0] for d in dsa], (0, 2, 3, 4))
        ring.done(uv_slot, dsa[-1][1]["m"])
        for j in range(4, 12):
            ada_chunk(0, j)

        ln_sem = [ctx.enter_context(nc.semaphore(f"ln_rows_in{i}")) for i in range(2)]
        ln_reader = [None]
        ln_uses = [0]
        x_state = {"x": (in_x[0], in_x[1])}

        def out_product(chunks, src, t_src, between=None, src_toks=lambda t: slice(t * P, (t + 1) * P)):
            ys = [[banks.take() for _ in range(2)] for _ in range(QT)]
            n = len(chunks) * 4
            for ci, chunk in enumerate(chunks):
                w, landed, slot = ring.load(chunk)
                for kk in range(4):
                    k = ci * 4 + kk
                    for t in range(QT):
                        for half in range(2):
                            b = ys[t][half]
                            m = mm(b.t[:, :], src[:, k, src_toks(t)], w[:, kk, half * 512:(half + 1) * 512],
                                   landed, *t_src(k), *(b.after if k == 0 else ()), start=k == 0, stop=k == n - 1)
                ring.done(slot, m)
                if between is not None:
                    between(ci)
            return ys, m

        def k_chunks(w):
            r = w.rearrange("(c k p) n -> c p k n", k=4, p=P)
            return [r[i] for i in range(r.shape[0])]

        def residual_norm(ys, m, sub, ln, next_mod):
            rows_in = []
            for i, name in enumerate(("ln_g", "ln_b")):
                ln_uses[0] += 1
                rows_in.append(q.dma(lambda e, i=i, name=name: e.dma_start(
                    ln_rows[:, i, :], I[name][ln // 2, ln % 2].partition_broadcast(P)), ln_sem[i],
                    16 * ((ln_uses[0] + 1) // 2), ln_reader[0], engine="gpsimd" if False else "sync"))
            t_mod = next_mod() if next_mod else None
            done, xs = [], []
            tr = []
            for t in range(QT):
                y = y_tmp[:, t, :]
                for half in range(2):
                    b = ys[t][half]
                    v = tt("vector", y[:, half * 512:(half + 1) * 512], b.t[:, :], gate_rows[:, sub, half * 512:(half + 1) * 512],
                           ALU.mult, m, t_gate[sub], loose=True)
                    banks.give(b, v)
                stt(y, x_tok[:, t, :], ALPHA, y, ALU.mult, ALU.add, x_state["x"][t])
                st = stats[:, t, :]
                for half in range(2):
                    V(lambda e, o=st[:, 6 * half:6 * half + 6], i_=y[:, half * 512:(half + 1) * 512]: e.bn_stats(o, i_))
                v = V(lambda e, o=st[:, 12:14], i_=st[:, 0:12]: e.bn_aggr(o, i_))
                mean, var, tmp, rstd, shift = (st[:, 12 + i:13 + i] for i in range(5))
                copy("vector", st[:, 17:18], var)
                v = rsqrt_col(rstd, st[:, 17:18], tmp, 1e-5)
                v = stt(shift, mean, -1.0, rstd, ALU.mult, ALU.mult)
                tr.append(act(n_tok[:, t, :], y, ACT.Identity, v, scale=rstd, bias=shift, *()))
                if next_mod:
                    done += to_features(n_tok[:, t, :], tr[t], hT, mod_cols[:, 0, :], mod_cols[:, 1, :], t_mod, (m,), t)
                tt("gpsimd", x_tok[:, t, :], n_tok[:, t, :], ln_rows[:, 0, :], ALU.mult, tr[t], *rows_in)
                g_ = tt("gpsimd", x_tok[:, t, :], x_tok[:, t, :], ln_rows[:, 1, :], ALU.add)
                xs.append(g_)
            gate_reader[sub] = v
            ln_reader[0] = g_
            x_state["x"] = xs
            return done

        u_base = wk
        ar.at = phase_base
        uT = ar.take(32, SEQ)

        def mlp(w1, w2, src, t_src, between=None, toks=slice(0, SEQ)):
            w1 = w1.rearrange("(k p) n -> p k n", p=P)
            t_u = []
            for c in range(DFF // 512):
                w, landed, slot = ring.load(w1[:, :, c * 512:(c + 1) * 512])
                for i in range(4):
                    b = banks.take()
                    m = feature_product(w, i * P, P, src, toks, b.t[:, 0:SEQ], landed, *t_src, *b.after)
                    r = act(uT[:, c * 4 + i, :], b.t[:, 0:SEQ], ACT.Relu, m)
                    g_ = tt("gpsimd", uT[:, c * 4 + i, :], uT[:, c * 4 + i, :], uT[:, c * 4 + i, :], ALU.mult, r, loose=True)
                    banks.give(b, r)
                    t_u.append(g_)
                ring.done(slot, m)
                if between is not None:
                    between(c)
            ys, m = out_product(k_chunks(w2), uT, lambda k: (t_u[k],),
                                (lambda c: between(8 + c)) if between is not None else None)
            return ys, m

        ys, m = out_product(k_chunks(I["ev_w_out"][0]), oT, lambda k: t_oT)
        t_h = residual_norm(ys, m, 0, 0, lambda: modulation(1, 0))

        later = [0, 1, 2, 3, 4, 5, 6, 7, 8, 9]

        def ada_between(c):
            if c >= 1 and c - 1 < len(later):
                ada_chunk(1, later[c - 1])

        ys, m = mlp(I["mlp_w1"][0], I["mlp_w2"][0], hT, t_h, ada_between)
        t_h = residual_norm(ys, m, 1, 1, lambda: modulation(0, 1))

        ar.at = phase_base
        q2T = ar.take(8, SEQ)
        k2T = ar.take(8, SEQ)
        v2 = ar.take(QT, D)
        zb = ar.take(NB, UC)
        pT = ar.take(NB, UC)
        ust = ar.take(NB, 8)
        o_tok = ar.take(2, SEQ)
        o_st = ar.take(2, 8)
        lam = ar.take(4 * 64)
        lam_p = ar.take(2 * 64)
        lam_c = ar.take(4)
        z_reader, pT_reader = [(m,)] * NB, [(m,)] * NB
        in_lam = q.load("lam", lam, I["diff_lam"][0].rearrange("a d -> (a d)").partition_broadcast(P), m)
        l4 = lam.rearrange("p (a b d) -> p a b d", a=2, b=2)
        tt("vector", lam_p.rearrange("p (a d) -> p a d", a=2), l4[:, :, 0, :], l4[:, :, 1, :], ALU.mult, in_lam)
        v1 = reduce_(lam_c[:, 0:2], lam_p.rearrange("p (a d) -> p a d", a=2), ALU.add)
        s1 = act(lam_c[:, 0:2], lam_c[:, 0:2], ACT.Exp, v1)
        tt("vector", lam_c[:, 2:3], lam_c[:, 1:2], lam_c[:, 0:1], ALU.subtract, s1)
        t_lam = ts("vector", lam_c[:, 2:3], lam_c[:, 2:3], -LAMBDA_INIT, None, ALU.add, None)

        w_od = I["od_w_in"][0].rearrange("(k p) n -> p k n", p=P)
        for part, dst in ((0, q2T), (1, k2T)):
            for c in range(2):
                w, landed, slot = ring.load(w_od[:, :, part * D + c * 512:part * D + (c + 1) * 512])
                for i in range(4):
                    b = banks.take()
                    m = feature_product(w, i * P, P, hT, all_toks, b.t[:, 0:SEQ], landed, *t_h, *b.after)
                    t_qk = copy("scalar", dst[:, c * 4 + i, :], b.t[:, 0:SEQ], m)
                    banks.give(b, t_qk)
                ring.done(slot, m)
        for c in range(2):
            w, landed, slot = ring.load(w_od[:, :, 2 * D + c * 512:2 * D + (c + 1) * 512])
            for t in range(QT):
                b = banks.take()
                m = token_product(w, 0, 512, hT, slice(t * P, (t + 1) * P), b.t[:, :], landed, *b.after)
                t_v2 = copy("scalar", v2[:, t, c * 512:(c + 1) * 512], b.t[:, :], m)
                banks.give(b, t_v2)
            ring.done(slot, m)

        t_oT = []
        subln = ar.take(1)
        t_subln = ts("vector", subln, col("subln"), 1.0 - LAMBDA_INIT, None, ALU.mult, None)

        def diff_unit(h):
            ua, ub = {}, {}
            o_reader = {}

            def logits():
                for mp, u in ((0, ua), (1, ub)):
                    lo = mp * HALF

                    def coef(st, v):
                        return ts("vector", st[:, 4:6], st[:, 4:6], lam_c[:, 2:3], None, ALU.mult, None, t_lam)
                    unit_logits(u, lambda t: q2T[lo:lo + HALF, h, t * P:(t + 1) * P],
                                lambda k: k2T[lo:lo + HALF, h, k], SCALE, lambda: bias_pair(2 * h + mp), (t_qk,),
                                coef if mp else None)
                unit_scale(ua)
                stt(ua["z"][:, 0:P], ub["z"][:, 0:P], ub["st"][:, 4:5], ua["z"][:, 0:P], ALU.mult, ALU.add, ua["p"])
                v = stt(ua["z"][:, P:UC], ub["z"][:, P:UC], ub["st"][:, 5:6], ua["z"][:, P:UC], ALU.mult, ALU.add)
                ua["p"] = v
                z_reader[ub["s"]] = (v,)

            def values():
                s = h % 2
                p_ = pT[:, ua["s"], :]
                b = banks.take()
                mm(b.t[:, 0:P], p_[:, 0:P], v2[:, 0, h * P:(h + 1) * P], ua["pT"], t_v2, *b.after)
                mm(b.t[:, P:SEQ], p_[:, P:SEQ], v2[:, 0, h * P:(h + 1) * P], stop=False)
                m = mm(b.t[:, P:SEQ], p_[:, SEQ:UC], v2[:, 1, h * P:(h + 1) * P], start=False)
                pT_reader[ua["s"]] = (m,)
                st, o = o_st[:, s, :], o_tok[:, s, :]
                for t in range(QT):
                    s1 = act(o[:, t * P:(t + 1) * P], b.t[:, t * P:(t + 1) * P], ACT.Square, m, o_free[s],
                             accum=st[:, t:t + 1])
                ts("vector", st[:, 0:2], st[:, 0:2], 1.0 / P, None, ALU.mult, None, s1)
                v = rsqrt_col(st[:, 2:4], st[:, 0:2], st[:, 4:6], 1e-5)
                for t in range(QT):
                    v = ts("vector", o[:, t * P:(t + 1) * P], b.t[:, t * P:(t + 1) * P], st[:, 2 + t:3 + t], None,
                           ALU.mult, None)
                banks.give(b, v)
                ua["o"] = v

            def turn():
                s = h % 2
                b = banks.take()
                for t in range(QT):
                    m = turned(b.t[:, t * P:(t + 1) * P], o_tok[:, s, t * P:(t + 1) * P], ident,
                           ua["o"], *b.after)
                o_free[s] = m
                c = act(oT[:, h, :], b.t[:, 0:SEQ], ACT.Copy, m, t_subln, scale=subln[:, 0:1])
                banks.give(b, c)
                t_oT.append(c)
            return [logits, lambda: unit_transpose(ua), values, turn]

        o_free = [None, None]
        run_units([diff_unit(h) for h in range(8)], (0, 1, 2, 3))
        ada_chunk(1, 10)
        ada_chunk(1, 11)
        ys, m = out_product(k_chunks(I["od_w_out"][0]), oT, lambda k: t_oT)
        t_h = residual_norm(ys, m, 0, 2, lambda: modulation(1, 2))
        ar.at = phase_base
        uT = ar.take(32, SEQ)
        ys, m = mlp(I["mlp_w1"][1], I["mlp_w2"][1], hT, t_h)
        residual_norm(ys, m, 1, 3, None)
        ar.at = after_cols
        TT_ROWS = (P, P, META)
        TOK_AT = (META, META + P, 0)
        masks = ar.take(4 + 2 * LEVELS, P)
        a_log_row, dtb_row = ar.take(8), ar.take(8)
        qk_norm_row = ar.take(2, 64)
        rope = ar.take(3, 64)
        cT = ar.take(12, L2)
        kv_tok = ar.take(3, 2, 512)
        z_tok = ar.take(QT, 512)
        aqk = ar.take(3, 10, 64)
        av = ar.take(3, P)
        ba = ar.take(3, 16)
        o_acc = ar.take(QT, 512)
        st2 = ar.take(3, 24)
        ex_row = ar.take(8)
        delta_at = ar.at
        n2 = ar.take(3, D)
        u2T = ar.take(KT, L2)
        meta_tok = ar.take(D, rows=META)
        conv = ar.take(12, L2 + 4)
        end_block_one = [m, *x_state["x"]]
        in_masks = q.load("masks", masks.rearrange("p a b -> p (a b)"), I["square_masks"][:, P:], *end_block_one)
        in_alog = q.load("alog", a_log_row, I["a_log_2"][0].rearrange("a b -> (a b)").partition_broadcast(P), *end_block_one)
        in_dtb = q.load("dtb", dtb_row, I["dt_bias_2"][0].rearrange("a b -> (a b)").partition_broadcast(P), *end_block_one)
        in_qn = q.load("qn", qk_norm_row[:, 0, :], I["q_norm_2"][0].partition_broadcast(P), *end_block_one)
        in_kn = q.load("kn", qk_norm_row[:, 1, :], I["k_norm_2"][0].partition_broadcast(P), *end_block_one)
        in_meta = q.load("meta", meta_tok, I["meta_tokens_2"][:, :], *end_block_one)
        in_rope = [q.load(f"rope{t}", rope[0:TT_ROWS[t], t, :], I["rope_tables"][t * P:t * P + TT_ROWS[t], :], *end_block_one)
                   for t in range(3)]

        def rms_rows(src, t_src, dst, rows, st, width, eps, *after):
            s1 = act(dst, src, ACT.Square, t_src, *after, accum=st[0:rows, 0:1])
            ts("vector", st[0:rows, 1:2], st[0:rows, 0:1], 1.0 / width, None, ALU.mult, None, s1)
            v = rsqrt_col(st[0:rows, 2:3], st[0:rows, 1:2], st[0:rows, 3:4], eps)
            return act(dst, src, ACT.Copy, v, scale=st[0:rows, 2:3])

        t_u = []
        for t in (0, 1, 2):
            src = x_tok[:, t, :] if t < 2 else meta_tok
            t_src = x_state["x"][t] if t < 2 else in_meta
            s1 = rms_rows(src, t_src, n2[0:TT_ROWS[t], t, :], TT_ROWS[t], st2[:, t, :], D, 1e-6, *end_block_one)
            t_u += to_features(n2[0:TT_ROWS[t], t, :], s1, u2T, col("mix_pre", 0, KT), None, t_cols, (m,), t,
                               TT_ROWS[t], TOK_AT[t])

        w_in = I["w_in_2"][0].rearrange("(k p) n -> p k n", p=P)
        every = slice(0, L2)
        t_pad = memset("gpsimd", conv[:, :, 0:2], 0.0)
        t_pad = memset("gpsimd", conv[:, :, L2 + 2:L2 + 4], 0.0)
        t_conv_in = []
        for part in range(3):
            w, landed, slot = ring.load(w_in[:, :, part * 512:(part + 1) * 512])
            for i in range(4):
                b = banks.take()
                m = feature_product(w, i * P, P, u2T, every, b.t[:, 0:L2], landed, *t_u, *b.after)
                c = copy("scalar", conv[:, part * 4 + i, 2:L2 + 2], b.t[:, 0:L2], m)
                banks.give(b, c)
                t_conv_in.append(c)
            ring.done(slot, m)

        def conv_tile(i):
            tap = lambda j: col("conv", j * 12 + i)
            v = ts("vector", cT[:, i, :], conv[:, i, 0:L2], tap(0), None, ALU.mult, None, t_conv_in[i], t_pad, t_cols_b)
            for j in range(1, 5):
                v = stt(cT[:, i, :], conv[:, i, j:j + L2], tap(j), cT[:, i, :], ALU.mult, ALU.add)
            return v

        def silu(dst, x, tmp, *after):
            v = ts("vector", tmp, x, -EXP_MAX, None, ALU.max, None, *after)
            s_ = act(tmp, tmp, ACT.Exp, v, scale=-1.0)
            ts("vector", tmp, tmp, 1.0, None, ALU.add, None, s_)
            recip(tmp, tmp)
            return tt("vector", dst, x, tmp, ALU.mult)

        t_cT = [None] * 12
        for g4 in range(3):
            for i in range(4 * g4, 4 * g4 + 4):
                v = conv_tile(i)
            grp = slice(4 * g4, 4 * g4 + 4)
            v = silu(cT[:, grp, :], cT[:, grp, :], conv[:, grp, 0:L2], v)
            for i in range(4 * g4, 4 * g4 + 4):
                if g4 == 2:
                    t_cT[i] = v
                    continue
                sq_ = conv[:, i, 0:L2]
                v1 = tt("vector", sq_, cT[:, i, :], cT[:, i, :], ALU.mult)
                b = banks.take()
                m1 = mm(b.t[:, 0:L2], ones, sq_, v1, *b.after)
                s_ = act(sq_, b.t[:, 0:L2], ACT.Ln, m1, m_eps, bias=eps6[:, 0:1])
                banks.give(b, s_)
                s_ = act(sq_, sq_, ACT.Exp, scale=-0.5)
                if g4 == 0:
                    t_cT[i] = stt(cT[:, i, :], sq_, P ** -0.5, cT[:, i, :], ALU.mult, ALU.mult, s_)
                else:
                    t_cT[i] = tt("vector", cT[:, i, :], sq_, cT[:, i, :], ALU.mult, s_)

        w, landed, slot = ring.load(w_in[:, :, 1536:2048])
        for t in range(QT):
            b = banks.take()
            m = token_product(w, 0, 512, u2T, slice(TOK_AT[t], TOK_AT[t] + P), b.t[:, :], landed, *b.after)
            t_z = copy("scalar", z_tok[:, t, :], b.t[:, :], m)
            banks.give(b, t_z)
        ring.done(slot, m)
        w, landed, slot = ring.load(w_in[:, :, 2048:2320])
        for t in range(3):
            r = TT_ROWS[t]
            n = 272 if t < 2 else 16
            b = banks.take()
            m = token_product(w, 0, n, u2T, slice(TOK_AT[t], TOK_AT[t] + r), b.t[0:r, 0:n], landed, *b.after)
            t_ba = copy("scalar", ba[0:r, t, :], b.t[0:r, 0:16], m)
            if t < 2:
                t_ba = copy("scalar", aqk[:, t, 0:4, :], b.t[:, 16:272].rearrange("p (h d) -> p h d", d=64), m)
            banks.give(b, t_ba)
        ring.done(slot, m)
        w, landed, slot = ring.load(w_in[:, :, 2320:2832])
        for t in range(3):
            r = TT_ROWS[t]
            n0 = 0 if t < 2 else 256
            b = banks.take()
            m = token_product(w, n0, 512 - n0, u2T, slice(TOK_AT[t], TOK_AT[t] + r), b.t[0:r, n0:512], landed, *b.after)
            h0 = 4 if t < 2 else 8
            copy("scalar", aqk[0:r, t, h0:10, :], b.t[0:r, n0:384].rearrange("p (h d) -> p h d", d=64), m)
            t_av = copy("scalar", av[0:r, t, :], b.t[0:r, 384:512])
            banks.give(b, t_av)
        ring.done(slot, m)
        proj_done = m

        s1 = act(ex_row, a_log_row, ACT.Exp, in_alog)
        ts("vector", ex_row, ex_row, -1.0, None, ALU.mult, None, s1)
        for t in range(3):
            r = TT_ROWS[t]
            b_, g_, tmp = ba[0:r, t, 0:8], ba[0:r, t, 8:16], st2[0:r, t, 8:16]
            silu_tmp = st2[0:r, t, 16:24]
            v = ts("vector", tmp, b_, -EXP_MAX, None, ALU.max, None, t_ba)
            s1 = act(tmp, tmp, ACT.Exp, v, scale=-1.0)
            ts("vector", tmp, tmp, 1.0, None, ALU.add, None, s1)
            recip(b_, tmp)
            v = tt("vector", g_, g_, dtb_row[0:r, :], ALU.add, in_dtb)
            ts("vector", silu_tmp, g_, -1.0, None, ALU.mult, None)
            v = tt("vector", tmp, g_, silu_tmp, ALU.max)
            act(tmp, tmp, ACT.Exp, v, scale=-1.0)
            s1 = act(tmp, tmp, ACT.Ln, bias=ones[0:r, 0:1])
            stt(g_, g_, 0.0, tmp, ALU.max, ALU.add, s1)
            t_bg = tt("vector", g_, g_, ex_row[0:r, :], ALU.mult)

        for kv in range(2):
            for t in range(3):
                r = TT_ROWS[t]
                b = banks.take()
                for h in range(4):
                    m = turned(b.t[0:r, h * P:(h + 1) * P], cT[:, 4 + 4 * kv + h, TOK_AT[t]:TOK_AT[t] + r], ident,
                               *t_cT, *b.after)
                t_kv = copy("scalar", kv_tok[0:r, t, kv, :], b.t[0:r, :], m)
                banks.give(b, t_kv)

        ar.at = delta_at
        rot = ar.take(3, 10, 64)
        sqk = ar.take(10, 64)
        rst = ar.take(3, 3, 10)
        aT = ar.take(4, SEQ)
        akT = ar.take(2, L2)
        t_rot = []
        for t in range(3):
            r, h0 = TT_ROWS[t], 0 if t < 2 else 8
            x_ = aqk[0:r, t, h0:10, :]
            n = 10 - h0
            sq_ = sqk[0:r, h0:10, :]
            s0_, s1_, s2_ = (rst[0:r, t, i, h0:10] for i in range(3))
            tt("vector", sq_, x_, x_, ALU.mult, t_av, proj_done)
            reduce_(s0_, sq_, ALU.add)
            ts("vector", s0_, s0_, 1.0 / 64, None, ALU.mult, None)
            rsqrt_col(s1_, s0_, s2_, 1e-6)
            tt("vector", x_, x_, s1_.unsqueeze(2).broadcast_to([r, n, 64]), ALU.mult)
            if t < 2:
                tt("vector", x_[:, 0:8, :], x_[:, 0:8, :],
                   qk_norm_row[0:r, 0:1, :].broadcast_to([r, 8, 64]), ALU.mult, in_qn)
            tt("vector", x_[:, n - 2:n, :], x_[:, n - 2:n, :],
               qk_norm_row[0:r, 1:2, :].broadcast_to([r, 2, 64]), ALU.mult, in_kn)
            for ax in range(2):
                lo_, hi_ = x_[:, :, 32 * ax:32 * ax + 16], x_[:, :, 32 * ax + 16:32 * ax + 32]
                cos = rope[0:r, t, 16 * ax:16 * ax + 16].unsqueeze(1).broadcast_to([r, n, 16])
                sin = rope[0:r, t, 32 + 16 * ax:48 + 16 * ax].unsqueeze(1).broadcast_to([r, n, 16])
                o_lo = rot[0:r, t, h0:10, 32 * ax:32 * ax + 16]
                o_hi = rot[0:r, t, h0:10, 32 * ax + 16:32 * ax + 32]
                tmp = sq_[:, :, 0:16]
                tt("vector", o_lo, lo_, cos, ALU.mult, in_rope[t])
                tt("vector", tmp, hi_, sin, ALU.mult)
                tt("vector", o_lo, o_lo, tmp, ALU.subtract)
                tt("vector", o_hi, hi_, cos, ALU.mult)
                tt("vector", tmp, lo_, sin, ALU.mult)
                v = tt("vector", o_hi, o_hi, tmp, ALU.add)
            t_rot.append(v)
        for t in range(QT):
            b = banks.take()
            for i in range(4):
                m = turned(b.t[:, i * P:(i + 1) * P], rot[:, t, 2 * i:2 * i + 2, :].rearrange("p a b -> p (a b)"), ident,
                           t_rot[t], *b.after)
            t_aT = copy("scalar", aT[:, :, t * P:(t + 1) * P], b.t[:, :].rearrange("p (a b) -> p a b", a=4), m)
            banks.give(b, t_aT)
        b = banks.take()
        for t in range(3):
            r = TT_ROWS[t]
            m = turned(b.t[:, t * P:t * P + r], rot[0:r, t, 8:10, :].rearrange("p a b -> p (a b)"), ident[0:r, 0:r],
                       t_rot[t], *b.after)
        for g in range(2):
            for half in range(2):
                t_ak = copy("scalar", akT[half * HALF:(half + 1) * HALF, g, :], b.t[g * HALF:(g + 1) * HALF, 0:L2], m)
        banks.give(b, t_ak)

        NA = 4
        za = ar.take(NA, L2)
        paT = ar.take(NA, 3 * P)
        ast = ar.take(NA, 4)
        za_reader, paT_reader = [None] * NA, [None] * NA
        a_n = [0]
        a_bank = {}
        t_oT = []

        def axial_unit(h, t):
            u = {}
            lo, pair, g = h % 2 * HALF, h // 2, h // 4

            def logits():
                s = u["s"] = a_n[0] % NA
                a_n[0] += 1
                b = banks.take()
                m = mm(b.t[:, 0:L2], aT[lo:lo + HALF, pair, t * P:(t + 1) * P], akT[lo:lo + HALF, g, :], t_aT, t_ak,
                       *b.after)
                st = ast[:, s, :]
                reduce_(st[:, 0:1], b.t[:, 0:L2], ALU.max, m, negate=True)
                v = ts("vector", st[:, 0:1], st[:, 0:1], SCALE, None, ALU.mult, None)
                a = act(za[:, s, :], b.t[:, 0:L2], ACT.Exp, v, za_reader[s], bias=st[:, 0:1], scale=SCALE,
                        accum=st[:, 1:2], loose=True)
                banks.give(b, a)
                v = recip(st[:, 2:3], st[:, 1:2], a)
                u["p"] = ts("gpsimd", za[:, s, :], za[:, s, :], st[:, 2:3], None, ALU.mult, None, v, loose=True)

            def turn():
                s = u["s"]
                b = banks.take()
                turned(b.t[:, 0:P], za[:, s, 0:P], ident, u["p"], *b.after)
                turned(b.t[:, P:2 * P], za[:, s, P:2 * P], ident)
                m = turned(b.t[0:META, 2 * P:3 * P], za[:, s, SEQ:L2], ident)
                za_reader[s] = m
                copy("scalar", paT[:, s, 0:SEQ], b.t[:, 0:SEQ], m, paT_reader[s], loose=True)
                u["pT"] = copy("scalar", paT[0:META, s, SEQ:3 * P], b.t[0:META, SEQ:3 * P])
                banks.give(b, u["pT"])

            def values():
                s = u["s"]
                if h % 2 == 0:
                    a_bank[pair, t] = banks.take()
                b = a_bank[pair, t]
                o = b.t[lo:lo + HALF, 0:P]
                for kt in range(3):
                    r = TT_ROWS[kt]
                    m = mm(o, av[0:r, kt, g * HALF:(g + 1) * HALF], paT[0:r, s, kt * P:(kt + 1) * P], u["pT"], t_av,
                           *b.after, start=kt == 0, stop=kt == 2)
                paT_reader[s] = m
                if h % 2:
                    c = copy("vector", oT[:, 4 + pair, t * P:(t + 1) * P], b.t[:, 0:P], m)
                    banks.give(b, c)
                    t_oT.append(c)
            return [logits, turn, values]

        run_units([axial_unit(2 * pair + i, t) for pair in range(4) for t in range(QT) for i in range(2)], (0, 2, 3))
        axial_done = m = t_oT[-1]

        ar.at = delta_at
        names = ("a", "qk", "aT", "lT", "x", "xT", "w", "bv", "bek", "kdec", "qdec", "s")
        buf = [{n: ar.take(4, P) for n in names} for _ in range(2)]
        dst_ = [ar.take(6, 4) for _ in range(2)]
        t_o = [None] * QT
        t_s = [None, None]

        def chunk(d, t, first):
            B, st = buf[d], dst_[d]
            C, at = TT_ROWS[t], TOK_AT[t]
            back = d if t < 2 else 0
            real = t < 2
            M1, strict = masks[0:C, back, 0:C], masks[0:C, 2 + back, 0:C]
            level = lambda l, back_: masks[0:C, 4 + LEVELS * back_ + l, 0:C]
            beta, g = ba[0:C, t, 4 * d:4 * d + 4], ba[0:C, t, 8 + 4 * d:12 + 4 * d]
            wide = lambda a: a.unsqueeze(1).broadcast_to([C, 4, C])
            per = lambda c: c.unsqueeze(2).broadcast_to([C, 4, P])
            v_ = lambda n, w_=C: B[n][0:C, :, 0:w_]
            gc, e_tot, e_gc, e_last, bg = (st[:, i, :] for i in range(5))
            cols_ = slice(at, at + C)

            b = banks.take()
            mm(b.t[0:C, 0:4], M1, g, t_bg, in_masks, axial_done, *b.after)
            m = mm(b.t[:, 4:8], ones[0:C, :], g)
            copy("scalar", gc[0:C], b.t[0:C, 0:4], m, t_s[d])
            act(e_last, b.t[:, 4:8], ACT.Exp)
            c = copy("scalar", e_tot[0:C], b.t[0:C, 4:8])
            banks.give(b, c)
            v = tt("vector", e_tot[0:C], e_tot[0:C], gc[0:C], ALU.subtract, c)
            act(e_tot[0:C], e_tot[0:C], ACT.Exp, v)
            s_ = act(e_gc[0:C], gc[0:C], ACT.Exp)
            v = tt("vector", bg[0:C], e_gc[0:C], beta, ALU.mult, s_)
            gw = copy("gpsimd", B["w"][0:C], per(g), t_bg, m, t_s[d])
            yield
            R = banks.take()
            for h in range(4):
                m = mm(R.t[0:P if real else C, h * P:h * P + C], B["w"][0:C, h, 0:P if real else C], M1, gw, *R.after)
            Rv = R.t[:, :].rearrange("p (h c) -> p h c", h=4)
            K = banks.take()
            for h in range(4):
                kT_ = cT[:, 4 + h, cols_]
                mk = mm(K.t[0:C, h * P:h * P + C], kT_, kT_, *t_cT, *K.after)
            for h in range(4):
                v = ts("vector", B["a"][0:C, h, 0:C], Rv[0:C, h, 0:C], gc[0:C, h:h + 1], 0.0, ALU.subtract, ALU.max, m)
                if real:
                    v = ts("vector", B["qk"][0:C, h, 0:C], Rv[0:C, h, 0:C], gc[0:C, h:h + 1], 0.0, ALU.subtract, ALU.min)
            if real:
                act(B["qdec"], Rv, ACT.Exp, v)
            s_ = act(v_("a"), v_("a"), ACT.Exp, v, scale=-1.0)
            banks.give(R, s_)
            yield
            v = tt("vector", v_("a"), v_("a"), wide(strict), ALU.mult, s_)
            for h in range(4):
                v = stt(B["a"][0:C, h, 0:C], K.t[0:C, h * P:h * P + C], beta[:, h:h + 1], B["a"][0:C, h, 0:C], ALU.mult, ALU.mult, mk)
            banks.give(K, v)
            b = banks.take()
            for h in range(4):
                m = turned(b.t[0:C, h * P:h * P + C], B["a"][0:C, h, 0:C], ident[0:C, 0:C], v, *b.after)
            c = copy("scalar", v_("aT"), b.t[0:C, :].rearrange("p (h c) -> p h c", h=4)[:, :, 0:C], m)
            banks.give(b, c)
            tt("gpsimd", v_("x"), v_("a"), wide(level(0, 1 - back)), ALU.mult, v)
            gx = tt("gpsimd", v_("xT"), v_("aT"), wide(level(0, back)), ALU.mult, c)
            tt("gpsimd", B["bv"][0:C], kv_tok[0:C, t, 1, :].rearrange("p (h c) -> p h c", h=4), per(beta), ALU.mult, t_kv)
            if real:
                act(B["qk"], B["qk"], ACT.Exp)
                tt("gpsimd", B["qdec"], B["qdec"], cT[:, 0:4, cols_], ALU.mult)
            yield
            idn = wide(ident[0:C, 0:C])
            tt("vector", v_("x"), idn, v_("x"), ALU.subtract, gx)
            v = tt("vector", v_("xT"), idn, v_("xT"), ALU.subtract)
            n_levels = LEVELS if real else 4
            for l in range(1, n_levels):
                lt = "lT" if l % 2 else "a"
                g_ = tt("gpsimd", v_(lt), v_("aT"), wide(level(l, back)), ALU.mult, *((v,) if l == 1 else (mw,)))
                if l == 1:
                    tt("gpsimd", B["bek"][0:C], kv_tok[0:C, t, 0, :].rearrange("p (h c) -> p h c", h=4), per(bg[0:C]), ALU.mult, t_kv)
                    gk = tt("gpsimd", B["kdec"][0:C], kv_tok[0:C, t, 0, :].rearrange("p (h c) -> p h c", h=4), per(e_tot[0:C]), ALU.mult)
                b = banks.take()
                for h in range(4):
                    mw = mm(b.t[0:C, h * P:h * P + C], B[lt][0:C, h, 0:C], B["x"][0:C, h, 0:C], g_, v, *b.after)
                c = copy("scalar", v_("w"), b.t[0:C, :].rearrange("p (h c) -> p h c", h=4)[:, :, 0:C], mw)
                banks.give(b, c)
                yield
                last = l == n_levels - 1
                b2 = banks.take()
                b1 = None if last else banks.take()
                for h in range(4):
                    m2 = mm(b2.t[0:C, h * P:h * P + C], B["w"][0:C, h, 0:C], B["xT"][0:C, h, 0:C], c, *b2.after)
                if not last:
                    for h in range(4):
                        m1 = mm(b1.t[0:C, h * P:h * P + C], B["xT"][0:C, h, 0:C], B["w"][0:C, h, 0:C], *b1.after)
                    m2 = m1
                v = tt("vector", v_("xT"), v_("xT"), b2.t[0:C, :].rearrange("p (h c) -> p h c", h=4)[:, :, 0:C], ALU.subtract, m2)
                banks.give(b2, v)
                if not last:
                    v = tt("vector", v_("x"), v_("x"), b1.t[0:C, :].rearrange("p (h c) -> p h c", h=4)[:, :, 0:C], ALU.subtract)
                    banks.give(b1, v)
                yield
            if real:
                b = banks.take()
                for h in range(4):
                    m = mm(b.t[:, h * P:(h + 1) * P], cT[:, 4 + h, cols_], cT[:, h, cols_], *b.after)
                vq = tt("vector", B["qk"], B["qk"], wide(M1), ALU.mult)
                vq = tt("vector", B["qk"], B["qk"], b.t[:, :].rearrange("p (h c) -> p h c", h=4), ALU.mult, m)
                banks.give(b, vq)
                b = banks.take()
                for h in range(4):
                    m = mm(b.t[:, h * P:(h + 1) * P], B["bek"][:, h, :], B["xT"][:, h, :], gk, v, *b.after)
                nw = act(B["x"], b.t[:, :].rearrange("p (h c) -> p h c", h=4), ACT.Copy, m, scale=-1.0)
                banks.give(b, nw)
                yield
            b = banks.take()
            for h in range(4):
                m = mm(b.t[0:C, h * P:(h + 1) * P], B["xT"][0:C, h, 0:C], B["bv"][0:C, h, :], v, gk, *b.after, stop=not real)
                if real:
                    m = mm(b.t[0:C, h * P:(h + 1) * P], B["x"][:, h, :], B["s"][:, h, :], nw, t_s[d], start=False)
            vn = copy("scalar", B["bek"][0:C], b.t[0:C, :].rearrange("p (h c) -> p h c", h=4), m)
            banks.give(b, vn)
            yield
            if real:
                b = banks.take()
                for h in range(4):
                    mm(b.t[:, h * P:(h + 1) * P], B["qdec"][:, h, :], B["s"][:, h, :], *b.after, stop=False)
                    m = mm(b.t[:, h * P:(h + 1) * P], B["qk"][:, h, :], B["bek"][:, h, :], vn, vq, start=False)
                if t_o[t] is None:
                    t_o[t] = copy("vector", o_acc[:, t, :], b.t[:, :], m)
                else:
                    t_o[t] = tt("vector", o_acc[:, t, :], o_acc[:, t, :], b.t[:, :], ALU.add, m)
                banks.give(b, t_o[t])
                if not first:
                    return
            b = banks.take()
            for h in range(4):
                m = mm(b.t[:, h * P:(h + 1) * P], B["kdec"][0:C, h, :], B["bek"][0:C, h, :], gk, vn, *b.after)
            if not real:
                v = copy("vector", B["s"], b.t[:, :].rearrange("p (h c) -> p h c", h=4), m)
            else:
                for h in range(4):
                    v = stt(B["s"][:, h, :], B["s"][:, h, :], e_last[:, h:h + 1], b.t[:, h * P:(h + 1) * P], ALU.mult, ALU.add, m)
            banks.give(b, v)
            t_s[d] = v
            yield

        for order in ((2, 2), (0, 1), (1, 0)):
            live = [chunk(d, order[d], order == (0, 1)) for d in range(2)]
            while live:
                live = [c for c in live if next(c, "end") != "end"]

        ztmp = buf[0]["a"].rearrange("p h c -> p (h c)")
        osq = buf[0]["qk"]
        dn = []
        for t in range(QT):
            z_ = z_tok[:, t, :]
            silu(z_, z_, ztmp, t_z, m)
            o4 = o_acc[:, t, :].rearrange("p (h c) -> p h c", h=4)
            tt("vector", osq, o4, o4, ALU.mult, t_o[t])
            s0_, s1_, s2_ = (st2[:, t, 4 * i:4 * i + 4] for i in range(3))
            reduce_(s0_, osq, ALU.add)
            ts("vector", s0_, s0_, 1.0 / P, None, ALU.mult, None)
            rsqrt_col(s1_, s0_, s2_, 1e-6)
            tt("vector", o4, o4, s1_.unsqueeze(2).broadcast_to([P, 4, P]), ALU.mult)
            v = tt("vector", o_acc[:, t, :], o_acc[:, t, :], z_, ALU.mult)
            b = banks.take()
            for h in range(4):
                m2 = turned(b.t[:, h * P:(h + 1) * P], o_acc[:, t, h * P:(h + 1) * P], ident, v, *b.after)
            c = act(oT[:, 0:4, t * P:(t + 1) * P], b.t[:, :].rearrange("p (a b) -> p a b", a=4), ACT.Copy, m2,
                    scale=col("dn_norm"))
            banks.give(b, c)
            dn.append(c)
        t_oT = t_oT + dn

        ar.at = after_cols
        n_tok = ar.take(QT, D)
        hT = ar.take(KT, SEQ)
        uT = ar.take(32, SEQ)
        post = ar.take(2, D)
        st3 = ar.take(QT, 16)
        delta_done = dn[-1]
        in_post = [q.load(f"post{i}", post[:, i, :], I[name][0].partition_broadcast(P), delta_done)
                   for i, name in enumerate(("norm_mix_post_2", "norm_mlp_post_2"))]

        def post_norm_residual(ys, m, which):
            res = []
            for t in range(QT):
                st = st3[:, t, :]
                for half in range(2):
                    s1 = act(n_tok[:, t, half * 512:(half + 1) * 512], ys[t][half].t[:, :], ACT.Square, m, delta_done,
                             accum=st[:, half:half + 1])
                tt("vector", st[:, 2:3], st[:, 0:1], st[:, 1:2], ALU.add, s1)
                ts("vector", st[:, 2:3], st[:, 2:3], 1.0 / D, None, ALU.mult, None)
                rsqrt_col(st[:, 3:4], st[:, 2:3], st[:, 4:5], 1e-6)
                for half in range(2):
                    c = slice(half * 512, (half + 1) * 512)
                    v = stt(n_tok[:, t, c], ys[t][half].t[:, :], st[:, 3:4], post[:, which, c], ALU.mult, ALU.mult,
                            in_post[which])
                    banks.give(ys[t][half], v)
                res.append(tt("vector", x_tok[:, t, :], x_tok[:, t, :], n_tok[:, t, :], ALU.add))
            return res

        ys, m = out_product(k_chunks(I["w_out_2"][0]), oT, lambda k: t_oT)
        t_x = post_norm_residual(ys, m, 0)
        t_h = []
        for t in range(QT):
            s1 = rms_rows(x_tok[:, t, :], t_x[t], n_tok[:, t, :], P, st3[:, t, 8:16], D, 1e-6)
            t_h += to_features(n_tok[:, t, :], s1, hT, col("mlp_pre", 0, KT), None, t_cols, (delta_done,), t)
        ys, m = mlp(I["w_up_2"][0], I["w_down_2"][0], hT, t_h)
        t_x = post_norm_residual(ys, m, 1)
        out_sem = ctx.enter_context(nc.semaphore("out_stored"))
        for t in range(QT):
            stored = q.dma(lambda e, o=out[0, t * P:(t + 1) * P, :], i_=x_tok[:, t, :]: e.dma_start(o, i_),
                           out_sem, 16 * QT, t_x[t])
        q.stores.append(stored)
        finish(nc, q, ctx)


def finish(nc, q, ctx):
    block = ctx.enter_context(nc.Block())

    @block.sync
    def _(eng):
        q.emit("sync", eng)
        for name, sem, value in q.stores:
            eng.wait_ge(sem, value)

    @block.tensor
    def _(eng):
        q.emit("tensor", eng)

    @block.vector
    def _(eng):
        q.emit("vector", eng)

    @block.scalar
    def _(eng):
        q.emit("scalar", eng)

    @block.gpsimd
    def _(eng):
        q.emit("gpsimd", eng)


INPUTS = [
    "x", "c", "rel_bias", "ada_w", "ada_b", "ln_g", "ln_b", "ev_w_in", "ev_w_out", "nsa_pe_k", "nsa_pe_v",
    "nsa_w1_k", "nsa_w2_k", "nsa_w1_v", "nsa_w2_v", "dsa_kv_norm", "dsa_w_uk", "dsa_w_uv", "od_w_in", "od_w_out",
    "diff_lam", "diff_subln", "mlp_w1", "mlp_w2", "meta_tokens_2", "w_in_2", "conv_w_2", "a_log_2", "dt_bias_2",
    "dn_out_norm_2", "q_norm_2", "k_norm_2", "w_out_2", "norm_mix_pre_2", "norm_mix_post_2", "w_up_2",
    "w_down_2", "norm_mlp_pre_2", "norm_mlp_post_2",
]


def prepare(inputs):
    arrays = {n: np.ascontiguousarray(inputs[n]) for n in INPUTS}
    arrays["bucket_windows"] = bucket_windows()
    arrays["square_masks"] = square_masks()
    arrays["rope_tables"] = rope_tables()
    return arrays


def kernel(**inputs):
    import concourse.bacc as bacc
    from concourse.bass_utils import run_bass_kernel_spmd

    nc = bacc.Bacc("TRN2", target_bir_lowering=False, num_devices=1)
    arrays = prepare(inputs)
    aps = {n: nc.dram_tensor(n, a.shape, mybir.dt.from_np(a.dtype), kind="ExternalInput").ap()
           for n, a in arrays.items()}
    out = nc.dram_tensor("out", (1, SEQ, D), F32, kind="ExternalOutput").ap()
    program(nc, aps, out)
    r = run_bass_kernel_spmd(nc, [arrays], core_ids=[0])
    return r.results[0]["out"]
```

```python
import math
from contextlib import ExitStack

import numpy as np

import concourse.bass as bass
from concourse import mybir

F32 = mybir.dt.float32
F32R = mybir.dt.float32r
ALU = mybir.AluOpType
ACT = mybir.ActivationFunctionType
AX_X = mybir.AxisListType.X

P = 128
D = 1024
KT = D // P
SEQ = 256
QT = SEQ // P
DFF = 4 * D
META = 16
L2 = META + SEQ
ALPHA = (2 * 2) ** 0.25
NEG = -1e30
CLAMP = -1e29
REPLACED = -3e38
LAMBDA_INIT = 0.8 - 0.6 * math.exp(-0.3)
TOPK = 64
NUM_BUCKETS = 32
CMP_LEN, CMP_STRIDE = 32, 16
NCMP = (SEQ - CMP_LEN) // CMP_STRIDE + 1
SCALE = 64 ** -0.5
EXP_MAX = 80.0
SLOT = 2048
SLOTS = 4
ARENA = 28100
HL = KT * L2 + KT * SEQ
MLP_LAG = 2
SPLIT_SLOTS = 2
CW = SLOT // KT
KW = SLOT // D
LEVELS = 7


def t5_bucket(dist):
    n = np.maximum(dist, 0)
    exact = NUM_BUCKETS // 2
    nf = np.maximum(n, 1).astype(np.float32)
    large = exact + (np.log(nf / exact) / math.log(128 / exact) * (NUM_BUCKETS - exact)).astype(np.int32)
    return np.where(n < exact, n, np.minimum(large, NUM_BUCKETS - 1))


def bucket_rows():
    dist = 255 - np.arange(3 * P)
    hot = np.zeros((NUM_BUCKETS + 1, 3 * P), np.float32)
    hot[t5_bucket(dist), np.arange(3 * P)] = dist >= 0
    hot[NUM_BUCKETS] = dist < 0
    return hot


def square_masks():
    i, j = np.arange(P)[:, None], np.arange(P)[None, :]
    blocks = [i == j, i <= j, i >= j, i > j, i < j]
    for back in (0, 1):
        for level in range(LEVELS):
            b = 1 << level
            joined = (i // (2 * b) == j // (2 * b)) & (i // b % 2 == 0) & (j // b % 2 == 1)
            blocks.append(joined.T if back else joined)
    return np.concatenate(blocks, 1).astype(np.float32)


def rope_tables():
    grid, f = 64, 16
    t = np.arange(SEQ)
    freqs = np.float32(10000.0) ** (-np.arange(f, dtype=np.float32) / np.float32(f))
    ang = np.concatenate([(t // grid).astype(np.float32)[:, None] * freqs,
                          (t % grid).astype(np.float32)[:, None] * freqs], 1)
    ang = np.concatenate([ang, np.zeros((META, 2 * f), np.float32)], 0)
    return np.concatenate([np.cos(ang), np.sin(ang)], 1).astype(np.float32)


class Queues:

    def __init__(self, nc, ctx):
        self.nc, self.ctx = nc, ctx
        self.names = ("tensor", "vector", "scalar", "gpsimd", "sync")
        self.items = {n: [] for n in self.names}
        self.sem = {n: ctx.enter_context(nc.semaphore(f"done_{n}")) for n in self.names[:4]}
        self.count = dict.fromkeys(self.names, 0)
        self.stores = []

    def put(self, engine, emit, *after, loose=False):
        waits = [s for s in after if s is not None and not (engine == "tensor" and s[0] == "tensor")]
        if engine != "tensor" and not loose and self.count[engine]:
            waits.append((engine, self.sem[engine], self.count[engine]))
        self.count[engine] += 1
        self.items[engine].append((waits, emit, self.sem[engine], 1))
        return (engine, self.sem[engine], self.count[engine])

    def dma(self, emit, sem, total, *after, engine="sync"):
        waits = [s for s in after if s is not None]
        self.items[engine].append((waits, emit, sem, 16))
        return (sem.name, sem, total)

    def load(self, name, dst, src, *after, engine="sync"):
        sem = self.ctx.enter_context(self.nc.semaphore(f"in_{name}"))
        return self.dma(lambda e: e.dma_start(dst, src), sem, 16, *after, engine=engine)

    def emit(self, engine, eng):
        seen = {}
        for waits, emit, sem, by in self.items[engine]:
            for name, s, value in waits:
                if seen.get(name, 0) < value:
                    eng.wait_ge(s, value)
                    seen[name] = value
            emit(eng).then_inc(sem, by)


class Bank:
    def __init__(self, tensor):
        self.t, self.after = tensor, []


class Banks:

    def __init__(self, nc, ctx):
        self.free = [Bank(ctx.enter_context(nc.psum_tensor(f"bank{i}", [P, 512], F32))) for i in range(8)]

    def take(self):
        return self.free.pop(0)

    def give(self, bank, *readers):
        bank.after = list(readers)
        self.free.append(bank)


class Ring:

    def __init__(self, q, nc, ctx):
        self.q = q
        self.slots = [ctx.enter_context(nc.sbuf_tensor(f"ring{i}", [P, SLOT], F32)) for i in range(SLOTS)]
        self.sems = [ctx.enter_context(nc.semaphore(f"ring_in{i}")) for i in range(SLOTS)]
        self.uses = [0] * SLOTS
        self.reader = [None] * SLOTS
        self.n = 0

    def load(self, src):
        s = self.n % SLOTS
        self.n += 1
        view = shaped(self.slots[s], src.shape)
        self.uses[s] += 1
        assert self.uses[s] == 1 or self.reader[s] is not None
        landed = self.q.dma(lambda e: e.dma_start(view, src), self.sems[s], 16 * self.uses[s], self.reader[s])
        self.reader[s] = None
        return view, landed, s

    def done(self, slot, reader):
        self.reader[slot] = reader

    def lend(self):
        s = self.n % SLOTS
        self.n += 1
        return self.slots[s], s


class SplitWeights:

    def __init__(self, q, ring, nc, ctx, srcs):
        self.q, self.ring, self.srcs = q, ring, srcs
        self.highs = [ctx.enter_context(nc.sbuf_tensor(f"high{i}", [P, SLOT], F32R)) for i in range(SPLIT_SLOTS)]
        self.lows = [ctx.enter_context(nc.sbuf_tensor(f"low{i}", [P, SLOT], F32R)) for i in range(SPLIT_SLOTS)]
        self.reader = [None] * SPLIT_SLOTS
        self.queued = []
        self.n = 0

    def ahead(self):
        if self.n == len(self.srcs):
            return
        src, s = self.srcs[self.n], self.n % SPLIT_SLOTS
        assert self.n < SPLIT_SLOTS or self.reader[s] is not None
        raw, landed, slot = self.ring.load(src)
        high, low = shaped(self.highs[s], src.shape), shaped(self.lows[s], src.shape)
        rounded = self.q.put("scalar", lambda e: e.activation(high, raw, ACT.Copy), landed, self.reader[s])
        ready = self.q.put("vector", lambda e: e.tensor_tensor(low, raw, high.bitcast(F32), ALU.subtract), rounded)
        self.ring.done(slot, ready)
        self.reader[s] = None
        self.queued.append(((high, low), ready, s))
        self.n += 1

    def take(self):
        return self.queued.pop(0)

    def done(self, slot, reader):
        self.reader[slot] = reader


def shaped(tensor, shape):
    view = tensor[0:shape[0], 0:int(np.prod(shape[1:]))]
    return view.rearrange("p (a b) -> p a b", a=shape[1]) if len(shape) == 3 else view


class Arena:

    def __init__(self, nc, ctx, cols):
        self.t = ctx.enter_context(nc.sbuf_tensor("arena", [P, cols], F32))
        self.cols, self.at, self.top = cols, 0, 0

    def over(self, start, cols):
        a = object.__new__(Arena)
        a.t, a.cols, a.at, a.top = self.t, start + cols, start, 0
        return a

    def take(self, *shape, rows=P):
        n = int(np.prod(shape))
        assert self.at + n <= self.cols, f"arena: {self.at} + {n} of {self.cols}"
        a = self.t[0:rows, self.at:self.at + n]
        self.at += n
        self.top = max(self.top, self.at)
        if len(shape) == 2:
            return a.rearrange("p (a b) -> p a b", a=shape[0])
        if len(shape) == 3:
            return a.rearrange("p (a b c) -> p a b c", a=shape[0], b=shape[1])
        return a


class HiLo:

    def __init__(self, nc, ctx):
        self.h = ctx.enter_context(nc.sbuf_tensor("act_high", [P, HL], F32R))
        self.l = ctx.enter_context(nc.sbuf_tensor("act_low", [P, HL], F32R))

    def at(self, start, tiles, width):
        n = tiles * width
        assert start + n <= HL
        return tuple(t[:, start:start + n].rearrange("p (a b) -> p a b", a=tiles) for t in (self.h, self.l))


def program(nc, I, out):
    ctx = ExitStack()
    with ctx:
        q = Queues(nc, ctx)
        banks = Banks(nc, ctx)
        ring = Ring(q, nc, ctx)
        ar = Arena(nc, ctx, ARENA)
        hi_lo = HiLo(nc, ctx)

        def PE(emit, *after):
            return q.put("tensor", emit, *after)

        def V(emit, *after, **k):
            return q.put("vector", emit, *after, **k)

        def S(emit, *after, **k):
            return q.put("scalar", emit, *after, **k)

        def G(emit, *after, **k):
            return q.put("gpsimd", emit, *after, **k)

        def mm(out_, lhsT, rhs, *after, start=True, stop=True):
            return PE(lambda e: e.matmul(out_, lhsT, rhs, start=start, stop=stop), *after)

        def copy(engine, dst, src, *after, **k):
            if engine == "scalar":
                return S(lambda e: e.activation(dst, src, ACT.Copy), *after, **k)
            return q.put(engine, lambda e: e.tensor_copy(dst, src), *after, **k)

        def tt(engine, dst, a, b, op, *after, **k):
            return q.put(engine, lambda e: e.tensor_tensor(dst, a, b, op), *after, **k)

        def ts(engine, dst, a, s1, s2, op0, op1, *after, **k):
            return q.put(engine, lambda e: e.tensor_scalar(dst, a, s1, s2, op0, op1) if s2 is not None
                         else e.tensor_scalar(dst, a, s1, None, op0), *after, **k)

        def stt(dst, a, s, b, op0, op1, *after, **k):
            return V(lambda e: e.scalar_tensor_tensor(out=dst, in0=a, scalar=s, in1=b, op0=op0, op1=op1),
                     *after, **k)

        def act(dst, src, func, *after, bias=None, scale=1.0, accum=None, **k):
            kw = {"scale": scale}
            if bias is not None:
                kw["bias"] = bias
            if accum is not None:
                kw["accum_out"] = accum
            return S(lambda e: e.activation(dst, src, func, **kw), *after, **k)

        def memset(engine, dst, value, *after):
            return q.put(engine, lambda e: e.memset(dst, value), *after)

        def turned(out_, in_, ident_, *after):
            return PE(lambda e: e.transpose(out_, in_, ident_), *after)

        def recip(dst, src, *after, **k):
            return V(lambda e: e.reciprocal(dst, src), *after, **k)

        def reduce_(dst, src, op, *after, negate=False, **k):
            return V(lambda e: e.tensor_reduce(dst, src, AX_X, op, negate=True) if negate
                     else e.tensor_reduce(dst, src, AX_X, op), *after, **k)

        def small(name, dst, src, *after):
            return q.load(name, dst, src, *after, engine="gpsimd")

        ident = ar.take(P)
        in_ident = q.load("ident", ident, I["square_masks"][:, 0:P])
        c_rows = ar.take(P, rows=KT)
        in_c = q.load("c", c_rows, I["c"].rearrange("a (k p) -> (a k) p", p=P))
        ones = ar.take(P)
        m_ones = memset("vector", ones, 1.0)
        eps6 = ar.take(1)
        m_eps = memset("vector", eps6, 1e-6)
        hot = ar.take(3 * P, rows=NUM_BUCKETS + 1)
        in_hot = small("hot", hot, I["bucket_rows"][:, :])
        tab = ar.take(16, rows=NUM_BUCKETS + 1)
        in_tab = small("tab", tab[0:NUM_BUCKETS, :], I["rel_bias"][:, :])
        m_tab = memset("vector", tab[NUM_BUCKETS:NUM_BUCKETS + 1, :], NEG)

        rows_t = [ar.take(P, rows=P) for _ in range(3)]
        n_rows, in_rows, col_at = [0, 0, 0], [[], [], []], {}

        def as_rows(which, name, src, n):
            r0 = n_rows[which]
            in_rows[which].append(small(name, rows_t[which][r0:r0 + n, :], src))
            col_at[name] = (which, r0)
            n_rows[which] += n

        as_rows(0, "ada_b", I["ada_b"].rearrange("l (k p) -> (l k) p", p=P), 96)
        as_rows(1, "ln_g", I["ln_g"].rearrange("l s (k p) -> (l s k) p", p=P), 4 * KT)
        as_rows(1, "ln_b", I["ln_b"].rearrange("l s (k p) -> (l s k) p", p=P), 4 * KT)
        as_rows(1, "mix_pre", I["norm_mix_pre_2"].rearrange("a (k p) -> (a k) p", p=P), KT)
        as_rows(1, "mlp_pre", I["norm_mlp_pre_2"].rearrange("a (k p) -> (a k) p", p=P), KT)
        as_rows(1, "subln", I["diff_subln"], 1)
        as_rows(1, "dn_norm", I["dn_out_norm_2"], 1)
        as_rows(2, "pe_k", I["nsa_pe_k"].rearrange("a (l j) d -> (a l) (j d)", j=2), 16)
        as_rows(2, "pe_v", I["nsa_pe_v"].rearrange("a (l j) d -> (a l) (j d)", j=2), 16)
        as_rows(2, "conv", I["conv_w_2"].rearrange("a w (k p) -> (a w k) p", p=P), 60)
        cols = ar.take(3, 96)

        def transpose_rows(which):
            n = n_rows[which]
            b = banks.take()
            t = turned(b.t[:, 0:n], rows_t[which][0:n, :], ident[0:n, 0:n], in_ident, *in_rows[which], *b.after)
            c = copy("scalar", cols[:, which, 0:n], b.t[:, 0:n], t)
            banks.give(b, c)
            return c

        def col(name, i=0, n=1):
            which, r0 = col_at[name]
            return cols[:, which, r0 + i:r0 + i + n]

        c_act, c_exp = ar.take(KT), ar.take(KT)
        b = banks.take()
        t = turned(b.t[:, 0:KT], c_rows, ident[0:KT, 0:KT], in_ident, in_c)
        v1 = copy("vector", c_act, b.t[:, 0:KT], t)
        banks.give(b, v1)
        v1 = ts("vector", c_exp, c_act, -EXP_MAX, None, ALU.max, None)
        s1 = act(c_exp, c_exp, ACT.Exp, v1, scale=-1.0)
        ts("vector", c_exp, c_exp, 1.0, None, ALU.add, None, s1)
        recip(c_exp, c_exp)
        t_cact = tt("vector", c_act, c_act, c_exp, ALU.mult)

        x_tok = ar.take(QT, D)
        in_x = [q.load(f"x{t}", x_tok[:, t, :], I["x"][0, t * P:(t + 1) * P, :], engine="gpsimd") for t in range(QT)]
        hH, hL = hi_lo.at(0, KT, SEQ)
        oH, oL = hi_lo.at(KT * L2, KT, SEQ)
        after_cols = ar.at
        spare_at = ar.at
        n_tok = ar.take(QT, D)
        y_tmp = ar.take(QT, D)
        hT = ar.take(KT, SEQ)
        bias = ar.take(16, SEQ)
        ln_at = ar.at
        ln_rows = ar.take(2, D)
        gate_rows = ar.take(2, D)
        ada_cols = ar.take(4, KT)
        mod_cols = ar.take(2, KT)
        ada_acc = ar.take(2, 512)
        stats = ar.take(QT, 24)
        relu_at = ar.at
        relu_tmp = ar.take(2, 512)
        phase_base = ar.at

        acc_reader = [(), ()]
        ada_n = [0]
        gate_sem = [ctx.enter_context(nc.semaphore(f"gate_b_in{i}")) for i in range(2)]
        gate_uses = [0, 0]
        gate_reader = [(), ()]
        col_reader = [None] * 4
        t_gate = [None, None]
        t_adac = [None] * 4
        pending = []

        def ada_start(layer, j):
            s = ada_n[0] % 2
            ada_n[0] += 1
            acc = ada_acc[:, s, :]
            w_l = I["ada_w"][layer].rearrange("(k p) n -> p k n", p=P)
            for kc in range(2):
                w, landed, slot = ring.load(w_l[:, 4 * kc:4 * kc + 4, j * 512:(j + 1) * 512])
                for k in range(4):
                    c_ = c_act[:, 4 * kc + k:4 * kc + k + 1]
                    if kc == k == 0:
                        v = ts("vector", acc, w[:, k, :], c_, None, ALU.mult, None, landed, t_cact, *acc_reader[s])
                    else:
                        v = stt(acc, w[:, k, :], c_, acc, ALU.mult, ALU.add, landed)
                ring.done(slot, v)
            part, half = j // 2, j % 2
            b_in = None
            if part in (2, 5):
                g = part // 3
                gate_uses[g] += 1
                dst = gate_rows[:, g, half * 512:(half + 1) * 512]
                src = I["ada_b"][layer, j * 512:(j + 1) * 512].partition_broadcast(P)
                if half == 0:
                    dst, src = gate_rows[:, g, :], I["ada_b"][layer, j * 512:(j + 2) * 512].partition_broadcast(P)
                    gate_in[g] = q.dma(lambda e: e.dma_start(dst, src), gate_sem[g], 16 * ((gate_uses[g] + 1) // 2),
                                       *gate_reader[g])
                b_in = gate_in[g]
            pending.append((layer, j, s, v, b_in))

        gate_in = [None, None]

        def ada_finish():
            layer, j, s, v, b_in = pending.pop(0)
            part, half = j // 2, j % 2
            acc = ada_acc[:, s, :]
            b = banks.take()
            if part in (2, 5):
                g = part // 3
                m = mm(b.t[:, :], ones, acc, v, m_ones, *b.after)
                rows = gate_rows[:, g, half * 512:(half + 1) * 512]
                c = t_gate[g] = stt(rows, b.t[:, :], 1.0, rows, ALU.add, ALU.add, m, b_in)
            else:
                for i in range(4):
                    m = turned(b.t[:, i * P:(i + 1) * P], acc[:, i * P:(i + 1) * P], ident, v, in_ident, *b.after)
                which = {0: 0, 1: 1, 3: 2, 4: 3}[part]
                dst = ada_cols[:, which, half * 4:half * 4 + 4]
                c = reduce_(dst, b.t[:, :].rearrange("p (a b) -> p a b", a=4), ALU.add, m, col_reader[which])
                t_adac[which] = tt("vector", dst, dst, col("ada_b", layer * 48 + j * 4, 4), ALU.add, t_cols)
            banks.give(b, c)
            acc_reader[s] = (m,)

        def feature_product(w, c0, m, src, toks, out_, *after):
            n = w.shape[1]
            for k in range(n):
                last = mm(out_, w[:, k, c0:c0 + m], src[:, k, toks], *(after if k == 0 else ()),
                          start=k == 0, stop=k == n - 1)
            return last

        def token_product(w, c0, n_cols, src, toks, out_, *after):
            n = w.shape[1]
            for k in range(n):
                last = mm(out_, src[:, k, toks], w[:, k, c0:c0 + n_cols], *(after if k == 0 else ()),
                          start=k == 0, stop=k == n - 1)
            return last

        def split_mm(out_, a, b_, *after, start, stop):
            (ah, al), (bh, bl) = a, b_
            mm(out_, ah, bh, *after, start=start, stop=False)
            mm(out_, ah, bl, start=False, stop=False)
            return mm(out_, al, bh, start=False, stop=stop)

        def feature_product3(w, c0, src, toks, out_, *after):
            for k in range(KT):
                last = split_mm(out_, (w[0][:, k, c0:c0 + P], w[1][:, k, c0:c0 + P]),
                                (src[0][:, k, toks], src[1][:, k, toks]), *(after if k == 0 else ()),
                                start=k == 0, stop=k == KT - 1)
            return last

        def token_product3(w, n_cols, src, toks, out_, *after):
            for k in range(KT):
                last = split_mm(out_, (src[0][:, k, toks], src[1][:, k, toks]),
                                (w[0][:, k, 0:n_cols], w[1][:, k, 0:n_cols]), *(after if k == 0 else ()),
                                start=k == 0, stop=k == KT - 1)
            return last

        def split_into(high, low, src, *after, scale=None):
            h = act(high, src, ACT.Copy, *after, **({} if scale is None else {"scale": scale}))
            if scale is None:
                return tt("vector", low, src, high.bitcast(F32), ALU.subtract, h)
            return stt(low, src, scale, high.bitcast(F32), ALU.mult, ALU.subtract, h)

        def rsqrt_col(dst, var, tmp, eps, *after):
            a = ts("vector", tmp, var, eps, None, ALU.add, None, *after)
            s = act(dst, tmp, ACT.Ln, a)
            s = act(dst, dst, ACT.Exp, scale=-0.5)
            tt("vector", var, dst, dst, ALU.mult, s)
            tt("vector", var, var, tmp, ALU.mult)
            ts("vector", var, var, -0.5, 1.5, ALU.mult, ALU.add)
            return tt("vector", dst, dst, var, ALU.mult)

        def to_features(src_tok, t_src, dst, halves, scale_cols, shift_cols, t_coef, t_free, at, toks=P):
            done = []
            for k0 in range(0, KT, 4):
                b = banks.take()
                for k in range(k0, k0 + 4):
                    m = turned(b.t[:, (k - k0) * P:(k - k0) * P + toks], src_tok[:, k * P:(k + 1) * P],
                               ident[0:toks, 0:toks], t_src, in_ident, *b.after)
                for k in range(k0, k0 + 4):
                    o, i_ = dst[:, k, at:at + toks], b.t[:, (k - k0) * P:(k - k0) * P + toks]
                    free = (t_coef, *t_free)
                    if k0 == 0:
                        kw = {"bias": shift_cols[:, k:k + 1]} if shift_cols is not None else {}
                        c = act(o, i_, ACT.Identity if kw else ACT.Copy, m, *free, scale=scale_cols[:, k:k + 1],
                                loose=k > k0, **kw)
                    elif shift_cols is None:
                        c = ts("vector", o, i_, scale_cols[:, k:k + 1], None, ALU.mult, None, m, *free, loose=k > k0)
                    else:
                        c = ts("vector", o, i_, scale_cols[:, k:k + 1], shift_cols[:, k:k + 1], ALU.mult, ALU.add,
                               m, *free, loose=k > k0)
                banks.give(b, c)
                grp = (slice(None), slice(k0, k0 + 4), slice(at, at + toks))
                done.append(split_into(halves[0][grp], halves[1][grp], dst[grp], c))
            return done

        def k_chunks(w, order=None):
            r = w.rearrange("(c k p) n -> c p k n", k=KW, p=P)
            return [r[i] for i in (range(r.shape[0]) if order is None else order)]

        def mlp_chunks(w1, w2):
            up, down = w1.rearrange("(k p) n -> p k n", p=P), k_chunks(w2)
            order = []
            for step in range(len(down) + MLP_LAG):
                if step < len(down):
                    order.append(up[:, :, step * CW:(step + 1) * CW])
                if step >= MLP_LAG:
                    order.append(down[step - MLP_LAG])
            return order

        w_ev = I["ev_w_in"][0].rearrange("(k p) n -> p k n", p=P)
        w_od = I["od_w_in"][0].rearrange("(k p) n -> p k n", p=P)
        w_in = I["w_in_2"][0].rearrange("(k p) n -> p k n", p=P)
        cols_of = lambda w, *starts: [w[:, :, c0:c0 + CW] for c0 in starts]
        weights = SplitWeights(q, ring, nc, ctx, [
            *cols_of(w_ev, 1944, 1944 + CW, 512), w_ev[:, :, 1024:1152], *cols_of(w_ev, 0, CW, 1304, 1304 + CW),
            *k_chunks(I["ev_w_out"][0]), *mlp_chunks(I["mlp_w1"][0], I["mlp_w2"][0]),
            *[c_ for i in range(4) for c_ in cols_of(w_od, i * CW, D + i * CW, 2 * D + i * CW)],
            *k_chunks(I["od_w_out"][0]), *mlp_chunks(I["mlp_w1"][1], I["mlp_w2"][1]),
            *cols_of(w_in, 512, 512 + CW, 0, CW, 1024, 1024 + CW, 2064, 2064 + CW, 1536, 1536 + CW),
            *k_chunks(I["w_out_2"][0], (2, 3, 0, 1)), *mlp_chunks(I["w_up_2"][0], I["w_down_2"][0])])

        ada_start(0, 0)
        t_cols = transpose_rows(0)
        for j in range(1, 4):
            ada_start(0, j)
            ada_finish()
        ada_finish()
        t_cols_ln = transpose_rows(1)
        t_cols_b = transpose_rows(2)

        def modulation(sub, ln=None):
            sh, sc = ada_cols[:, 2 * sub, :], ada_cols[:, 2 * sub + 1, :]
            after = (t_adac[2 * sub], t_adac[2 * sub + 1])
            a = ts("vector", mod_cols[:, 0, :], sc, 1.0, None, ALU.add, None, *after)
            if ln is None:
                a = copy("vector", mod_cols[:, 1, :], sh)
            else:
                tt("vector", mod_cols[:, 1, :], mod_cols[:, 0, :], col("ln_b", ln * KT, KT), ALU.mult, t_cols_ln)
                tt("vector", mod_cols[:, 1, :], mod_cols[:, 1, :], sh, ALU.add)
                a = tt("vector", mod_cols[:, 0, :], mod_cols[:, 0, :], col("ln_g", ln * KT, KT), ALU.mult)
            col_reader[2 * sub] = col_reader[2 * sub + 1] = a
            return a

        t_mod = modulation(0)
        t_h = []
        for t in range(QT):
            t_h += to_features(x_tok[:, t, :], in_x[t], hT, (hH, hL), mod_cols[:, 0, :], mod_cols[:, 1, :], t_mod, (), t * P)

        bias_row = y_tmp[0:16, 0, 0:3 * P]
        b = banks.take()
        m = mm(b.t[0:16, 0:3 * P], tab, hot, in_hot, in_tab, m_tab, *b.after)
        c = copy("scalar", bias_row, b.t[0:16, 0:3 * P], m)
        banks.give(b, c)
        rows_dram = nc.dram_tensor("bias_rows", (16, P, 3 * P), F32, kind="Internal").ap()
        rows_out = q.load("bias_rows", rows_dram, bias_row.unsqueeze(1).broadcast_to([16, P, 3 * P]), c, engine="gpsimd")
        shifted = bass.AP(tensor=rows_dram.tensor, offset=P - 1, ap=[[3 * P - 1, P], [P * 3 * P, 16], [1, SEQ]])
        t_bias = q.load("bias", bias, shifted, rows_out, engine="gpsimd")

        all_toks = slice(0, SEQ)
        tok_tile = lambda t: slice(t * P, (t + 1) * P)
        HALF = 64
        spare = ar.over(spare_at, 2 * QT * D)
        over_ln = ar.over(ln_at, 2 * D)
        over_relu = ar.over(relu_at, 2 * 512)
        qT = ar.take(4, SEQ)
        dqT = ar.take(4, SEQ)
        iq_raw_at = ar.at
        iqT = ar.take(4, SEQ)
        raw = ar.take(4, SEQ)
        qlatT = ar.over(iq_raw_at, 8 * SEQ).take(8, SEQ)
        k_sel = ar.take(2, SEQ)
        k_win = ar.take(2, SEQ)
        ikT = ar.take(SEQ)
        v_sw = ar.take(QT, SEQ)
        gates = ar.take(QT, 24)
        ckv = ar.take(QT, P)
        ckvT = ar.take(SEQ)
        iw = ar.take(QT, 8)
        x_split = (hH, hL)

        UC = 3 * P
        NB = 4
        zb = spare.take(NB, UC)
        pT = spare.take(NB, UC)
        ukT = spare.take(4, P)
        sq = spare.take(QT, P)
        over_z = ar.over(spare_at, 2 * NB * UC)
        blk = over_z.take(2, 16, 30)
        hid = over_z.take(2, SEQ, rows=30)
        isc = over_ln.take(UC)
        taken = over_ln.take(UC)
        relu = over_ln.take(2, UC)
        olat = over_ln.take(2, SEQ)

        def feature_tiles(dst_of):
            w, ready, slot = weights.take()
            for i in range(w[0].shape[2] // P):
                b = banks.take()
                m = feature_product3(w, i * P, x_split, all_toks, b.t[:, 0:SEQ], ready, *t_h, *b.after)
                banks.give(b, dst_of(i, b, m))
            weights.done(slot, m)
            weights.ahead()
            return m

        def pair_copy(dst, i0):
            def put(i, b, m):
                return copy("scalar", dst[:, i0 + i, :], b.t[:, 0:SEQ], m)
            return put

        kvn_row = ar.take(P)
        in_kvn = small("kvn", kvn_row, I["dsa_kv_norm"][0].partition_broadcast(P))
        w, landed, slot = ring.load(w_ev[:, :, 1816:1944])
        for _ in range(SPLIT_SLOTS):
            weights.ahead()
        b = banks.take()
        for t in range(QT):
            m = token_product(w, 0, P, hT, tok_tile(t), b.t[:, t * P:(t + 1) * P], landed, *t_h, *b.after)
        ring.done(slot, m)
        for t in range(QT):
            s0 = act(sq[:, t, :], b.t[:, t * P:(t + 1) * P], ACT.Square, m, accum=stats[:, 0, t:t + 1])
        ts("vector", stats[:, 0, 2:4], stats[:, 0, 0:2], 1.0 / P, None, ALU.mult, None, s0)
        rsqrt_col(stats[:, 0, 4:6], stats[:, 0, 2:4], stats[:, 0, 6:8], 1e-5)
        for t in range(QT):
            t_ckv = stt(ckv[:, t, :], b.t[:, t * P:(t + 1) * P], stats[:, 0, 4 + t:5 + t], kvn_row, ALU.mult, ALU.mult,
                        in_kvn)
        banks.give(b, t_ckv)
        for half in range(2):
            feature_tiles(pair_copy(iqT, 2 * half))
        t_iq = ("scalar", q.sem["scalar"], q.count["scalar"])
        w, landed, slot = ring.load(w_ev[:, :, 2456:2528])
        b = banks.take()
        m = feature_product(w, 0, HALF, hT, all_toks, b.t[0:HALF, 0:SEQ], landed, *b.after)
        copy("scalar", ikT[0:HALF, :], b.t[0:HALF, 0:SEQ], m)
        t_ik = copy("scalar", ikT[HALF:P, :], b.t[0:HALF, 0:SEQ], m)
        banks.give(b, t_ik)
        b = banks.take()
        for t in range(QT):
            m = token_product(w, HALF, 8, hT, tok_tile(t), b.t[:, t * 8:(t + 1) * 8], *b.after)
        t_iw = act(iw, b.t[:, 0:16].rearrange("p (t n) -> p t n", t=QT), ACT.Copy, m, scale=8 ** -0.5 * 64 ** -0.5)
        banks.give(b, t_iw)
        ring.done(slot, m)
        b = banks.take()
        for t in range(QT):
            m2 = turned(b.t[:, t * P:(t + 1) * P], ckv[:, t, :], ident, t_ckv, *b.after)
        t_ckvT = copy("scalar", ckvT, b.t[:, 0:SEQ], m2)
        banks.give(b, t_ckvT)

        top8 = ar.take(QT, 8)
        r_reader = [(), ()]

        def indexer_head(j):
            lo = j % 2 * HALF
            b = banks.take()
            mm(b.t[:, 0:P], iqT[lo:lo + HALF, j // 2, 0:P], ikT[lo:lo + HALF, 0:P], t_iq, t_ik, *b.after)
            m = mm(b.t[:, P:UC], iqT[lo:lo + HALF, j // 2, P:SEQ], ikT[lo:lo + HALF, :])
            r = relu[:, j % 2, :]
            s1 = act(r, b.t[:, 0:UC], ACT.Relu, m, *r_reader[j % 2], loose=True)
            banks.give(b, s1)
            for t, c in ((0, slice(0, P)), (1, slice(P, UC))):
                if j == 0:
                    v1 = ts("vector", isc[:, c], r[:, c], iw[:, t, 0:1], None, ALU.mult, None, s1, t_iw)
                else:
                    v1 = stt(isc[:, c], r[:, c], iw[:, t, j:j + 1], isc[:, c], ALU.mult, ALU.add, s1)
            r_reader[j % 2] = (v1,)
            return v1, m

        def raw_copy(i, b, m):
            for g in range(2):
                s_ = b.t[g * HALF:(g + 1) * HALF, :]
                copy("scalar", raw[0:HALF, 2 * i + g, :], s_[:, 0:SEQ], m)
                last = copy("scalar", raw[HALF:P, 2 * i + g, 0:SEQ - 1], s_[:, 1:SEQ], m)
            return last
        feature_tiles(raw_copy)
        t_raw = ("scalar", q.sem["scalar"], q.count["scalar"])
        for kv in range(2):
            pe = col("pe_v" if kv else "pe_k", 0, 16)
            for g in range(2):
                even = raw[:, 2 * kv + g, :].rearrange("p (n l j) -> p l n j", l=8, j=2)[:, :, :, 0]
                for hi in range(2):
                    t_blk = tt("vector", blk[:, kv, 8 * hi:8 * hi + 8, g * NCMP:(g + 1) * NCMP], even[:, :, hi:hi + NCMP],
                               pe[:, 8 * hi:8 * hi + 8].unsqueeze(2).broadcast_to([P, 8, NCMP]), ALU.add, t_raw, t_cols_b,
                               t_bias)
        for j in range(8):
            v1, t_index_mm = indexer_head(j)
        for c in (slice(0, P), slice(2 * P, UC)):
            t_isc = G(lambda e, c=c: e.affine_select(out=isc[:, c], in_=isc[:, c], compare_op=ALU.is_ge, fill=NEG,
                                                     base=0, pattern=[[-1, P]], channel_multiplier=1), v1)

        gel = ar.take(2, 2, 30)
        kcT = ar.take(2, NCMP)
        v_cmp = ar.take(2, HALF)
        t_hid = []
        for kv in range(2):
            b = banks.take()
            w1 = I["nsa_w1_v" if kv else "nsa_w1_k"][0].rearrange("(l p) n -> p l n", p=P)
            for lc in range(2):
                w, landed, slot = ring.load(w1[:, 8 * lc:8 * lc + 8, :])
                for l in range(8):
                    m = mm(b.t[0:30, 0:SEQ], blk[:, kv, 8 * lc + l, :], w[:, l, :], landed, t_blk, *b.after,
                           start=lc == l == 0, stop=lc == 1 and l == 7)
                ring.done(slot, m)
            h_ = hid[0:30, 0, :]
            g_ = hid[0:30, 1, :]
            s1 = copy("scalar", h_, b.t[0:30, 0:SEQ], m, *t_hid)
            banks.give(b, s1)
            tt("gpsimd", g_, h_, h_, ALU.mult, s1)
            ts("gpsimd", g_, g_, 0.044715, 1.0, ALU.mult, ALU.add)
            tt("gpsimd", g_, g_, h_, ALU.mult)
            g1 = ts("gpsimd", g_, g_, -EXP_MAX / 2, None, ALU.max, None)
            s1 = act(g_, g_, ACT.Exp, g1, scale=-2.0 * math.sqrt(2.0 / math.pi))
            ts("vector", g_, g_, 1.0, None, ALU.add, None, s1)
            recip(g_, g_)
            v1 = tt("vector", g_, g_, h_, ALU.mult)
            b = banks.take()
            for i in range(2):
                m = turned(b.t[:, i * 32:i * 32 + 30], g_[:, i * P:(i + 1) * P], ident[0:30, 0:30], v1, *b.after)
            t_gel = copy("scalar", gel[:, kv, :, :], b.t[:, 0:64].rearrange("p (a b) -> p a b", a=2)[:, :, 0:30], m)
            t_hid = [m]
            banks.give(b, t_gel)
            if kv == 0:
                def kw_copy(i, b, m):
                    for g in range(2):
                        for half in range(2):
                            last = copy("scalar", k_win[half * HALF:(half + 1) * HALF, g, :], b.t[g * HALF:(g + 1) * HALF, 0:SEQ], m)
                    return last
                feature_tiles(kw_copy)
                t_kw = ("scalar", q.sem["scalar"], q.count["scalar"])

        w, landed, slot = ring.load(w_ev[:, :, 768:1024])
        b = banks.take()
        m = feature_product(w, 0, P, hT, all_toks, b.t[:, 0:SEQ], landed, *b.after)
        for g in range(2):
            for half in range(2):
                t_ks = copy("scalar", k_sel[half * HALF:(half + 1) * HALF, g, :], b.t[g * HALF:(g + 1) * HALF, 0:SEQ], m)
        banks.give(b, t_ks)
        b = banks.take()
        for t in range(QT):
            m = token_product(w, P, P, hT, tok_tile(t), b.t[:, t * P:(t + 1) * P], *b.after)
        t_vs = copy("scalar", v_sw[:, :, 0:P], b.t[:, 0:SEQ].rearrange("p (t n) -> p t n", t=QT), m)
        banks.give(b, t_vs)
        ring.done(slot, m)
        w, landed, slot = ring.load(w_ev[:, :, 1152:1304])
        b = banks.take()
        for t in range(QT):
            m = token_product(w, 0, P + 24, hT, tok_tile(t), b.t[:, t * 160:t * 160 + P + 24], landed, *b.after)
        ring.done(slot, m)
        vg = b.t[:, 0:320].rearrange("p (t n) -> p t n", t=QT)
        t_vw = copy("scalar", v_sw[:, :, P:2 * P], vg[:, :, 0:P], m)
        s1 = copy("scalar", gates, vg[:, :, P:P + 24])
        banks.give(b, s1)
        g1 = ts("gpsimd", gates, gates, -EXP_MAX, None, ALU.max, None, s1)
        s1 = act(gates, gates, ACT.Exp, g1, scale=-1.0)
        ts("vector", gates, gates, 1.0, None, ALU.add, None, s1)
        t_gates = recip(gates, gates)
        for half in range(2):
            feature_tiles(pair_copy(qT, 2 * half))
        t_q = ("scalar", q.sem["scalar"], q.count["scalar"])
        w, landed, slot = ring.load(I["nsa_w2_k"][0].rearrange("(l p) n -> p l n", p=P))
        b = banks.take()
        for i in range(2):
            m = mm(b.t[0:HALF, 0:30], w[:, i, :], gel[:, 0, i, :], landed, t_gel, *b.after, start=i == 0, stop=i == 1)
        ring.done(slot, m)
        for half in range(2):
            t_kc = copy("scalar", kcT[half * HALF:(half + 1) * HALF, :, :], b.t[0:HALF, 0:30].rearrange("p (g n) -> p g n", g=2), m)
        banks.give(b, t_kc)
        w, landed, slot = ring.load(I["nsa_w2_v"][0].rearrange("(l p) n -> p l n", p=P))
        b = banks.take()
        for g in range(2):
            for i in range(2):
                m = mm(b.t[0:NCMP, g * HALF:(g + 1) * HALF], gel[:, 1, i, g * NCMP:(g + 1) * NCMP], w[:, i, :],
                       landed, *b.after, start=i == 0, stop=i == 1)
        ring.done(slot, m)
        for base in range(0, P, 32):
            t_vc = copy("scalar", v_cmp[base:base + NCMP, :, :], b.t[0:NCMP, 0:2 * HALF].rearrange("p (g n) -> p g n", g=2), m)
        banks.give(b, t_vc)

        copy("vector", taken, isc, t_isc)
        for r in range(TOPK // 8):
            for t, c in ((0, slice(0, P)), (1, slice(P, UC))):
                V(lambda e, t=t, c=c: e.max(top8[:, t, :], taken[:, c]))
                V(lambda e, t=t, c=c: e.match_replace(taken[:, c], top8[:, t, :], taken[:, c], REPLACED))
        ts("vector", taken, taken, -1e38, 1.0, ALU.is_le, ALU.subtract)
        t_sel = ts("vector", taken, taken, -NEG, None, ALU.mult, None)

        over_sq = ar.over(spare_at + 2 * NB * UC + 4 * P, SEQ)
        pc = ar.take(QT * 8, 32)
        bc = over_sq.take(QT * 8, NCMP)
        pcT = ar.take(2, SEQ)
        m1 = memset("gpsimd", pc, 0.0)
        m2 = memset("gpsimd", bc, NEG, t_ckv)
        first = (2 * P - 1 - (P + CMP_LEN - 1)) // CMP_STRIDE + 1
        copy("gpsimd", bc[:, 0:8, 0:first], bias[:, 0:8, P + CMP_LEN - 1::CMP_STRIDE], m2, t_bias)
        t_bc = copy("gpsimd", bc[:, 8:16, :], bias[:, 0:8, CMP_LEN - 1::CMP_STRIDE][:, :, 0:NCMP])
        z = pc[:, :, 0:NCMP]
        for par in range(2):
            b = banks.take()
            lo = par * HALF
            for t in range(QT):
                for h2 in range(4):
                    o = (t * 4 + h2) * 32
                    m = mm(b.t[:, o:o + NCMP], qT[lo:lo + HALF, h2, t * P:(t + 1) * P],
                           kcT[lo:lo + HALF, h2 // 2, :], t_q, t_kc, *b.after)
            v1 = stt(pc[:, par::2, 0:NCMP], b.t[:, 0:SEQ].rearrange("p (a n) -> p a n", n=32)[:, :, 0:NCMP],
                     SCALE, bc[:, par::2, :], ALU.mult, ALU.add, m, m1, t_bc)
            banks.give(b, v1)
        cst = over_relu.take(4, QT * 8)

        w, landed, slot = ring.load(I["dsa_w_uk"][0].rearrange("r h d -> r (h d)"))
        b = banks.take()
        for i in range(4):
            m = turned(b.t[:, i * P:(i + 1) * P], w[:, i * P:(i + 1) * P], ident, landed, *b.after)
        t_uk = copy("scalar", ukT.rearrange("p a b -> p (a b)"), b.t[:, :], m)
        banks.give(b, t_uk)
        ring.done(slot, m)
        reduce_(cst[:, 0, :], z, ALU.max)
        ts("vector", cst[:, 0, :], cst[:, 0, :], CLAMP, None, ALU.max, None)
        v1 = tt("vector", z, z, cst[:, 0, :].unsqueeze(2).broadcast_to([P, QT * 8, NCMP]), ALU.subtract)
        s1 = act(z, z, ACT.Exp, v1)
        reduce_(cst[:, 1, :], z, ALU.add, s1)
        ts("vector", cst[:, 1, :], cst[:, 1, :], 1e-30, None, ALU.max, None)
        recip(cst[:, 2, :], cst[:, 1, :])
        tt("vector", cst[:, 3, :].rearrange("p (t h) -> p t h", t=QT), cst[:, 2, :].rearrange("p (t h) -> p t h", t=QT),
           gates[:, :, 0::3], ALU.mult)
        t_pc = tt("vector", z, z, cst[:, 3, :].unsqueeze(2).broadcast_to([P, QT * 8, NCMP]), ALU.mult)

        ust = over_relu.take(NB, 8)
        z_reader = [(t_hid[0],)] * NB
        pT_reader = [(t_hid[0],)] * NB
        unit_n = [0]

        def unit_logits(u, lhs_of, rhs_of, scale, bias_of, after, coef):
            s = u["s"] = unit_n[0] % NB
            unit_n[0] += 1
            b = banks.take()
            mm(b.t[:, 0:P], lhs_of(0), rhs_of(slice(0, P)), *after, *b.after)
            m = mm(b.t[:, P:UC], lhs_of(1), rhs_of(slice(0, SEQ)))
            z, st = zb[:, s, :], ust[:, s, :]
            bias_ap, t_b = bias_of()
            stt(z[:, 0:P], b.t[:, 0:P], scale, bias_ap[0], ALU.mult, ALU.add, m, t_b, *z_reader[s])
            v = stt(z[:, P:UC], b.t[:, P:UC], scale, bias_ap[1], ALU.mult, ALU.add, loose=True)
            banks.give(b, v)
            reduce_(st[:, 0:1], z[:, 0:P], ALU.max, negate=True)
            v = reduce_(st[:, 1:2], z[:, P:UC], ALU.max, negate=True, loose=True)
            act(z[:, 0:P], z[:, 0:P], ACT.Exp, v, bias=st[:, 0:1], accum=st[:, 2:3], loose=True)
            a = act(z[:, P:UC], z[:, P:UC], ACT.Exp, bias=st[:, 1:2], accum=st[:, 3:4], loose=True)
            v = recip(st[:, 4:6], st[:, 2:4], a)
            if coef is not None:
                v = coef(st, v)
            u["z"], u["st"], u["v"] = z, st, v

        def unit_scale(u):
            z, st = u["z"], u["st"]
            ts("gpsimd", z[:, 0:P], z[:, 0:P], st[:, 4:5], None, ALU.mult, None, u["v"], loose=True)
            u["p"] = ts("gpsimd", z[:, P:UC], z[:, P:UC], st[:, 5:6], None, ALU.mult, None, loose=True)

        def unit_transpose(u):
            s, z = u["s"], u["z"]
            b = banks.take()
            turned(b.t[:, 0:P], z[:, 0:P], ident, u["p"], *b.after)
            turned(b.t[:, P:2 * P], z[:, P:2 * P], ident)
            m = turned(b.t[:, 2 * P:UC], z[:, 2 * P:UC], ident)
            z_reader[s] = (m,)
            c = copy("scalar", pT[:, s, :], b.t[:, 0:UC], m, *pT_reader[s], loose=True)
            banks.give(b, c)
            u["pT"] = c

        def run_units(units, lags, fill=()):
            fill = iter(fill)
            for step in range(len(units) + lags[-1]):
                for stage, lag in reversed(list(enumerate(lags))):
                    if 0 <= step - lag < len(units):
                        units[step - lag][stage]()
                next(fill, None)
            for _ in fill:
                pass

        bias_pair = lambda h: ((bias[:, h, P:SEQ], bias[:, h, :]), t_bias)
        head_bank = {}
        t_oT = [None] * KT

        def head_out(b, i, m):
            t_oT[i] = split_into(oH[:, i, :], oL[:, i, :], b.t[:, 0:SEQ], m)
            banks.give(b, t_oT[i])

        def latent_queries():
            for half in range(2):
                feature_tiles(pair_copy(dqT, 2 * half))
                yield
            t_dq = ("scalar", q.sem["scalar"], q.count["scalar"])
            for h in range(8):
                b = banks.take()
                lo = h % 2 * HALF
                m = mm(b.t[:, 0:SEQ], ukT[lo:lo + HALF, h // 2, :], dqT[lo:lo + HALF, h // 2, :], t_uk, t_dq, *b.after)
                t_ql[h] = copy("scalar", qlatT[:, h, :], b.t[:, 0:SEQ], m, t_index_mm, t_blk)
                banks.give(b, t_ql[h])
                yield
            for j in range(4, 12):
                ada_start(0, j)
                yield
                if j > 4:
                    ada_finish()
            ada_finish()

        t_ql = [None] * 8

        def nsa_unit(h, branch):
            u = {}
            lo, g = h % 2 * HALF, h // 4
            kk, col0, ready = ((k_sel, 0, t_ks), (k_win, P, t_kw))[branch]

            def coef(st, v):
                for t in range(QT):
                    v = tt("vector", st[:, 4 + t:5 + t], st[:, 4 + t:5 + t], gates[:, t, 3 * h + 1 + branch:3 * h + 2 + branch],
                           ALU.mult, t_gates, loose=t > 0)
                return v

            def logits():
                unit_logits(u, lambda t: qT[lo:lo + HALF, h // 2, t * P:(t + 1) * P],
                            lambda k: kk[lo:lo + HALF, g, k], SCALE, lambda: bias_pair(h), (t_q, ready), coef)
                unit_scale(u)

            def values():
                pair = h // 2
                if branch == 0:
                    if h % 2 == 0:
                        head_bank[pair] = banks.take()
                    b = head_bank[pair]
                    base = 32 * (h % 4)
                    mm(b.t[lo:lo + HALF, 0:SEQ], v_cmp[base:base + NCMP, g, :], pcT[base:base + NCMP, g, :], t_vc, t_pcT,
                       *b.after, stop=False)
                b = head_bank[pair]
                p_ = pT[:, u["s"], :]
                mm(b.t[lo:lo + HALF, 0:SEQ], v_sw[:, 0, col0 + g * HALF:col0 + (g + 1) * HALF], p_[:, 0:SEQ],
                   u["pT"], t_vs, t_vw, start=False, stop=False)
                m = mm(b.t[lo:lo + HALF, P:SEQ], v_sw[:, 1, col0 + g * HALF:col0 + (g + 1) * HALF], p_[:, SEQ:UC],
                       start=False, stop=branch == 1)
                pT_reader[u["s"]] = (m,)
                if h % 2 and branch:
                    head_out(b, pair, m)
            return [logits, lambda: unit_transpose(u), values]

        b = banks.take()
        for g in range(2):
            for t in range(QT):
                m = turned(b.t[:, g * SEQ + t * P:g * SEQ + (t + 1) * P],
                           pc[:, t * 8 + g * 4:t * 8 + g * 4 + 4, :].rearrange("p a b -> p (a b)"), ident, t_pc, *b.after)
        t_pcT = copy("scalar", pcT.rearrange("p a b -> p (a b)"), b.t[:, :], m)
        banks.give(b, t_pcT)
        run_units([nsa_unit(h, br) for h in range(8) for br in range(2)], (0, 2, 3), latent_queries())

        w_uv, uv_landed, uv_slot = ring.load(I["dsa_w_uv"][0].rearrange("r h d -> r (h d)"))
        dbias = over_relu.take(2, UC)
        db_reader = [(), ()]
        olat_reader = [(), ()]

        def dsa_unit(h):
            u = {}

            def logits():
                s = h % 2
                tt("gpsimd", dbias[:, s, 0:P], bias[:, 8 + h, P:SEQ], taken[:, 0:P], ALU.add, t_sel, *db_reader[s])
                g_ = tt("gpsimd", dbias[:, s, P:UC], bias[:, 8 + h, :], taken[:, P:UC], ALU.add)
                unit_logits(u, lambda t: qlatT[:, h, t * P:(t + 1) * P], lambda k: ckvT[:, k], SCALE,
                            lambda: ((dbias[:, s, 0:P], dbias[:, s, P:UC]), g_), (t_ql[h], t_ckvT), None)
                db_reader[s] = (u["v"],)
                unit_scale(u)

            def values():
                s = h % 2
                b = banks.take()
                p_ = pT[:, u["s"], :]
                mm(b.t[:, 0:SEQ], ckv[:, 0, :], p_[:, 0:SEQ], u["pT"], t_ckv, *b.after, stop=False)
                m = mm(b.t[:, P:SEQ], ckv[:, 1, :], p_[:, SEQ:UC], start=False)
                pT_reader[u["s"]] = (m,)
                c = copy("scalar", olat[:, s, :], b.t[:, 0:SEQ], m, *olat_reader[s])
                banks.give(b, c)
                u["olat"] = c

            def project():
                s, lo, pair = h % 2, h % 2 * HALF, h // 2
                if h % 2 == 0:
                    head_bank[pair] = banks.take()
                b = head_bank[pair]
                m = mm(b.t[lo:lo + HALF, 0:SEQ], w_uv[:, h * HALF:(h + 1) * HALF], olat[:, s, :], uv_landed,
                       u["olat"], *b.after)
                olat_reader[s] = (m,)
                if h == 7:
                    ring.done(uv_slot, m)
                if h % 2:
                    head_out(b, 4 + pair, m)
            return [logits, lambda: unit_transpose(u), values, project]

        ln_sem = [ctx.enter_context(nc.semaphore(f"ln_rows_in{i}")) for i in range(2)]
        ln_reader = [()]
        ln_uses = [0]
        x_state = {"x": (in_x[0], in_x[1])}

        class OutProduct:

            def __init__(self, n_chunks):
                self.n, self.i, self.tail = n_chunks, 0, []
                self.ys = None
                self.m = [None] * QT

            def multiply(self, chunk, src, t, first, last):
                w, w_ready, _ = chunk
                for kk, (h_, l_, src_ready) in enumerate(src):
                    for half in range(2):
                        b = self.ys[t][half]
                        cs = slice(half * 512, (half + 1) * 512)
                        self.m[t] = split_mm(
                            b.t[:, :], (h_[:, t * P:(t + 1) * P], l_[:, t * P:(t + 1) * P]),
                            (w[0][:, kk, cs], w[1][:, kk, cs]), w_ready, src_ready,
                            *(b.after if first and kk == 0 else ()),
                            start=first and kk == 0, stop=last and kk == KW - 1)

            def step(self, src):
                if self.ys is None:
                    self.ys = [[banks.take() for _ in range(2)] for _ in range(QT)]
                chunk = weights.take()
                i = self.i
                self.i += 1
                if i < self.n - 2:
                    for t in range(QT):
                        self.multiply(chunk, src, t, i == 0, False)
                    weights.done(chunk[2], self.m[QT - 1])
                    weights.ahead()
                    return
                self.tail.append((chunk, src, i))
                if len(self.tail) == 2:
                    for t in range(QT):
                        for c_, src_, i_ in self.tail:
                            self.multiply(c_, src_, t, i_ == 0, i_ == self.n - 1)
                            if t == QT - 1:
                                weights.done(c_[2], self.m[t])

        head_halves = lambda i: [(oH[:, k, :], oL[:, k, :], t_oT[k]) for k in range(KW * i, KW * i + KW)]

        def out_steps(op, order):
            for i in order:
                while any(t_oT[k] is None for k in range(KW * i, KW * i + KW)):
                    yield
                op.step(head_halves(i))
                yield

        def residual_norm(op, sub, ln, next_mod):
            rows_in = []
            ln_uses[0] += 1
            for i, name in enumerate(("ln_g", "ln_b")):
                rows_in.append(q.dma(lambda e, i=i, name=name: e.dma_start(
                    ln_rows[:, i, :], I[name][ln // 2, ln % 2].partition_broadcast(P)), ln_sem[i],
                    16 * ln_uses[0], *ln_reader[0]))
            t_mod = next_mod() if next_mod else None
            done, xs = [], []
            for t in range(QT):
                y = y_tmp[:, t, :]
                for half in range(2):
                    b = op.ys[t][half]
                    v = tt("vector", y[:, half * 512:(half + 1) * 512], b.t[:, :], gate_rows[:, sub, half * 512:(half + 1) * 512],
                           ALU.mult, op.m[t], t_gate[sub], loose=True)
                    banks.give(b, v)
                stt(y, x_tok[:, t, :], ALPHA, y, ALU.mult, ALU.add, x_state["x"][t])
                st = stats[:, t, :]
                for half in range(2):
                    V(lambda e, o=st[:, 6 * half:6 * half + 6], i_=y[:, half * 512:(half + 1) * 512]: e.bn_stats(o, i_),
                      loose=half > 0)
                v = V(lambda e, o=st[:, 12:14], i_=st[:, 0:12]: e.bn_aggr(o, i_))
                mean, var, tmp, rstd, shift = (st[:, 12 + i:13 + i] for i in range(5))
                v = rsqrt_col(rstd, var, tmp, 1e-5)
                v = stt(shift, mean, -1.0, rstd, ALU.mult, ALU.mult)
                n_done = act(n_tok[:, t, :], y, ACT.Identity, v, scale=rstd, bias=shift)
                if next_mod:
                    done += to_features(n_tok[:, t, :], n_done, hT, (hH, hL), mod_cols[:, 0, :], mod_cols[:, 1, :], t_mod,
                                        (op.m[QT - 1],), t * P)
                weights.ahead()
                tt("gpsimd", x_tok[:, t, :], n_tok[:, t, :], ln_rows[:, 0, :], ALU.mult, n_done, *rows_in)
                g_ = tt("gpsimd", x_tok[:, t, :], x_tok[:, t, :], ln_rows[:, 1, :], ALU.add)
                xs.append(g_)
            gate_reader[sub] = (v,)
            ln_reader[0] = (g_,)
            x_state["x"] = xs
            return done

        US = 4
        uH, uL = hi_lo.at(KT * L2, US * KW, SEQ)

        def mlp(t_src, between=None):
            n = DFF // CW
            op = OutProduct(n)
            made, used = {}, {}
            for step in range(n + MLP_LAG):
                if step < n:
                    w, ready, slot = weights.take()
                    b = banks.take()
                    for i in range(KW):
                        m = feature_product3(w, i * P, (hH, hL), all_toks, b.t[:, i * SEQ:(i + 1) * SEQ], ready, *t_src, *b.after)
                    weights.done(slot, m)
                    weights.ahead()
                    r_ = relu_tmp[:, step % 2, :]
                    s1 = act(r_, b.t[:, :], ACT.Relu, m, made.get(step - 2))
                    banks.give(b, s1)
                    g1 = tt("gpsimd", r_, r_, r_, ALU.mult, s1)
                    s_ = step % US
                    grp = (slice(None), slice(s_ * KW, (s_ + 1) * KW))
                    made[step] = split_into(uH[grp], uL[grp], r_.rearrange("p (a b) -> p a b", a=KW), g1, used.get(step - US))
                if step >= MLP_LAG:
                    i = step - MLP_LAG
                    s_ = i % US
                    op.step([(uH[:, s_ * KW + k, :], uL[:, s_ * KW + k, :], made[i]) for k in range(KW)])
                    used[i] = op.m[QT - 1]
                if between is not None:
                    between(step)
            return op

        op = OutProduct(KT // KW)
        run_units([dsa_unit(h) for h in range(8)], (0, 2, 3, 4), out_steps(op, range(KT // KW)))
        ln_reader[0] = (t_oT[7],)
        t_h = residual_norm(op, 0, 0, lambda: modulation(1, 0))

        def ada_between(step):
            if pending:
                ada_finish()
            if 1 <= step <= 10:
                ada_start(1, step - 1)

        op = mlp(t_h, ada_between)
        t_h = residual_norm(op, 1, 1, lambda: modulation(0, 1))

        ar.at = phase_base
        spare = ar.over(spare_at, 2 * QT * D)
        x_done = x_state["x"]
        PAIRS = 3
        q2T = ar.take(2 * PAIRS, SEQ)
        k2T = ar.take(2 * PAIRS, SEQ)
        v2 = ar.take(2 * PAIRS, SEQ)
        zb = spare.take(NB, UC)
        pT = spare.take(NB, UC)
        ust = ar.take(NB, 8)
        o_tok = spare.take(2, SEQ)
        o_st = ar.take(2, 8)
        lam = ar.take(4 * 64)
        lam_p = ar.take(2 * 64)
        lam_c = ar.take(4)
        m = op.m[QT - 1]
        z_reader, pT_reader = [(m, *x_done)] * NB, [(m, *x_done)] * NB
        in_lam = q.load("lam", lam, I["diff_lam"][0].rearrange("a d -> (a d)").partition_broadcast(P), m)
        l4 = lam.rearrange("p (a b d) -> p a b d", a=2, b=2)
        tt("vector", lam_p.rearrange("p (a d) -> p a d", a=2), l4[:, :, 0, :], l4[:, :, 1, :], ALU.mult, in_lam)
        v1 = reduce_(lam_c[:, 0:2], lam_p.rearrange("p (a d) -> p a d", a=2), ALU.add)
        s1 = act(lam_c[:, 0:2], lam_c[:, 0:2], ACT.Exp, v1)
        tt("vector", lam_c[:, 2:3], lam_c[:, 1:2], lam_c[:, 0:1], ALU.subtract, s1)
        t_lam = ts("vector", lam_c[:, 2:3], lam_c[:, 2:3], -LAMBDA_INIT, None, ALU.add, None)
        subln = ar.take(1)
        t_subln = ts("vector", subln, col("subln"), 1.0 - LAMBDA_INIT, None, ALU.mult, None)

        t_oT = [None] * KT
        pair_in, pair_read = {}, {}

        def pair_projection(i):
            s = i % PAIRS
            while i >= PAIRS and i - PAIRS not in pair_read:
                yield
            free = pair_read.get(i - PAIRS, ())
            for part, dst in ((0, q2T), (1, k2T)):
                w, ready, slot = weights.take()
                b = banks.take()
                for j in range(2):
                    m = feature_product3(w, j * P, (hH, hL), all_toks, b.t[:, j * SEQ:(j + 1) * SEQ], ready, *t_h, *b.after)
                weights.done(slot, m)
                weights.ahead()
                t_qk = copy("scalar", dst[:, 2 * s:2 * s + 2, :], b.t[:, :].rearrange("p (a b) -> p a b", a=2), m, *free)
                banks.give(b, t_qk)
                yield
            w, ready, slot = weights.take()
            b = banks.take()
            for t in range(QT):
                m = token_product3(w, CW, (hH, hL), tok_tile(t), b.t[:, t * CW:(t + 1) * CW], ready, *b.after)
            weights.done(slot, m)
            weights.ahead()
            t_v2 = copy("scalar", v2[:, 2 * s:2 * s + 2, :], b.t[:, :].rearrange("p (a b) -> p a b", a=2), m, *free)
            banks.give(b, t_v2)
            pair_in[i] = (t_qk, t_v2)
            yield

        def diff_unit(h):
            ua, ub = {}, {}
            i, tile = h // 2, 2 * (h // 2 % PAIRS) + h % 2

            def logits():
                for mp, u in ((0, ua), (1, ub)):
                    lo = mp * HALF

                    def coef(st, v):
                        return ts("vector", st[:, 4:6], st[:, 4:6], lam_c[:, 2:3], None, ALU.mult, None, t_lam)
                    unit_logits(u, lambda t: q2T[lo:lo + HALF, tile, t * P:(t + 1) * P],
                                lambda k: k2T[lo:lo + HALF, tile, k], SCALE, lambda: bias_pair(2 * h + mp), (pair_in[i][0],),
                                coef if mp else None)
                unit_scale(ua)
                stt(ua["z"][:, 0:P], ub["z"][:, 0:P], ub["st"][:, 4:5], ua["z"][:, 0:P], ALU.mult, ALU.add, ua["p"])
                v = stt(ua["z"][:, P:UC], ub["z"][:, P:UC], ub["st"][:, 5:6], ua["z"][:, P:UC], ALU.mult, ALU.add)
                ua["p"] = v
                z_reader[ub["s"]] = (v,)

            def values():
                s = h % 2
                p_ = pT[:, ua["s"], :]
                t_v2 = pair_in[i][1]
                vh = slice((h % 2) * P, (h % 2 + 1) * P)
                v0, v1_ = v2[:, 2 * (i % PAIRS), vh], v2[:, 2 * (i % PAIRS) + 1, vh]
                b = banks.take()
                mm(b.t[:, 0:P], p_[:, 0:P], v0, ua["pT"], t_v2, *b.after)
                mm(b.t[:, P:SEQ], p_[:, P:SEQ], v0, stop=False)
                m = mm(b.t[:, P:SEQ], p_[:, SEQ:UC], v1_, start=False)
                pT_reader[ua["s"]] = (m,)
                if h % 2:
                    pair_read[i] = (m,)
                st, o = o_st[:, s, :], o_tok[:, s, :]
                for t in range(QT):
                    s1 = act(o[:, t * P:(t + 1) * P], b.t[:, t * P:(t + 1) * P], ACT.Square, m, *o_free[s],
                             accum=st[:, t:t + 1])
                ts("vector", st[:, 0:2], st[:, 0:2], 1.0 / P, None, ALU.mult, None, s1)
                rsqrt_col(st[:, 2:4], st[:, 0:2], st[:, 4:6], 1e-5)
                for t in range(QT):
                    v = ts("vector", o[:, t * P:(t + 1) * P], b.t[:, t * P:(t + 1) * P], st[:, 2 + t:3 + t], None,
                           ALU.mult, None)
                banks.give(b, v)
                ua["o"] = v

            def turn():
                s = h % 2
                b = banks.take()
                for t in range(QT):
                    m = turned(b.t[:, t * P:(t + 1) * P], o_tok[:, s, t * P:(t + 1) * P], ident, ua["o"], *b.after)
                o_free[s] = (m,)
                t_oT[h] = split_into(oH[:, h, :], oL[:, h, :], b.t[:, 0:SEQ], m, t_subln, scale=subln[:, 0:1])
                banks.give(b, t_oT[h])
            return [logits, lambda: unit_transpose(ua), values, turn]

        o_free = [x_done, x_done]
        op = OutProduct(KT // KW)

        def layer_two_fill():
            for i in range(1, 4):
                yield from pair_projection(i)
                ada = 10 + (i - 1)
                if ada < 12:
                    ada_start(1, ada)
                if pending and i > 1:
                    ada_finish()
            while pending:
                ada_finish()
            yield from out_steps(op, range(KT // KW))

        for _ in pair_projection(0):
            pass
        fill = layer_two_fill()
        units = [diff_unit(h) for h in range(8)]
        lags = (0, 1, 2, 4)
        for step in range(len(units) + lags[-1]):
            for stage, lag in reversed(list(enumerate(lags))):
                if 0 <= step - lag < len(units):
                    units[step - lag][stage]()
            for _ in range(2):
                next(fill, None)
        for _ in fill:
            pass
        t_h = residual_norm(op, 0, 2, lambda: modulation(1, 2))
        op = mlp(t_h)
        residual_norm(op, 1, 3, None)
        m = op.m[QT - 1]

        ar.at = after_cols
        TT_ROWS = (P, P, META)
        TOK_AT = (META, META + P, 0)
        masks = ar.take(4 + 2 * LEVELS, P)
        a_log_row, dtb_row = ar.take(8), ar.take(8)
        qk_norm_row = ar.take(2, 64)
        rope = ar.take(3, 64)
        cT = ar.take(12, L2)
        kv_tok = ar.take(3, 2, 512)
        z_tok = ar.take(QT, 512)
        av = ar.take(3, P)
        ba = ar.take(3, 16)
        o_acc = ar.take(QT, 512)
        st2 = ar.take(3, 24)
        ex_row = ar.take(8)
        aqk_at = ar.at
        aqk = ar.take(3, 10, 64)
        delta_at = ar.at
        n2 = ar.take(2, D)
        u2T = ar.take(KT, L2)
        conv = ar.take(12, L2 + 4)
        end_block_one = [m, *x_state["x"]]
        in_masks = q.load("masks", masks.rearrange("p a b -> p (a b)"), I["square_masks"][:, P:], *end_block_one)
        in_alog = q.load("alog", a_log_row, I["a_log_2"][0].rearrange("a b -> (a b)").partition_broadcast(P), *end_block_one)
        in_dtb = q.load("dtb", dtb_row, I["dt_bias_2"][0].rearrange("a b -> (a b)").partition_broadcast(P), *end_block_one)
        in_qn = q.load("qn", qk_norm_row[:, 0, :], I["q_norm_2"][0].partition_broadcast(P), *end_block_one)
        in_kn = q.load("kn", qk_norm_row[:, 1, :], I["k_norm_2"][0].partition_broadcast(P), *end_block_one)
        meta_x = n2[0:META, 1, :]
        in_meta = q.load("meta", meta_x, I["meta_tokens_2"][:, :], *end_block_one)
        in_rope = [q.load(f"rope{t}", rope[0:TT_ROWS[t], t, :], I["rope_tables"][t * P:t * P + TT_ROWS[t], :], *end_block_one)
                   for t in range(3)]
        uH, uL = hi_lo.at(0, KT, L2)

        def rms_rows(src, t_src, dst, rows, st, width, eps, *after):
            s1 = act(dst, src, ACT.Square, t_src, *after, accum=st[0:rows, 0:1])
            ts("vector", st[0:rows, 1:2], st[0:rows, 0:1], 1.0 / width, None, ALU.mult, None, s1)
            v = rsqrt_col(st[0:rows, 2:3], st[0:rows, 1:2], st[0:rows, 3:4], eps)
            return act(dst, src, ACT.Copy, v, scale=st[0:rows, 2:3])

        t_u = []
        nm = ar.over(delta_at + 2 * D + KT * L2, D).take(D, rows=META)
        for t in (2, 0, 1):
            src = x_tok[:, t, :] if t < 2 else meta_x
            dst = (n2[:, 0, :], n2[:, 1, :], nm)[t]
            s1 = rms_rows(src, x_state["x"][t] if t < 2 else in_meta, dst, TT_ROWS[t], st2[:, t, :], D, 1e-6,
                          *end_block_one)
            t_u += to_features(dst, s1, u2T, (uH, uL), col("mix_pre", 0, KT), None, t_cols_ln, (m,), TOK_AT[t], TT_ROWS[t])

        every = slice(0, L2)
        memset("gpsimd", conv[:, :, 0:2], 0.0, *t_u)
        t_pad = memset("gpsimd", conv[:, :, L2 + 2:L2 + 4], 0.0)
        t_conv_in = [None] * 12

        def conv_projection(i0):
            w, ready, slot = weights.take()
            for i in range(2):
                b = banks.take()
                m = feature_product3(w, i * P, (uH, uL), every, b.t[:, 0:L2], ready, *t_u, *b.after)
                t_conv_in[i0 + i] = copy("scalar", conv[:, i0 + i, 2:L2 + 2], b.t[:, 0:L2], m)
                banks.give(b, t_conv_in[i0 + i])
            weights.done(slot, m)
            weights.ahead()

        def conv_group(g4):
            for i in range(4 * g4, 4 * g4 + 4):
                tap = lambda j: col("conv", j * 12 + i)
                v = ts("vector", cT[:, i, :], conv[:, i, 0:L2], tap(0), None, ALU.mult, None, t_conv_in[i], t_pad, t_cols_b)
                for j in range(1, 5):
                    v = stt(cT[:, i, :], conv[:, i, j:j + L2], tap(j), cT[:, i, :], ALU.mult, ALU.add)
            grp = slice(4 * g4, 4 * g4 + 4)
            return act(cT[:, grp, :], cT[:, grp, :], ACT.Silu, v)

        def l2_group(g4, t_silu):
            for i in range(4 * g4, 4 * g4 + 4):
                g_ = tt("gpsimd", conv[:, i, 0:L2], cT[:, i, :], cT[:, i, :], ALU.mult, t_silu, *t_convs[g4])
                sq_t[i] = g_

        sq_t = [None] * 12
        t_convs = [()] * 3
        t_cT = [None] * 12

        def l2_finish(g4):
            for i in range(4 * g4, 4 * g4 + 4):
                b = banks.take()
                m1 = mm(b.t[:, 0:L2], ones, conv[:, i, 0:L2], sq_t[i], *b.after)
                s_ = act(conv[:, i, 0:L2], b.t[:, 0:L2], ACT.Ln, m1, m_eps, bias=eps6[:, 0:1])
                banks.give(b, s_)
            grp = slice(4 * g4, 4 * g4 + 4)
            s_ = act(conv[:, grp, 0:L2], conv[:, grp, 0:L2], ACT.Exp, scale=-0.5)
            if g4 == 0:
                v = stt(cT[:, grp, :], conv[:, grp, 0:L2], P ** -0.5, cT[:, grp, :], ALU.mult, ALU.mult, s_)
            else:
                v = tt("vector", cT[:, grp, :], conv[:, grp, 0:L2], cT[:, grp, :], ALU.mult, s_)
            for i in range(4 * g4, 4 * g4 + 4):
                t_cT[i] = v

        for g4 in (1, 0):
            for half in range(2):
                conv_projection(4 * g4 + 2 * half)
            l2_group(g4, conv_group(g4))
        for half in range(2):
            conv_projection(8 + 2 * half)
        t_silu_v = conv_group(2)
        for i in range(8, 12):
            t_cT[i] = t_silu_v

        w, landed, slot = ring.load(w_in[:, :, 2048:2064])
        b = banks.take()
        for t in range(3):
            r = TT_ROWS[t]
            m = token_product(w, 0, 16, u2T, slice(TOK_AT[t], TOK_AT[t] + r), b.t[0:r, t * 16:t * 16 + 16], landed, *b.after)
        ring.done(slot, m)
        for t in range(3):
            r = TT_ROWS[t]
            t_ba = copy("scalar", ba[0:r, t, :], b.t[0:r, t * 16:t * 16 + 16], m)
        banks.give(b, t_ba)
        for half in range(2):
            w, ready, slot = weights.take()
            b = banks.take()
            for t in range(QT):
                m = token_product3(w, CW, (uH, uL), slice(TOK_AT[t], TOK_AT[t] + P), b.t[:, t * CW:(t + 1) * CW],
                                   ready, *b.after)
            weights.done(slot, m)
            weights.ahead()
            t_aq = copy("scalar", aqk[:, 0:2, 4 * half:4 * half + 4, :],
                        b.t[:, :].rearrange("p (t h d) -> p t h d", t=2, d=64), m)
            banks.give(b, t_aq)
        w, landed, slot = ring.load(w_in[:, :, 2576:2832])
        for t in range(3):
            r = TT_ROWS[t]
            b = banks.take()
            m = token_product(w, 0, CW, u2T, slice(TOK_AT[t], TOK_AT[t] + r), b.t[0:r, 0:CW], landed, *b.after)
            copy("scalar", aqk[0:r, t, 8:10, :], b.t[0:r, 0:P].rearrange("p (h d) -> p h d", d=64), m)
            t_av = copy("scalar", av[0:r, t, :], b.t[0:r, P:CW])
            banks.give(b, t_av)
        ring.done(slot, m)
        for half in range(2):
            w, ready, slot = weights.take()
            b = banks.take()
            for t in range(QT):
                m = token_product3(w, CW, (uH, uL), slice(TOK_AT[t], TOK_AT[t] + P), b.t[:, t * CW:(t + 1) * CW],
                                   ready, *b.after)
            weights.done(slot, m)
            weights.ahead()
            t_z = act(z_tok[:, :, half * CW:(half + 1) * CW], b.t[:, :].rearrange("p (t n) -> p t n", t=2), ACT.Silu, m)
            banks.give(b, t_z)
        proj_done = m

        s1 = act(ex_row, a_log_row, ACT.Exp, in_alog)
        ts("vector", ex_row, ex_row, -1.0, None, ALU.mult, None, s1)
        for t in range(3):
            r = TT_ROWS[t]
            b_, g_, tmp, tmp2 = ba[0:r, t, 0:8], ba[0:r, t, 8:16], st2[0:r, t, 8:16], st2[0:r, t, 16:24]
            v = ts("vector", tmp, b_, -EXP_MAX, None, ALU.max, None, t_ba)
            s1 = act(tmp, tmp, ACT.Exp, v, scale=-1.0)
            ts("vector", tmp, tmp, 1.0, None, ALU.add, None, s1)
            recip(b_, tmp)
            v = tt("vector", g_, g_, dtb_row[0:r, :], ALU.add, in_dtb)
            ts("vector", tmp2, g_, -1.0, None, ALU.mult, None)
            v = tt("vector", tmp, g_, tmp2, ALU.max)
            act(tmp, tmp, ACT.Exp, v, scale=-1.0)
            s1 = act(tmp, tmp, ACT.Ln, bias=ones[0:r, 0:1])
            stt(g_, g_, 0.0, tmp, ALU.max, ALU.add, s1)
            t_bg = tt("vector", g_, g_, ex_row[0:r, :], ALU.mult)
        l2_finish(1)
        l2_finish(0)

        for kv in (1, 0):
            for t in (2, 0, 1):
                r = TT_ROWS[t]
                b = banks.take()
                for h in range(4):
                    m = turned(b.t[0:r, h * P:(h + 1) * P], cT[:, 4 + 4 * kv + h, TOK_AT[t]:TOK_AT[t] + r], ident,
                               *(t_cT[8:] if kv else t_cT), *b.after)
                t_kv = copy("scalar", kv_tok[0:r, t, kv, :], b.t[0:r, :], m)
                banks.give(b, t_kv)

        ar.at = delta_at
        delta_cols = 12 * 512 * 2 + 2 * 24
        rot_at = delta_at
        aT = ar.take(4, SEQ)
        akT = ar.take(2, L2)
        buf_at = ar.at
        rot = ar.take(3, 10, 64)
        rst = ar.take(3, 3, 10)
        sqk = ar.take(10, 64)
        t_rot = []
        for t in range(3):
            r, h0 = TT_ROWS[t], 0 if t < 2 else 8
            x_ = aqk[0:r, t, h0:10, :]
            n = 10 - h0
            sq_ = sqk[0:r, h0:10, :]
            s0_, s1_, s2_ = (rst[0:r, t, i, h0:10] for i in range(3))
            tt("vector", sq_, x_, x_, ALU.mult, t_av, t_aq, proj_done, *t_cT, t_kv)
            reduce_(s0_, sq_, ALU.add)
            ts("vector", s0_, s0_, 1.0 / 64, None, ALU.mult, None)
            rsqrt_col(s1_, s0_, s2_, 1e-6)
            tt("vector", x_, x_, s1_.unsqueeze(2).broadcast_to([r, n, 64]), ALU.mult)
            if t < 2:
                tt("vector", x_[:, 0:8, :], x_[:, 0:8, :],
                   qk_norm_row[0:r, 0:1, :].broadcast_to([r, 8, 64]), ALU.mult, in_qn)
            tt("vector", x_[:, n - 2:n, :], x_[:, n - 2:n, :],
               qk_norm_row[0:r, 1:2, :].broadcast_to([r, 2, 64]), ALU.mult, in_kn)
            for ax in range(2):
                lo_, hi_ = x_[:, :, 32 * ax:32 * ax + 16], x_[:, :, 32 * ax + 16:32 * ax + 32]
                cos = rope[0:r, t, 16 * ax:16 * ax + 16].unsqueeze(1).broadcast_to([r, n, 16])
                sin = rope[0:r, t, 32 + 16 * ax:48 + 16 * ax].unsqueeze(1).broadcast_to([r, n, 16])
                o_lo = rot[0:r, t, h0:10, 32 * ax:32 * ax + 16]
                o_hi = rot[0:r, t, h0:10, 32 * ax + 16:32 * ax + 32]
                tmp = sq_[:, :, 0:16]
                tt("vector", o_lo, lo_, cos, ALU.mult, in_rope[t])
                tt("vector", tmp, hi_, sin, ALU.mult)
                tt("vector", o_lo, o_lo, tmp, ALU.subtract)
                tt("vector", o_hi, hi_, cos, ALU.mult)
                tt("vector", tmp, lo_, sin, ALU.mult)
                v = tt("vector", o_hi, o_hi, tmp, ALU.add)
            t_rot.append(v)
        for t in range(QT):
            b = banks.take()
            for i in range(4):
                m = turned(b.t[:, i * P:(i + 1) * P], rot[:, t, 2 * i:2 * i + 2, :].rearrange("p a b -> p (a b)"), ident,
                           t_rot[t], *b.after)
            t_aT = copy("scalar", aT[:, :, t * P:(t + 1) * P], b.t[:, :].rearrange("p (a b) -> p a b", a=4), m)
            banks.give(b, t_aT)
        b = banks.take()
        for t in range(3):
            r = TT_ROWS[t]
            m = turned(b.t[:, t * P:t * P + r], rot[0:r, t, 8:10, :].rearrange("p a b -> p (a b)"), ident[0:r, 0:r],
                       t_rot[t], *b.after)
        for g in range(2):
            for half in range(2):
                t_ak = copy("scalar", akT[half * HALF:(half + 1) * HALF, g, :], b.t[g * HALF:(g + 1) * HALF, 0:L2], m)
        banks.give(b, t_ak)
        rot_done = m

        NA = 3
        over_aqk = ar.over(aqk_at, 3 * 640)
        za = over_aqk.take(NA, L2)
        paT_at = ar.at = buf_at
        paT = ar.take(NA, 3 * P)
        ast = ar.take(NA, 4)
        za_reader, paT_reader = [(t_rot[2],)] * NA, [(rot_done,)] * NA
        a_n = [0]
        a_bank = {}
        t_oT = [None] * KT
        ready_oT = {}

        def axial_unit(h, t):
            u = {}
            lo, pair, g = h % 2 * HALF, h // 2, h // 4

            def logits():
                s = u["s"] = a_n[0] % NA
                a_n[0] += 1
                b = banks.take()
                m = mm(b.t[:, 0:L2], aT[lo:lo + HALF, pair, t * P:(t + 1) * P], akT[lo:lo + HALF, g, :], t_aT, t_ak,
                       *b.after)
                st = ast[:, s, :]
                reduce_(st[:, 0:1], b.t[:, 0:L2], ALU.max, m, rot_done, negate=True)
                v = ts("vector", st[:, 0:1], st[:, 0:1], SCALE, None, ALU.mult, None)
                a = act(za[:, s, :], b.t[:, 0:L2], ACT.Exp, v, *za_reader[s], bias=st[:, 0:1], scale=SCALE,
                        accum=st[:, 1:2], loose=True)
                banks.give(b, a)
                v = recip(st[:, 2:3], st[:, 1:2], a)
                u["p"] = ts("gpsimd", za[:, s, :], za[:, s, :], st[:, 2:3], None, ALU.mult, None, v, loose=True)

            def turn():
                s = u["s"]
                b = banks.take()
                turned(b.t[:, 0:P], za[:, s, 0:P], ident, u["p"], *b.after)
                turned(b.t[:, P:2 * P], za[:, s, P:2 * P], ident)
                m = turned(b.t[0:META, 2 * P:3 * P], za[:, s, SEQ:L2], ident)
                za_reader[s] = (m,)
                copy("scalar", paT[:, s, 0:SEQ], b.t[:, 0:SEQ], m, *paT_reader[s], loose=True)
                u["pT"] = copy("scalar", paT[0:META, s, SEQ:3 * P], b.t[0:META, SEQ:3 * P])
                banks.give(b, u["pT"])

            def values():
                s = u["s"]
                if h % 2 == 0 and t == 0:
                    a_bank[pair] = banks.take()
                b = a_bank[pair]
                o = b.t[lo:lo + HALF, t * P:(t + 1) * P]
                for kt in range(3):
                    r = TT_ROWS[kt]
                    m = mm(o, av[0:r, kt, g * HALF:(g + 1) * HALF], paT[0:r, s, kt * P:(kt + 1) * P], u["pT"], t_av,
                           *b.after, start=kt == 0, stop=kt == 2)
                paT_reader[s] = (m,)
                if h % 2 and t == 1:
                    head_out(b, 4 + pair, m)
            return [logits, turn, values]

        def axial_steps():
            units = [axial_unit(2 * pair + i, t) for pair in range(4) for t in range(QT) for i in range(2)]
            lags = (0, 1, 2)
            for step in range(len(units) + lags[-1]):
                for stage, lag in reversed(list(enumerate(lags))):
                    if 0 <= step - lag < len(units):
                        units[step - lag][stage]()
                        yield

        names = ("a", "qk", "aT", "lT", "x", "xT", "w", "bv", "bek", "kdec", "qdec", "s")
        lent = [ring.lend() for _ in range(2)]
        slot_buf = [s_[:, i * 512:(i + 1) * 512].rearrange("p (a b) -> p a b", a=4) for s_, _ in lent for i in range(4)]
        buf = [{n: ar.take(4, P) for n in names}, {n: slot_buf[i] if i < 8 else ar.take(4, P) for i, n in enumerate(names)}]
        dst_ = [ar.take(6, 4) for _ in range(2)]
        t_o = [None] * QT
        t_s = [None, None]
        axial_done = rot_done

        def chunk(d, t, first):
            B, st = buf[d], dst_[d]
            C, at = TT_ROWS[t], TOK_AT[t]
            back = d if t < 2 else 0
            real = t < 2
            M1, strict = masks[0:C, back, 0:C], masks[0:C, 2 + back, 0:C]
            level = lambda l, back_: masks[0:C, 4 + LEVELS * back_ + l, 0:C]
            beta, g = ba[0:C, t, 4 * d:4 * d + 4], ba[0:C, t, 8 + 4 * d:12 + 4 * d]
            wide = lambda a: a.unsqueeze(1).broadcast_to([C, 4, C])
            per = lambda c: c.unsqueeze(2).broadcast_to([C, 4, P])
            v_ = lambda n, w_=C: B[n][0:C, :, 0:w_]
            gc, e_tot, e_gc, e_last, bg = (st[:, i, :] for i in range(5))
            cols_ = slice(at, at + C)

            b = banks.take()
            mm(b.t[0:C, 0:4], M1, g, t_bg, in_masks, axial_done, *b.after)
            m = mm(b.t[:, 4:8], ones[0:C, :], g)
            copy("scalar", gc[0:C], b.t[0:C, 0:4], m, t_s[d])
            act(e_last, b.t[:, 4:8], ACT.Exp)
            c = copy("scalar", e_tot[0:C], b.t[0:C, 4:8])
            banks.give(b, c)
            v = tt("vector", e_tot[0:C], e_tot[0:C], gc[0:C], ALU.subtract, c)
            act(e_tot[0:C], e_tot[0:C], ACT.Exp, v)
            s_ = act(e_gc[0:C], gc[0:C], ACT.Exp)
            v = tt("vector", bg[0:C], e_gc[0:C], beta, ALU.mult, s_)
            gw = copy("gpsimd", B["w"][0:C], per(g), t_bg, m, t_s[d])
            yield
            R = banks.take()
            for h in range(4):
                m = mm(R.t[0:P if real else C, h * P:h * P + C], B["w"][0:C, h, 0:P if real else C], M1, gw, *R.after)
            Rv = R.t[:, :].rearrange("p (h c) -> p h c", h=4)
            K = banks.take()
            for h in range(4):
                kT_ = cT[:, 4 + h, cols_]
                mk = mm(K.t[0:C, h * P:h * P + C], kT_, kT_, *t_cT, *K.after)
            for h in range(4):
                v = ts("vector", B["a"][0:C, h, 0:C], Rv[0:C, h, 0:C], gc[0:C, h:h + 1], 0.0, ALU.subtract, ALU.max, m)
                if real:
                    v = ts("vector", B["qk"][0:C, h, 0:C], Rv[0:C, h, 0:C], gc[0:C, h:h + 1], 0.0, ALU.subtract, ALU.min)
            if real:
                act(B["qdec"], Rv, ACT.Exp, v)
            s_ = act(v_("a"), v_("a"), ACT.Exp, v, scale=-1.0)
            banks.give(R, s_)
            yield
            v = tt("vector", v_("a"), v_("a"), wide(strict), ALU.mult, s_)
            for h in range(4):
                v = stt(B["a"][0:C, h, 0:C], K.t[0:C, h * P:h * P + C], beta[:, h:h + 1], B["a"][0:C, h, 0:C], ALU.mult, ALU.mult, mk)
            banks.give(K, v)
            b = banks.take()
            for h in range(4):
                m = turned(b.t[0:C, h * P:h * P + C], B["a"][0:C, h, 0:C], ident[0:C, 0:C], v, *b.after)
            c = copy("scalar", v_("aT"), b.t[0:C, :].rearrange("p (h c) -> p h c", h=4)[:, :, 0:C], m)
            banks.give(b, c)
            tt("gpsimd", v_("x"), v_("a"), wide(level(0, 1 - back)), ALU.mult, v)
            gx = tt("gpsimd", v_("xT"), v_("aT"), wide(level(0, back)), ALU.mult, c)
            tt("gpsimd", B["bv"][0:C], kv_tok[0:C, t, 1, :].rearrange("p (h c) -> p h c", h=4), per(beta), ALU.mult, t_kv)
            if real:
                act(B["qk"], B["qk"], ACT.Exp)
                tt("gpsimd", B["qdec"], B["qdec"], cT[:, 0:4, cols_], ALU.mult)
            yield
            idn = wide(ident[0:C, 0:C])
            tt("vector", v_("x"), idn, v_("x"), ALU.subtract, gx)
            v = tt("vector", v_("xT"), idn, v_("xT"), ALU.subtract)
            n_levels = LEVELS if real else 4
            for l in range(1, n_levels):
                lt = "lT" if l % 2 else "a"
                g_ = tt("gpsimd", v_(lt), v_("aT"), wide(level(l, back)), ALU.mult, *((v,) if l == 1 else (mw,)))
                if l == 1:
                    tt("gpsimd", B["bek"][0:C], kv_tok[0:C, t, 0, :].rearrange("p (h c) -> p h c", h=4), per(bg[0:C]), ALU.mult, t_kv)
                    gk = tt("gpsimd", B["kdec"][0:C], kv_tok[0:C, t, 0, :].rearrange("p (h c) -> p h c", h=4), per(e_tot[0:C]), ALU.mult)
                b = banks.take()
                for h in range(4):
                    mw = mm(b.t[0:C, h * P:h * P + C], B[lt][0:C, h, 0:C], B["x"][0:C, h, 0:C], g_, v, *b.after)
                c = copy("scalar", v_("w"), b.t[0:C, :].rearrange("p (h c) -> p h c", h=4)[:, :, 0:C], mw)
                banks.give(b, c)
                yield
                last = l == n_levels - 1
                b2 = banks.take()
                b1 = None if last else banks.take()
                for h in range(4):
                    m2 = mm(b2.t[0:C, h * P:h * P + C], B["w"][0:C, h, 0:C], B["xT"][0:C, h, 0:C], c, *b2.after)
                if not last:
                    for h in range(4):
                        m1 = mm(b1.t[0:C, h * P:h * P + C], B["xT"][0:C, h, 0:C], B["w"][0:C, h, 0:C], *b1.after)
                    m2 = m1
                v = tt("vector", v_("xT"), v_("xT"), b2.t[0:C, :].rearrange("p (h c) -> p h c", h=4)[:, :, 0:C], ALU.subtract, m2)
                banks.give(b2, v)
                if not last:
                    v = tt("vector", v_("x"), v_("x"), b1.t[0:C, :].rearrange("p (h c) -> p h c", h=4)[:, :, 0:C], ALU.subtract)
                    banks.give(b1, v)
                yield
            if real:
                b = banks.take()
                for h in range(4):
                    m = mm(b.t[:, h * P:(h + 1) * P], cT[:, 4 + h, cols_], cT[:, h, cols_], *b.after)
                vq = tt("vector", B["qk"], B["qk"], wide(M1), ALU.mult)
                vq = tt("vector", B["qk"], B["qk"], b.t[:, :].rearrange("p (h c) -> p h c", h=4), ALU.mult, m)
                banks.give(b, vq)
                b = banks.take()
                for h in range(4):
                    m = mm(b.t[:, h * P:(h + 1) * P], B["bek"][:, h, :], B["xT"][:, h, :], gk, v, *b.after)
                nw = act(B["x"], b.t[:, :].rearrange("p (h c) -> p h c", h=4), ACT.Copy, m, scale=-1.0)
                banks.give(b, nw)
                yield
            b = banks.take()
            for h in range(4):
                m = mm(b.t[0:C, h * P:(h + 1) * P], B["xT"][0:C, h, 0:C], B["bv"][0:C, h, :], v, gk, *b.after, stop=not real)
                if real:
                    m = mm(b.t[0:C, h * P:(h + 1) * P], B["x"][:, h, :], B["s"][:, h, :], nw, t_s[d], start=False)
            vn = copy("scalar", B["bek"][0:C], b.t[0:C, :].rearrange("p (h c) -> p h c", h=4), m)
            banks.give(b, vn)
            yield
            if real:
                b = banks.take()
                for h in range(4):
                    mm(b.t[:, h * P:(h + 1) * P], B["qdec"][:, h, :], B["s"][:, h, :], *b.after, stop=False)
                    m = mm(b.t[:, h * P:(h + 1) * P], B["qk"][:, h, :], B["bek"][:, h, :], vn, vq, start=False)
                if t_o[t] is None:
                    t_o[t] = copy("vector", o_acc[:, t, :], b.t[:, :], m)
                else:
                    t_o[t] = tt("vector", o_acc[:, t, :], o_acc[:, t, :], b.t[:, :], ALU.add, m)
                banks.give(b, t_o[t])
                if not first:
                    return
            b = banks.take()
            for h in range(4):
                m = mm(b.t[:, h * P:(h + 1) * P], B["kdec"][0:C, h, :], B["bek"][0:C, h, :], gk, vn, *b.after)
            if not real:
                v = copy("vector", B["s"], b.t[:, :].rearrange("p (h c) -> p h c", h=4), m)
            else:
                for h in range(4):
                    v = stt(B["s"][:, h, :], B["s"][:, h, :], e_last[:, h:h + 1], b.t[:, h * P:(h + 1) * P], ALU.mult, ALU.add, m)
            banks.give(b, v)
            t_s[d] = v
            yield

        def delta_rule():
            for order in ((2, 2), (0, 1), (1, 0)):
                live = [chunk(d, order[d], order == (0, 1)) for d in range(2)]
                while live:
                    live = [c for c in live if next(c, "end") != "end"]
                    yield

        op = OutProduct(KT // KW)
        axial = axial_steps()
        for _ in delta_rule():
            for _ in range(2):
                next(axial, None)
        for _ in axial:
            pass
        delta_end = ("vector", q.sem["vector"], q.count["vector"])
        for _, slot in lent:
            ring.done(slot, delta_end)
        for i in (2, 3):
            op.step(head_halves(i))

        osq = buf[0]["qk"]
        hb = [banks.take() for _ in range(QT)]
        for t in range(QT):
            z_ = z_tok[:, t, :]
            o4 = o_acc[:, t, :].rearrange("p (h c) -> p h c", h=4)
            tt("vector", osq, o4, o4, ALU.mult, t_o[t], t_z)
            s0_, s1_, s2_ = (st2[:, t, 4 * i:4 * i + 4] for i in range(3))
            reduce_(s0_, osq, ALU.add)
            ts("vector", s0_, s0_, 1.0 / P, None, ALU.mult, None)
            rsqrt_col(s1_, s0_, s2_, 1e-6)
            tt("vector", o4, o4, s1_.unsqueeze(2).broadcast_to([P, 4, P]), ALU.mult)
            v = tt("vector", o_acc[:, t, :], o_acc[:, t, :], z_, ALU.mult)
            b = hb[t]
            for h in range(4):
                m2 = turned(b.t[:, h * P:(h + 1) * P], o_acc[:, t, h * P:(h + 1) * P], ident, v, *b.after)
            grp = (slice(None), slice(0, 4), slice(t * P, (t + 1) * P))
            c = split_into(oH[grp], oL[grp], b.t[:, :].rearrange("p (a b) -> p a b", a=4), m2, t_cols_ln,
                           scale=col("dn_norm"))
            banks.give(b, c)
        for i in range(4):
            t_oT[i] = c
        delta_done = c

        ar.at = after_cols
        n_tok = ar.take(QT, D)
        hT = ar.take(KT, SEQ)
        post = ar.take(2, D)
        st3 = ar.take(QT, 16)
        relu_tmp = ar.take(2, 512)
        in_post = [q.load(f"post{i}", post[:, i, :], I[name][0].partition_broadcast(P), delta_done)
                   for i, name in enumerate(("norm_mix_post_2", "norm_mlp_post_2"))]

        def post_norm_residual(op, which):
            res = []
            for t in range(QT):
                st = st3[:, t, :]
                for half in range(2):
                    s1 = act(n_tok[:, t, half * 512:(half + 1) * 512], op.ys[t][half].t[:, :], ACT.Square, op.m[t],
                             delta_done, accum=st[:, half:half + 1])
                tt("vector", st[:, 2:3], st[:, 0:1], st[:, 1:2], ALU.add, s1)
                ts("vector", st[:, 2:3], st[:, 2:3], 1.0 / D, None, ALU.mult, None)
                rsqrt_col(st[:, 3:4], st[:, 2:3], st[:, 4:5], 1e-6)
                for half in range(2):
                    c = slice(half * 512, (half + 1) * 512)
                    v = stt(n_tok[:, t, c], op.ys[t][half].t[:, :], st[:, 3:4], post[:, which, c], ALU.mult, ALU.mult,
                            in_post[which])
                    banks.give(op.ys[t][half], v)
                weights.ahead()
                res.append(tt("vector", x_tok[:, t, :], x_tok[:, t, :], n_tok[:, t, :], ALU.add))
            return res

        for i in (0, 1):
            op.step(head_halves(i))
        t_x = post_norm_residual(op, 0)
        t_h = []
        for t in range(QT):
            s1 = rms_rows(x_tok[:, t, :], t_x[t], n_tok[:, t, :], P, st3[:, t, 8:16], D, 1e-6)
            t_h += to_features(n_tok[:, t, :], s1, hT, (hH, hL), col("mlp_pre", 0, KT), None, t_cols_ln, (delta_done,), t * P)
        uH, uL = hi_lo.at(KT * L2, US * KW, SEQ)
        op = mlp(t_h)
        t_x = post_norm_residual(op, 1)
        out_sem = ctx.enter_context(nc.semaphore("out_stored"))
        for t in range(QT):
            stored = q.dma(lambda e, o=out[0, t * P:(t + 1) * P, :], i_=x_tok[:, t, :]: e.dma_start(o, i_),
                           out_sem, 16 * QT, t_x[t])
        q.stores.append(stored)
        finish(nc, q, ctx)


def finish(nc, q, ctx):
    block = ctx.enter_context(nc.Block())

    @block.sync
    def _(eng):
        q.emit("sync", eng)
        for name, sem, value in q.stores:
            eng.wait_ge(sem, value)

    @block.tensor
    def _(eng):
        q.emit("tensor", eng)

    @block.vector
    def _(eng):
        q.emit("vector", eng)

    @block.scalar
    def _(eng):
        q.emit("scalar", eng)

    @block.gpsimd
    def _(eng):
        q.emit("gpsimd", eng)


INPUTS = [
    "x", "c", "rel_bias", "ada_w", "ada_b", "ln_g", "ln_b", "ev_w_in", "ev_w_out", "nsa_pe_k", "nsa_pe_v",
    "nsa_w1_k", "nsa_w2_k", "nsa_w1_v", "nsa_w2_v", "dsa_kv_norm", "dsa_w_uk", "dsa_w_uv", "od_w_in", "od_w_out",
    "diff_lam", "diff_subln", "mlp_w1", "mlp_w2", "meta_tokens_2", "w_in_2", "conv_w_2", "a_log_2", "dt_bias_2",
    "dn_out_norm_2", "q_norm_2", "k_norm_2", "w_out_2", "norm_mix_pre_2", "norm_mix_post_2", "w_up_2",
    "w_down_2", "norm_mlp_pre_2", "norm_mlp_post_2",
]


def prepare(inputs):
    arrays = {n: np.ascontiguousarray(inputs[n]) for n in INPUTS}
    arrays["bucket_rows"] = bucket_rows()
    arrays["square_masks"] = square_masks()
    arrays["rope_tables"] = rope_tables()
    return arrays


def kernel(**inputs):
    import concourse.bacc as bacc
    from concourse.bass_utils import run_bass_kernel_spmd

    nc = bacc.Bacc("TRN2", target_bir_lowering=False, num_devices=1)
    arrays = prepare(inputs)
    aps = {n: nc.dram_tensor(n, a.shape, mybir.dt.from_np(a.dtype), kind="ExternalInput").ap()
           for n, a in arrays.items()}
    out = nc.dram_tensor("out", (1, SEQ, D), F32, kind="ExternalOutput").ap()
    program(nc, aps, out)
    r = run_bass_kernel_spmd(nc, [arrays], core_ids=[0])
    return r.results[0]["out"]
```

```python
import math
from contextlib import ExitStack
from itertools import chain

import numpy as np

import concourse.bass as bass
from concourse import mybir

F32 = mybir.dt.float32
F32R = mybir.dt.float32r
ALU = mybir.AluOpType
ACT = mybir.ActivationFunctionType
AX_X = mybir.AxisListType.X

P = 128
D = 1024
KT = D // P
SEQ = 256
QT = SEQ // P
DFF = 4 * D
META = 16
L2 = META + SEQ
ALPHA = (2 * 2) ** 0.25
NEG = -1e30
CLAMP = -1e29
REPLACED = -3e38
LAMBDA_INIT = 0.8 - 0.6 * math.exp(-0.3)
TOPK = 64
NUM_BUCKETS = 32
CMP_LEN, CMP_STRIDE = 32, 16
NCMP = (SEQ - CMP_LEN) // CMP_STRIDE + 1
SCALE = 64 ** -0.5
EXP_MAX = 80.0
SLOT = 2048
SLOTS = 4
ARENA = 28100
HL = KT * L2 + KT * SEQ
MLP_LAG = 2
SPLIT_SLOTS = 2
CW = SLOT // KT
KW = SLOT // D
LEVELS = 7


def t5_bucket(dist):
    n = np.maximum(dist, 0)
    exact = NUM_BUCKETS // 2
    nf = np.maximum(n, 1).astype(np.float32)
    large = exact + (np.log(nf / exact) / math.log(128 / exact) * (NUM_BUCKETS - exact)).astype(np.int32)
    return np.where(n < exact, n, np.minimum(large, NUM_BUCKETS - 1))


def bucket_rows():
    dist = 255 - np.arange(3 * P)
    hot = np.zeros((NUM_BUCKETS + 1, 3 * P), np.float32)
    hot[t5_bucket(dist), np.arange(3 * P)] = dist >= 0
    hot[NUM_BUCKETS] = dist < 0
    return hot


def square_masks():
    i, j = np.arange(P)[:, None], np.arange(P)[None, :]
    blocks = [i == j, i <= j, i >= j, i > j, i < j]
    for back in (0, 1):
        for level in range(LEVELS):
            b = 1 << level
            joined = (i // (2 * b) == j // (2 * b)) & (i // b % 2 == 0) & (j // b % 2 == 1)
            blocks.append(joined.T if back else joined)
    return np.concatenate(blocks, 1).astype(np.float32)


def rope_tables():
    grid, f = 64, 16
    t = np.arange(SEQ)
    freqs = np.float32(10000.0) ** (-np.arange(f, dtype=np.float32) / np.float32(f))
    ang = np.concatenate([(t // grid).astype(np.float32)[:, None] * freqs,
                          (t % grid).astype(np.float32)[:, None] * freqs], 1)
    ang = np.concatenate([ang, np.zeros((META, 2 * f), np.float32)], 0)
    return np.concatenate([np.cos(ang), np.sin(ang)], 1).astype(np.float32)


class Queues:

    def __init__(self, nc, ctx):
        self.nc, self.ctx = nc, ctx
        self.names = ("tensor", "vector", "scalar", "gpsimd", "sync")
        self.items = {n: [] for n in self.names}
        self.sem = {n: ctx.enter_context(nc.semaphore(f"done_{n}")) for n in self.names[:4]}
        self.count = dict.fromkeys(self.names, 0)
        self.stores = []

    def put(self, engine, emit, *after, loose=False):
        waits = [s for s in after if s is not None and not (engine == "tensor" and s[0] == "tensor")]
        if engine != "tensor" and not loose and self.count[engine]:
            waits.append((engine, self.sem[engine], self.count[engine]))
        self.count[engine] += 1
        self.items[engine].append((waits, emit, self.sem[engine], 1))
        return (engine, self.sem[engine], self.count[engine])

    def dma(self, emit, sem, total, *after, engine="sync"):
        waits = [s for s in after if s is not None]
        self.items[engine].append((waits, emit, sem, 16))
        return (sem.name, sem, total)

    def load(self, name, dst, src, *after, engine="sync"):
        sem = self.ctx.enter_context(self.nc.semaphore(f"in_{name}"))
        return self.dma(lambda e: e.dma_start(dst, src), sem, 16, *after, engine=engine)

    def emit(self, engine, eng):
        seen = {}
        for waits, emit, sem, by in self.items[engine]:
            for name, s, value in waits:
                if seen.get(name, 0) < value:
                    eng.wait_ge(s, value)
                    seen[name] = value
            emit(eng).then_inc(sem, by)


class Bank:
    def __init__(self, tensor):
        self.t, self.after = tensor, []


class Banks:

    def __init__(self, nc, ctx):
        self.free = [Bank(ctx.enter_context(nc.psum_tensor(f"bank{i}", [P, 512], F32))) for i in range(8)]

    def take(self):
        return self.free.pop(0)

    def give(self, bank, *readers):
        bank.after = list(readers)
        self.free.append(bank)


class Ring:

    def __init__(self, q, nc, ctx):
        self.q = q
        self.slots = [ctx.enter_context(nc.sbuf_tensor(f"ring{i}", [P, SLOT], F32)) for i in range(SLOTS)]
        self.sems = [ctx.enter_context(nc.semaphore(f"ring_in{i}")) for i in range(SLOTS)]
        self.uses = [0] * SLOTS
        self.reader = [None] * SLOTS
        self.n = 0

    def load(self, src):
        s = self.n % SLOTS
        self.n += 1
        view = shaped(self.slots[s], src.shape)
        self.uses[s] += 1
        assert self.uses[s] == 1 or self.reader[s] is not None
        landed = self.q.dma(lambda e: e.dma_start(view, src), self.sems[s], 16 * self.uses[s], self.reader[s])
        self.reader[s] = None
        return view, landed, s

    def done(self, slot, reader):
        self.reader[slot] = reader

    def lend(self):
        s = self.n % SLOTS
        self.n += 1
        return self.slots[s], s


class SplitWeights:

    def __init__(self, q, ring, nc, ctx, srcs):
        self.q, self.ring, self.srcs = q, ring, srcs
        self.highs = [ctx.enter_context(nc.sbuf_tensor(f"high{i}", [P, SLOT], F32R)) for i in range(SPLIT_SLOTS)]
        self.lows = [ctx.enter_context(nc.sbuf_tensor(f"low{i}", [P, SLOT], F32R)) for i in range(SPLIT_SLOTS)]
        self.reader = [None] * SPLIT_SLOTS
        self.queued = []
        self.n = self.n_done = 0

    def ahead(self, engine="vector"):
        if self.n == len(self.srcs) or self.n - self.n_done == SPLIT_SLOTS:
            return
        src, s = self.srcs[self.n], self.n % SPLIT_SLOTS
        assert self.n < SPLIT_SLOTS or self.reader[s] is not None
        raw, landed, slot = self.ring.load(src)
        high, low = shaped(self.highs[s], src.shape), shaped(self.lows[s], src.shape)
        rounded = self.q.put("scalar", lambda e: e.activation(high, raw, ACT.Copy), landed, self.reader[s])
        ready = self.q.put(engine, lambda e: e.tensor_tensor(low, raw, high.bitcast(F32), ALU.subtract), rounded)
        self.ring.done(slot, ready)
        self.reader[s] = None
        self.queued.append(((high, low), ready, s))
        self.n += 1

    def take(self):
        self.ahead()
        return self.queued.pop(0)

    def done(self, slot, reader):
        self.reader[slot] = reader
        self.n_done += 1


def shaped(tensor, shape):
    view = tensor[0:shape[0], 0:int(np.prod(shape[1:]))]
    return view.rearrange("p (a b) -> p a b", a=shape[1]) if len(shape) == 3 else view


class Arena:

    def __init__(self, nc, ctx, cols):
        self.t = ctx.enter_context(nc.sbuf_tensor("arena", [P, cols], F32))
        self.cols, self.at, self.top = cols, 0, 0

    def over(self, start, cols):
        a = object.__new__(Arena)
        a.t, a.cols, a.at, a.top = self.t, start + cols, start, 0
        return a

    def take(self, *shape, rows=P):
        n = int(np.prod(shape))
        assert self.at + n <= self.cols, f"arena: {self.at} + {n} of {self.cols}"
        a = self.t[0:rows, self.at:self.at + n]
        self.at += n
        self.top = max(self.top, self.at)
        if len(shape) == 2:
            return a.rearrange("p (a b) -> p a b", a=shape[0])
        if len(shape) == 3:
            return a.rearrange("p (a b c) -> p a b c", a=shape[0], b=shape[1])
        return a


class HiLo:

    def __init__(self, nc, ctx):
        self.h = ctx.enter_context(nc.sbuf_tensor("act_high", [P, HL], F32R))
        self.l = ctx.enter_context(nc.sbuf_tensor("act_low", [P, HL], F32R))

    def at(self, start, tiles, width):
        n = tiles * width
        assert start + n <= HL
        return tuple(t[:, start:start + n].rearrange("p (a b) -> p a b", a=tiles) for t in (self.h, self.l))


def program(nc, I, out):
    ctx = ExitStack()
    with ctx:
        q = Queues(nc, ctx)
        banks = Banks(nc, ctx)
        ring = Ring(q, nc, ctx)
        ar = Arena(nc, ctx, ARENA)
        hi_lo = HiLo(nc, ctx)

        def PE(emit, *after):
            return q.put("tensor", emit, *after)

        def V(emit, *after, **k):
            return q.put("vector", emit, *after, **k)

        def S(emit, *after, **k):
            return q.put("scalar", emit, *after, **k)

        def G(emit, *after, **k):
            return q.put("gpsimd", emit, *after, **k)

        def mm(out_, lhsT, rhs, *after, start=True, stop=True):
            return PE(lambda e: e.matmul(out_, lhsT, rhs, start=start, stop=stop), *after)

        def copy(engine, dst, src, *after, **k):
            if engine == "scalar":
                return S(lambda e: e.activation(dst, src, ACT.Copy), *after, **k)
            return q.put(engine, lambda e: e.tensor_copy(dst, src), *after, **k)

        def tt(engine, dst, a, b, op, *after, **k):
            return q.put(engine, lambda e: e.tensor_tensor(dst, a, b, op), *after, **k)

        def ts(engine, dst, a, s1, s2, op0, op1, *after, **k):
            return q.put(engine, lambda e: e.tensor_scalar(dst, a, s1, s2, op0, op1) if s2 is not None
                         else e.tensor_scalar(dst, a, s1, None, op0), *after, **k)

        def stt(dst, a, s, b, op0, op1, *after, **k):
            return V(lambda e: e.scalar_tensor_tensor(out=dst, in0=a, scalar=s, in1=b, op0=op0, op1=op1),
                     *after, **k)

        def act(dst, src, func, *after, bias=None, scale=1.0, accum=None, **k):
            kw = {"scale": scale}
            if bias is not None:
                kw["bias"] = bias
            if accum is not None:
                kw["accum_out"] = accum
            return S(lambda e: e.activation(dst, src, func, **kw), *after, **k)

        def memset(engine, dst, value, *after):
            return q.put(engine, lambda e: e.memset(dst, value), *after)

        def turned(out_, in_, ident_, *after):
            return PE(lambda e: e.transpose(out_, in_, ident_), *after)

        def recip(dst, src, *after, **k):
            return V(lambda e: e.reciprocal(dst, src), *after, **k)

        def reduce_(dst, src, op, *after, negate=False, **k):
            return V(lambda e: e.tensor_reduce(dst, src, AX_X, op, negate=True) if negate
                     else e.tensor_reduce(dst, src, AX_X, op), *after, **k)

        def small(name, dst, src, *after):
            return q.load(name, dst, src, *after, engine="gpsimd")

        ident = ar.take(P)
        in_ident = q.load("ident", ident, I["square_masks"][:, 0:P])
        c_rows = ar.take(P, rows=KT)
        in_c = q.load("c", c_rows, I["c"].rearrange("a (k p) -> (a k) p", p=P))
        ones = ar.take(P)
        m_ones = memset("vector", ones, 1.0)
        eps6 = ar.take(1)
        m_eps = memset("vector", eps6, 1e-6)
        hot = ar.take(3 * P, rows=NUM_BUCKETS + 1)
        in_hot = small("hot", hot, I["bucket_rows"][:, :])
        tab = ar.take(16, rows=NUM_BUCKETS + 1)
        in_tab = small("tab", tab[0:NUM_BUCKETS, :], I["rel_bias"][:, :])
        m_tab = memset("vector", tab[NUM_BUCKETS:NUM_BUCKETS + 1, :], NEG)

        rows_t = [ar.take(P, rows=P) for _ in range(3)]
        n_rows, in_rows, col_at = [0, 0, 0], [[], [], []], {}

        def as_rows(which, name, src, n):
            r0 = n_rows[which]
            in_rows[which].append(small(name, rows_t[which][r0:r0 + n, :], src))
            col_at[name] = (which, r0)
            n_rows[which] += n

        as_rows(0, "ada_b", I["ada_b"].rearrange("l (k p) -> (l k) p", p=P), 96)
        as_rows(1, "ln_g", I["ln_g"].rearrange("l s (k p) -> (l s k) p", p=P), 4 * KT)
        as_rows(1, "ln_b", I["ln_b"].rearrange("l s (k p) -> (l s k) p", p=P), 4 * KT)
        as_rows(1, "mix_pre", I["norm_mix_pre_2"].rearrange("a (k p) -> (a k) p", p=P), KT)
        as_rows(1, "mlp_pre", I["norm_mlp_pre_2"].rearrange("a (k p) -> (a k) p", p=P), KT)
        as_rows(1, "subln", I["diff_subln"], 1)
        as_rows(1, "dn_norm", I["dn_out_norm_2"], 1)
        as_rows(2, "pe_k", I["nsa_pe_k"].rearrange("a (l j) d -> (a l) (j d)", j=2), 16)
        as_rows(2, "pe_v", I["nsa_pe_v"].rearrange("a (l j) d -> (a l) (j d)", j=2), 16)
        as_rows(2, "conv", I["conv_w_2"].rearrange("a w (k p) -> (a w k) p", p=P), 60)
        cols = ar.take(3, 96)

        def transpose_rows(which):
            n = n_rows[which]
            b = banks.take()
            t = turned(b.t[:, 0:n], rows_t[which][0:n, :], ident[0:n, 0:n], in_ident, *in_rows[which], *b.after)
            c = copy("scalar", cols[:, which, 0:n], b.t[:, 0:n], t)
            banks.give(b, c)
            return c

        def col(name, i=0, n=1):
            which, r0 = col_at[name]
            return cols[:, which, r0 + i:r0 + i + n]

        c_act, c_exp = ar.take(KT), ar.take(KT)
        b = banks.take()
        t = turned(b.t[:, 0:KT], c_rows, ident[0:KT, 0:KT], in_ident, in_c)
        v1 = copy("vector", c_act, b.t[:, 0:KT], t)
        banks.give(b, v1)
        v1 = ts("vector", c_exp, c_act, -EXP_MAX, None, ALU.max, None)
        s1 = act(c_exp, c_exp, ACT.Exp, v1, scale=-1.0)
        ts("vector", c_exp, c_exp, 1.0, None, ALU.add, None, s1)
        recip(c_exp, c_exp)
        t_cact = tt("vector", c_act, c_act, c_exp, ALU.mult)

        x_tok = ar.take(QT, D)
        in_x = [q.load(f"x{t}", x_tok[:, t, :], I["x"][0, t * P:(t + 1) * P, :], engine="gpsimd") for t in range(QT)]
        hH, hL = hi_lo.at(0, KT, SEQ)
        oH, oL = hi_lo.at(KT * L2, KT, SEQ)
        after_cols = ar.at
        spare_at = ar.at
        n_tok = ar.take(QT, D)
        y_tmp = ar.take(QT, D)
        hT = ar.take(KT, SEQ)
        bias = ar.take(16, SEQ)
        ln_at = ar.at
        ln_rows = ar.take(2, D)
        gate_rows = ar.take(2, D)
        ada_cols = ar.take(4, KT)
        mod_cols = ar.take(2, KT)
        ada_acc = ar.take(2, 512)
        stats = ar.take(QT, 24)
        relu_at = ar.at
        relu_tmp = ar.take(2, 512)
        phase_base = ar.at

        acc_reader = [(), ()]
        ada_n = [0]
        gate_sem = [ctx.enter_context(nc.semaphore(f"gate_b_in{i}")) for i in range(2)]
        gate_uses = [0, 0]
        gate_reader = [(), ()]
        col_reader = [None] * 4
        t_gate = [None, None]
        t_adac = [None] * 4
        pending = []

        def ada_start(layer, j):
            for _ in ada_halves(layer, j):
                pass

        def ada_halves(layer, j):
            s = ada_n[0] % 2
            ada_n[0] += 1
            acc = ada_acc[:, s, :]
            w_l = I["ada_w"][layer].rearrange("(k p) n -> p k n", p=P)
            for kc in range(2):
                w, landed, slot = ring.load(w_l[:, 4 * kc:4 * kc + 4, j * 512:(j + 1) * 512])
                for k in range(4):
                    c_ = c_act[:, 4 * kc + k:4 * kc + k + 1]
                    if kc == k == 0:
                        v = ts("vector", acc, w[:, k, :], c_, None, ALU.mult, None, landed, t_cact, *acc_reader[s])
                    else:
                        v = stt(acc, w[:, k, :], c_, acc, ALU.mult, ALU.add, landed)
                ring.done(slot, v)
                if kc == 0:
                    yield
            part, half = j // 2, j % 2
            b_in = None
            if part in (2, 5):
                g = part // 3
                gate_uses[g] += 1
                dst = gate_rows[:, g, half * 512:(half + 1) * 512]
                src = I["ada_b"][layer, j * 512:(j + 1) * 512].partition_broadcast(P)
                if half == 0:
                    dst, src = gate_rows[:, g, :], I["ada_b"][layer, j * 512:(j + 2) * 512].partition_broadcast(P)
                    gate_in[g] = q.dma(lambda e: e.dma_start(dst, src), gate_sem[g], 16 * ((gate_uses[g] + 1) // 2),
                                       *gate_reader[g])
                b_in = gate_in[g]
            pending.append((layer, j, s, v, b_in))

        gate_in = [None, None]

        def ada_finish():
            layer, j, s, v, b_in = pending.pop(0)
            part, half = j // 2, j % 2
            acc = ada_acc[:, s, :]
            b = banks.take()
            if part in (2, 5):
                g = part // 3
                m = mm(b.t[:, :], ones, acc, v, m_ones, *b.after)
                rows = gate_rows[:, g, half * 512:(half + 1) * 512]
                c = t_gate[g] = stt(rows, b.t[:, :], 1.0, rows, ALU.add, ALU.add, m, b_in)
            else:
                for i in range(4):
                    m = turned(b.t[:, i * P:(i + 1) * P], acc[:, i * P:(i + 1) * P], ident, v, in_ident, *b.after)
                which = {0: 0, 1: 1, 3: 2, 4: 3}[part]
                dst = ada_cols[:, which, half * 4:half * 4 + 4]
                c = reduce_(dst, b.t[:, :].rearrange("p (a b) -> p a b", a=4), ALU.add, m, col_reader[which])
                t_adac[which] = tt("vector", dst, dst, col("ada_b", layer * 48 + j * 4, 4), ALU.add, t_cols)
            banks.give(b, c)
            acc_reader[s] = (m,)

        def feature_product(w, c0, m, src, toks, out_, *after):
            n = w.shape[1]
            for k in range(n):
                last = mm(out_, w[:, k, c0:c0 + m], src[:, k, toks], *(after if k == 0 else ()),
                          start=k == 0, stop=k == n - 1)
            return last

        def token_product(w, c0, n_cols, src, toks, out_, *after):
            n = w.shape[1]
            for k in range(n):
                last = mm(out_, src[:, k, toks], w[:, k, c0:c0 + n_cols], *(after if k == 0 else ()),
                          start=k == 0, stop=k == n - 1)
            return last

        def split_mm(out_, a, b_, *after, start, stop):
            (ah, al), (bh, bl) = a, b_
            mm(out_, ah, bh, *after, start=start, stop=False)
            mm(out_, ah, bl, start=False, stop=False)
            return mm(out_, al, bh, start=False, stop=stop)

        def feature_product3(w, c0, src, toks, out_, *after):
            for k in range(KT):
                last = split_mm(out_, (w[0][:, k, c0:c0 + P], w[1][:, k, c0:c0 + P]),
                                (src[0][:, k, toks], src[1][:, k, toks]), *(after if k == 0 else ()),
                                start=k == 0, stop=k == KT - 1)
            return last

        def token_product3(w, n_cols, src, toks, out_, *after):
            for k in range(KT):
                last = split_mm(out_, (src[0][:, k, toks], src[1][:, k, toks]),
                                (w[0][:, k, 0:n_cols], w[1][:, k, 0:n_cols]), *(after if k == 0 else ()),
                                start=k == 0, stop=k == KT - 1)
            return last

        def split_into(high, low, src, *after, scale=None):
            h = act(high, src, ACT.Copy, *after, **({} if scale is None else {"scale": scale}))
            if scale is None:
                return tt("vector", low, src, high.bitcast(F32), ALU.subtract, h)
            return stt(low, src, scale, high.bitcast(F32), ALU.mult, ALU.subtract, h)

        def rsqrt_col(dst, var, tmp, eps, *after):
            ts("vector", tmp, var, eps, None, ALU.add, None, *after)
            a = recip(dst, tmp)
            s = act(dst, dst, ACT.Sqrt, a)
            tt("vector", var, dst, dst, ALU.mult, s)
            tt("vector", var, var, tmp, ALU.mult)
            ts("vector", var, var, -0.5, 1.5, ALU.mult, ALU.add)
            return tt("vector", dst, dst, var, ALU.mult)

        def to_features(src_tok, t_src, dst, halves, scale_cols, shift_cols, t_coef, t_free, at, toks=P):
            done = []
            for k0 in range(0, KT, 4):
                b = banks.take()
                for k in range(k0, k0 + 4):
                    m = turned(b.t[:, (k - k0) * P:(k - k0) * P + toks], src_tok[:, k * P:(k + 1) * P],
                               ident[0:toks, 0:toks], t_src[k0 // 4], in_ident, *b.after)
                for k in range(k0, k0 + 4):
                    o, i_ = dst[:, k, at:at + toks], b.t[:, (k - k0) * P:(k - k0) * P + toks]
                    free = (t_coef, *t_free)
                    if k0 == 0:
                        kw = {"bias": shift_cols[:, k:k + 1]} if shift_cols is not None else {}
                        c = act(o, i_, ACT.Identity if kw else ACT.Copy, m, *free, scale=scale_cols[:, k:k + 1],
                                loose=k > k0, **kw)
                    elif shift_cols is None:
                        c = ts("vector", o, i_, scale_cols[:, k:k + 1], None, ALU.mult, None, m, *free, loose=k > k0)
                    else:
                        c = ts("vector", o, i_, scale_cols[:, k:k + 1], shift_cols[:, k:k + 1], ALU.mult, ALU.add,
                               m, *free, loose=k > k0)
                banks.give(b, c)
                grp = (slice(None), slice(k0, k0 + 4), slice(at, at + toks))
                done.append(split_into(halves[0][grp], halves[1][grp], dst[grp], c))
            return done

        def k_chunks(w, order=None):
            r = w.rearrange("(c k p) n -> c p k n", k=KW, p=P)
            return [r[i] for i in (range(r.shape[0]) if order is None else order)]

        def mlp_chunks(w1, w2):
            up, down = w1.rearrange("(k p) n -> p k n", p=P), k_chunks(w2)
            order = []
            for step in range(len(down) + MLP_LAG):
                if step < len(down):
                    order.append(up[:, :, step * CW:(step + 1) * CW])
                if step >= MLP_LAG:
                    order.append(down[step - MLP_LAG])
            return order

        w_ev = I["ev_w_in"][0].rearrange("(k p) n -> p k n", p=P)
        w_od = I["od_w_in"][0].rearrange("(k p) n -> p k n", p=P)
        w_in = I["w_in_2"][0].rearrange("(k p) n -> p k n", p=P)
        cols_of = lambda w, *starts: [w[:, :, c0:c0 + CW] for c0 in starts]
        weights = SplitWeights(q, ring, nc, ctx, [
            *cols_of(w_ev, 1944, 1944 + CW, 512), w_ev[:, :, 1024:1152], *cols_of(w_ev, 0, CW, 1304, 1304 + CW),
            *k_chunks(I["ev_w_out"][0]), *mlp_chunks(I["mlp_w1"][0], I["mlp_w2"][0]),
            *[c_ for i in range(4) for c_ in cols_of(w_od, i * CW, D + i * CW, 2 * D + i * CW)],
            *k_chunks(I["od_w_out"][0]), *mlp_chunks(I["mlp_w1"][1], I["mlp_w2"][1]),
            *cols_of(w_in, 512, 512 + CW, 0, CW, 1024, 1024 + CW, 2576, 2064, 2064 + CW, 1536, 1536 + CW),
            *k_chunks(I["w_out_2"][0], (2, 3, 0, 1)), *mlp_chunks(I["w_up_2"][0], I["w_down_2"][0])])

        ada_start(0, 0)
        t_cols = transpose_rows(0)
        for j in range(1, 4):
            ada_start(0, j)
            ada_finish()
        ada_finish()
        t_cols_ln = transpose_rows(1)
        t_cols_b = transpose_rows(2)

        def modulation(sub, ln=None):
            sh, sc = ada_cols[:, 2 * sub, :], ada_cols[:, 2 * sub + 1, :]
            after = (t_adac[2 * sub], t_adac[2 * sub + 1])
            a = ts("vector", mod_cols[:, 0, :], sc, 1.0, None, ALU.add, None, *after)
            if ln is None:
                a = copy("vector", mod_cols[:, 1, :], sh)
            else:
                tt("vector", mod_cols[:, 1, :], mod_cols[:, 0, :], col("ln_b", ln * KT, KT), ALU.mult, t_cols_ln)
                tt("vector", mod_cols[:, 1, :], mod_cols[:, 1, :], sh, ALU.add)
                a = tt("vector", mod_cols[:, 0, :], mod_cols[:, 0, :], col("ln_g", ln * KT, KT), ALU.mult)
            col_reader[2 * sub] = col_reader[2 * sub + 1] = a
            return a

        t_mod = modulation(0)
        t_h = []
        for t in range(QT):
            t_h += to_features(x_tok[:, t, :], (in_x[t], in_x[t]), hT, (hH, hL), mod_cols[:, 0, :], mod_cols[:, 1, :], t_mod, (), t * P)

        bias_row = y_tmp[0:16, 0, 0:3 * P]
        b = banks.take()
        m = mm(b.t[0:16, 0:3 * P], tab, hot, in_hot, in_tab, m_tab, *b.after)
        c = copy("scalar", bias_row, b.t[0:16, 0:3 * P], m)
        banks.give(b, c)
        rows_dram = nc.dram_tensor("bias_rows", (16, P, 3 * P), F32, kind="Internal").ap()
        rows_out = q.load("bias_rows", rows_dram, bias_row.unsqueeze(1).broadcast_to([16, P, 3 * P]), c, engine="gpsimd")
        shifted = bass.AP(tensor=rows_dram.tensor, offset=P - 1, ap=[[3 * P - 1, P], [P * 3 * P, 16], [1, SEQ]])
        t_bias = q.load("bias", bias, shifted, rows_out, engine="gpsimd")

        all_toks = slice(0, SEQ)
        tok_tile = lambda t: slice(t * P, (t + 1) * P)
        HALF = 64
        spare = ar.over(spare_at, 2 * QT * D)
        over_ln = ar.over(ln_at, 2 * D)
        over_relu = ar.over(relu_at, 2 * 512)
        qT = ar.take(4, SEQ)
        dqT = ar.take(4, SEQ)
        iq_raw_at = ar.at
        iqT = ar.take(4, SEQ)
        raw = ar.take(4, SEQ)
        qlatT = ar.over(iq_raw_at, 8 * SEQ).take(8, SEQ)
        k_sel = ar.take(2, SEQ)
        k_win = ar.take(2, SEQ)
        ikT = ar.take(SEQ)
        v_sw = ar.take(QT, SEQ)
        gates = ar.take(QT, 24)
        ckv = ar.take(QT, P)
        ckvT = ar.take(SEQ)
        iw = ar.take(QT, 8)
        x_split = (hH, hL)

        UC = 3 * P
        NB = 4
        zb = spare.take(NB, UC)
        pT = spare.take(NB, UC)
        ukT = spare.take(4, P)
        sq = spare.take(QT, P)
        over_z = ar.over(spare_at, 2 * NB * UC)
        blk = over_z.take(2, 16, 30)
        hid = over_z.take(2, SEQ, rows=30)
        isc = over_ln.take(UC)
        taken = over_ln.take(UC)
        relu = over_ln.take(2, UC)
        olat = over_ln.take(2, SEQ)

        def modulation_parts(layer, parts):
            for j in parts:
                yield from ada_halves(layer, j)
                yield
                if len(pending) > 1:
                    ada_finish()

        background = modulation_parts(0, range(4, 10))

        def feature_tiles(dst_of):
            w, ready, slot = weights.take()
            for i in range(w[0].shape[2] // P):
                b = banks.take()
                m = feature_product3(w, i * P, x_split, all_toks, b.t[:, 0:SEQ], ready, *t_h, *b.after)
                banks.give(b, dst_of(i, b, m))
            weights.done(slot, m)
            next(background, None)
            return m

        def pair_copy(dst, i0):
            def put(i, b, m):
                return copy("scalar", dst[:, i0 + i, :], b.t[:, 0:SEQ], m)
            return put

        kvn_row = ar.take(P)
        in_kvn = small("kvn", kvn_row, I["dsa_kv_norm"][0].partition_broadcast(P))
        w, landed, slot = ring.load(w_ev[:, :, 1816:1944])
        for _ in range(SPLIT_SLOTS):
            weights.ahead()
        b = banks.take()
        for t in range(QT):
            m = token_product(w, 0, P, hT, tok_tile(t), b.t[:, t * P:(t + 1) * P], landed, *t_h, *b.after)
        ring.done(slot, m)
        for t in range(QT):
            s0 = act(sq[:, t, :], b.t[:, t * P:(t + 1) * P], ACT.Square, m, accum=stats[:, 0, t:t + 1])
        ts("vector", stats[:, 0, 2:4], stats[:, 0, 0:2], 1.0 / P, None, ALU.mult, None, s0)
        rsqrt_col(stats[:, 0, 4:6], stats[:, 0, 2:4], stats[:, 0, 6:8], 1e-5)
        for t in range(QT):
            t_ckv = stt(ckv[:, t, :], b.t[:, t * P:(t + 1) * P], stats[:, 0, 4 + t:5 + t], kvn_row, ALU.mult, ALU.mult,
                        in_kvn)
        banks.give(b, t_ckv)
        for half in range(2):
            feature_tiles(pair_copy(iqT, 2 * half))
        t_iq = ("scalar", q.sem["scalar"], q.count["scalar"])
        w, landed, slot = ring.load(w_ev[:, :, 2456:2528])
        b = banks.take()
        m = feature_product(w, 0, HALF, hT, all_toks, b.t[0:HALF, 0:SEQ], landed, *b.after)
        copy("scalar", ikT[0:HALF, :], b.t[0:HALF, 0:SEQ], m)
        t_ik = copy("scalar", ikT[HALF:P, :], b.t[0:HALF, 0:SEQ], m)
        banks.give(b, t_ik)
        b = banks.take()
        for t in range(QT):
            m = token_product(w, HALF, 8, hT, tok_tile(t), b.t[:, t * 8:(t + 1) * 8], *b.after)
        t_iw = act(iw, b.t[:, 0:16].rearrange("p (t n) -> p t n", t=QT), ACT.Copy, m, scale=8 ** -0.5 * 64 ** -0.5)
        banks.give(b, t_iw)
        ring.done(slot, m)
        b = banks.take()
        for t in range(QT):
            m2 = turned(b.t[:, t * P:(t + 1) * P], ckv[:, t, :], ident, t_ckv, *b.after)
        t_ckvT = copy("scalar", ckvT, b.t[:, 0:SEQ], m2)
        banks.give(b, t_ckvT)

        top8 = ar.take(QT, 8)
        r_reader = [(), ()]

        def indexer_head(j):
            lo = j % 2 * HALF
            b = banks.take()
            mm(b.t[:, 0:P], iqT[lo:lo + HALF, j // 2, 0:P], ikT[lo:lo + HALF, 0:P], t_iq, t_ik, *b.after)
            m = mm(b.t[:, P:UC], iqT[lo:lo + HALF, j // 2, P:SEQ], ikT[lo:lo + HALF, :])
            r = relu[:, j % 2, :]
            s1 = act(r, b.t[:, 0:UC], ACT.Relu, m, *r_reader[j % 2], loose=True)
            banks.give(b, s1)
            for t, c in ((0, slice(0, P)), (1, slice(P, UC))):
                if j == 0:
                    v1 = ts("vector", isc[:, c], r[:, c], iw[:, t, 0:1], None, ALU.mult, None, s1, t_iw)
                else:
                    v1 = stt(isc[:, c], r[:, c], iw[:, t, j:j + 1], isc[:, c], ALU.mult, ALU.add, s1)
            r_reader[j % 2] = (v1,)
            return v1, m

        def raw_copy(i, b, m):
            for g in range(2):
                s_ = b.t[g * HALF:(g + 1) * HALF, :]
                copy("scalar", raw[0:HALF, 2 * i + g, :], s_[:, 0:SEQ], m)
                last = copy("scalar", raw[HALF:P, 2 * i + g, 0:SEQ - 1], s_[:, 1:SEQ], m)
            return last
        feature_tiles(raw_copy)
        t_raw = ("scalar", q.sem["scalar"], q.count["scalar"])
        for kv in range(2):
            pe = col("pe_v" if kv else "pe_k", 0, 16)
            for g in range(2):
                even = raw[:, 2 * kv + g, :].rearrange("p (n l j) -> p l n j", l=8, j=2)[:, :, :, 0]
                for hi in range(2):
                    t_blk = tt("vector", blk[:, kv, 8 * hi:8 * hi + 8, g * NCMP:(g + 1) * NCMP], even[:, :, hi:hi + NCMP],
                               pe[:, 8 * hi:8 * hi + 8].unsqueeze(2).broadcast_to([P, 8, NCMP]), ALU.add, t_raw, t_cols_b,
                               t_bias)
        for j in range(8):
            v1, t_index_mm = indexer_head(j)
        for c in (slice(0, P), slice(2 * P, UC)):
            t_isc = G(lambda e, c=c: e.affine_select(out=isc[:, c], in_=isc[:, c], compare_op=ALU.is_ge, fill=NEG,
                                                     base=0, pattern=[[-1, P]], channel_multiplier=1), v1)

        gel = ar.take(2, 2, 30)
        kcT = ar.take(2, NCMP)
        v_cmp = ar.take(2, HALF)
        hid_reader = []

        def compress_hidden(kv):
            b = banks.take()
            w1 = I["nsa_w1_v" if kv else "nsa_w1_k"][0].rearrange("(l p) n -> p l n", p=P)
            for lc in range(2):
                w, landed, slot = ring.load(w1[:, 8 * lc:8 * lc + 8, :])
                for l in range(8):
                    m = mm(b.t[0:30, 0:SEQ], blk[:, kv, 8 * lc + l, :], w[:, l, :], landed, t_blk, *b.after,
                           start=lc == l == 0, stop=lc == 1 and l == 7)
                ring.done(slot, m)
                next(background, None)
            h_, g_ = hid[0:30, 0, :], hid[0:30, 1, :]
            s1 = copy("scalar", h_, b.t[0:30, 0:SEQ], m, *hid_reader)
            banks.give(b, s1)
            tt("gpsimd", g_, h_, h_, ALU.mult, s1)
            ts("gpsimd", g_, g_, 0.044715, 1.0, ALU.mult, ALU.add)
            tt("gpsimd", g_, g_, h_, ALU.mult)
            g1 = ts("gpsimd", g_, g_, -EXP_MAX / 2, None, ALU.max, None)
            s1 = act(g_, g_, ACT.Exp, g1, scale=-2.0 * math.sqrt(2.0 / math.pi))
            ts("vector", g_, g_, 1.0, None, ALU.add, None, s1)
            recip(g_, g_)
            return g_, tt("vector", g_, g_, h_, ALU.mult)

        def turn_hidden(kv, g_, t_g):
            b = banks.take()
            for i in range(2):
                m = turned(b.t[:, i * 32:i * 32 + 30], g_[:, i * P:(i + 1) * P], ident[0:30, 0:30], t_g, *b.after)
            c = copy("scalar", gel[:, kv, :, :], b.t[:, 0:64].rearrange("p (a b) -> p a b", a=2)[:, :, 0:30], m)
            hid_reader[:] = [m]
            banks.give(b, c)
            return c

        def kw_copy(i, b, m):
            for g in range(2):
                for half in range(2):
                    last = copy("scalar", k_win[half * HALF:(half + 1) * HALF, g, :], b.t[g * HALF:(g + 1) * HALF, 0:SEQ], m)
            return last

        g_, t_g = compress_hidden(0)
        feature_tiles(kw_copy)
        t_kw = ("scalar", q.sem["scalar"], q.count["scalar"])
        turn_hidden(0, g_, t_g)
        g_, t_g = compress_hidden(1)
        w, landed, slot = ring.load(w_ev[:, :, 768:1024])
        b = banks.take()
        m = feature_product(w, 0, P, hT, all_toks, b.t[:, 0:SEQ], landed, *b.after)
        for g in range(2):
            for half in range(2):
                t_ks = copy("scalar", k_sel[half * HALF:(half + 1) * HALF, g, :], b.t[g * HALF:(g + 1) * HALF, 0:SEQ], m)
        banks.give(b, t_ks)
        b = banks.take()
        for t in range(QT):
            m = token_product(w, P, P, hT, tok_tile(t), b.t[:, t * P:(t + 1) * P], *b.after)
        t_vs = copy("scalar", v_sw[:, :, 0:P], b.t[:, 0:SEQ].rearrange("p (t n) -> p t n", t=QT), m)
        banks.give(b, t_vs)
        ring.done(slot, m)
        next(background, None)
        t_gel = turn_hidden(1, g_, t_g)
        w, landed, slot = ring.load(w_ev[:, :, 1152:1304])
        b = banks.take()
        for t in range(QT):
            m = token_product(w, 0, P + 24, hT, tok_tile(t), b.t[:, t * 160:t * 160 + P + 24], landed, *b.after)
        ring.done(slot, m)
        next(background, None)
        vg = b.t[:, 0:320].rearrange("p (t n) -> p t n", t=QT)
        t_vw = copy("scalar", v_sw[:, :, P:2 * P], vg[:, :, 0:P], m)
        s1 = copy("scalar", gates, vg[:, :, P:P + 24])
        banks.give(b, s1)
        g1 = ts("gpsimd", gates, gates, -EXP_MAX, None, ALU.max, None, s1)
        s1 = act(gates, gates, ACT.Exp, g1, scale=-1.0)
        ts("vector", gates, gates, 1.0, None, ALU.add, None, s1)
        t_gates = recip(gates, gates)
        for half in range(2):
            feature_tiles(pair_copy(qT, 2 * half))
        t_q = ("scalar", q.sem["scalar"], q.count["scalar"])
        w, landed, slot = ring.load(I["nsa_w2_k"][0].rearrange("(l p) n -> p l n", p=P))
        b = banks.take()
        for i in range(2):
            m = mm(b.t[0:HALF, 0:30], w[:, i, :], gel[:, 0, i, :], landed, t_gel, *b.after, start=i == 0, stop=i == 1)
        ring.done(slot, m)
        next(background, None)
        for half in range(2):
            t_kc = copy("scalar", kcT[half * HALF:(half + 1) * HALF, :, :], b.t[0:HALF, 0:30].rearrange("p (g n) -> p g n", g=2), m)
        banks.give(b, t_kc)
        w, landed, slot = ring.load(I["nsa_w2_v"][0].rearrange("(l p) n -> p l n", p=P))
        b = banks.take()
        for g in range(2):
            for i in range(2):
                m = mm(b.t[0:NCMP, g * HALF:(g + 1) * HALF], gel[:, 1, i, g * NCMP:(g + 1) * NCMP], w[:, i, :],
                       landed, *b.after, start=i == 0, stop=i == 1)
        ring.done(slot, m)
        next(background, None)
        for base in range(0, P, 32):
            t_vc = copy("scalar", v_cmp[base:base + NCMP, :, :], b.t[0:NCMP, 0:2 * HALF].rearrange("p (g n) -> p g n", g=2), m)
        banks.give(b, t_vc)

        selected = {}

        def select():
            copy("vector", taken, isc, t_isc)
            for r in range(TOPK // 8):
                for t, c in ((0, slice(0, P)), (1, slice(P, UC))):
                    V(lambda e, t=t, c=c: e.max(top8[:, t, :], taken[:, c]))
                    V(lambda e, t=t, c=c: e.match_replace(taken[:, c], top8[:, t, :], taken[:, c], REPLACED))
                yield
            ts("vector", taken, taken, -1e38, 1.0, ALU.is_le, ALU.subtract)
            selected["mask"] = ts("vector", taken, taken, -NEG, None, ALU.mult, None)

        over_sq = ar.over(spare_at + 2 * NB * UC + 4 * P, SEQ)
        pc = ar.take(QT * 8, 32)
        bc = over_sq.take(QT * 8, NCMP)
        pcT = ar.take(2, SEQ)
        m1 = memset("gpsimd", pc, 0.0)
        m2 = memset("gpsimd", bc, NEG, t_ckv)
        first = (2 * P - 1 - (P + CMP_LEN - 1)) // CMP_STRIDE + 1
        copy("gpsimd", bc[:, 0:8, 0:first], bias[:, 0:8, P + CMP_LEN - 1::CMP_STRIDE], m2, t_bias)
        t_bc = copy("gpsimd", bc[:, 8:16, :], bias[:, 0:8, CMP_LEN - 1::CMP_STRIDE][:, :, 0:NCMP])
        z = pc[:, :, 0:NCMP]
        for par in range(2):
            b = banks.take()
            lo = par * HALF
            for t in range(QT):
                for h2 in range(4):
                    o = (t * 4 + h2) * 32
                    m = mm(b.t[:, o:o + NCMP], qT[lo:lo + HALF, h2, t * P:(t + 1) * P],
                           kcT[lo:lo + HALF, h2 // 2, :], t_q, t_kc, *b.after)
            v1 = stt(pc[:, par::2, 0:NCMP], b.t[:, 0:SEQ].rearrange("p (a n) -> p a n", n=32)[:, :, 0:NCMP],
                     SCALE, bc[:, par::2, :], ALU.mult, ALU.add, m, m1, t_bc)
            banks.give(b, v1)
        cst = over_relu.take(4, QT * 8)

        w, landed, slot = ring.load(I["dsa_w_uk"][0].rearrange("r h d -> r (h d)"))
        b = banks.take()
        for i in range(4):
            m = turned(b.t[:, i * P:(i + 1) * P], w[:, i * P:(i + 1) * P], ident, landed, *b.after)
        t_uk = copy("scalar", ukT.rearrange("p a b -> p (a b)"), b.t[:, :], m)
        banks.give(b, t_uk)
        ring.done(slot, m)
        reduce_(cst[:, 0, :], z, ALU.max)
        ts("vector", cst[:, 0, :], cst[:, 0, :], CLAMP, None, ALU.max, None)
        v1 = tt("vector", z, z, cst[:, 0, :].unsqueeze(2).broadcast_to([P, QT * 8, NCMP]), ALU.subtract)
        s1 = act(z, z, ACT.Exp, v1)
        reduce_(cst[:, 1, :], z, ALU.add, s1)
        ts("vector", cst[:, 1, :], cst[:, 1, :], 1e-30, None, ALU.max, None)
        recip(cst[:, 2, :], cst[:, 1, :])
        tt("vector", cst[:, 3, :].rearrange("p (t h) -> p t h", t=QT), cst[:, 2, :].rearrange("p (t h) -> p t h", t=QT),
           gates[:, :, 0::3], ALU.mult)
        t_pc = tt("vector", z, z, cst[:, 3, :].unsqueeze(2).broadcast_to([P, QT * 8, NCMP]), ALU.mult)

        ust = over_relu.take(NB, 8)
        z_reader = [(hid_reader[0],)] * NB
        pT_reader = [(hid_reader[0],)] * NB
        unit_n = [0]

        def unit_logits(u, lhs_of, rhs_of, scale, bias_of, after):
            s = u["s"] = unit_n[0] % NB
            unit_n[0] += 1
            b = banks.take()
            mm(b.t[:, 0:P], lhs_of(0), rhs_of(slice(0, P)), *after, *b.after)
            m = mm(b.t[:, P:UC], lhs_of(1), rhs_of(slice(0, SEQ)))
            z, st = zb[:, s, :], ust[:, s, :]
            bias_ap, t_b = bias_of()
            stt(z[:, 0:P], b.t[:, 0:P], scale, bias_ap[0], ALU.mult, ALU.add, m, t_b, *z_reader[s])
            v = stt(z[:, P:UC], b.t[:, P:UC], scale, bias_ap[1], ALU.mult, ALU.add, loose=True)
            banks.give(b, v)
            reduce_(st[:, 0:1], z[:, 0:P], ALU.max, negate=True)
            v = reduce_(st[:, 1:2], z[:, P:UC], ALU.max, negate=True, loose=True)
            act(z[:, 0:P], z[:, 0:P], ACT.Exp, v, bias=st[:, 0:1], accum=st[:, 2:3], loose=True)
            u["e"] = act(z[:, P:UC], z[:, P:UC], ACT.Exp, bias=st[:, 1:2], accum=st[:, 3:4], loose=True)
            u["z"], u["st"], u["v"] = z, st, v

        def unit_coefficients(u, coef=None):
            u["v"] = recip(u["st"][:, 4:6], u["st"][:, 2:4], u["e"], loose=True)
            if coef is not None:
                u["v"] = coef(u["st"], u["v"])

        def unit_scale(u):
            z, st = u["z"], u["st"]
            ts("gpsimd", z[:, 0:P], z[:, 0:P], st[:, 4:5], None, ALU.mult, None, u["v"], loose=True)
            u["p"] = ts("gpsimd", z[:, P:UC], z[:, P:UC], st[:, 5:6], None, ALU.mult, None, loose=True)

        def unit_transpose(u):
            s, z = u["s"], u["z"]
            b = banks.take()
            turned(b.t[:, 0:P], z[:, 0:P], ident, u["p"], *b.after)
            turned(b.t[:, P:2 * P], z[:, P:2 * P], ident)
            m = turned(b.t[:, 2 * P:UC], z[:, 2 * P:UC], ident)
            z_reader[s] = (m,)
            c = copy("scalar", pT[:, s, :], b.t[:, 0:UC], m, *pT_reader[s], loose=True)
            banks.give(b, c)
            u["pT"] = c

        FILL = "fill"

        def run_units(units, order, fill=()):
            fill = iter(fill)
            for step in range(len(units) + len(order) - order.count(FILL) - 1):
                for stage in order:
                    if stage == FILL:
                        next(fill, None)
                    elif 0 <= step - stage < len(units):
                        units[step - stage][stage]()
            for _ in fill:
                pass

        bias_pair = lambda h: ((bias[:, h, P:SEQ], bias[:, h, :]), t_bias)
        head_bank = {}
        t_oT = [None] * KT

        def head_out(b, i, m):
            t_oT[i] = split_into(oH[:, i, :], oL[:, i, :], b.t[:, 0:SEQ], m)
            banks.give(b, t_oT[i])

        def latent_queries():
            for half in range(2):
                feature_tiles(pair_copy(dqT, 2 * half))
                yield
            t_dq = ("scalar", q.sem["scalar"], q.count["scalar"])
            selection = select()
            for h in range(8):
                next(selection)
                b = banks.take()
                lo = h % 2 * HALF
                m = mm(b.t[:, 0:SEQ], ukT[lo:lo + HALF, h // 2, :], dqT[lo:lo + HALF, h // 2, :], t_uk, t_dq, *b.after)
                t_ql[h] = copy("scalar", qlatT[:, h, :], b.t[:, 0:SEQ], m, t_index_mm, t_blk)
                banks.give(b, t_ql[h])
                yield
            for _ in selection:
                pass

        t_ql = [None] * 8

        def nsa_unit(h, branch):
            u = {}
            lo, g = h % 2 * HALF, h // 4
            kk, col0, ready = ((k_sel, 0, t_ks), (k_win, P, t_kw))[branch]

            def coef(st, v):
                return tt("vector", st[:, 4:6], st[:, 4:6], gates[:, :, 3 * h + 1 + branch], ALU.mult, t_gates)

            def logits():
                unit_logits(u, lambda t: qT[lo:lo + HALF, h // 2, t * P:(t + 1) * P],
                            lambda k: kk[lo:lo + HALF, g, k], SCALE, lambda: bias_pair(h), (t_q, ready))

            def probabilities():
                unit_coefficients(u, coef)
                unit_scale(u)

            def values():
                pair = h // 2
                if branch == 0:
                    if h % 2 == 0:
                        head_bank[pair] = banks.take()
                    b = head_bank[pair]
                    base = 32 * (h % 4)
                    mm(b.t[lo:lo + HALF, 0:SEQ], v_cmp[base:base + NCMP, g, :], pcT[base:base + NCMP, g, :], t_vc, t_pcT,
                       *b.after, stop=False)
                b = head_bank[pair]
                p_ = pT[:, u["s"], :]
                mm(b.t[lo:lo + HALF, 0:SEQ], v_sw[:, 0, col0 + g * HALF:col0 + (g + 1) * HALF], p_[:, 0:SEQ],
                   u["pT"], t_vs, t_vw, start=False, stop=False)
                m = mm(b.t[lo:lo + HALF, P:SEQ], v_sw[:, 1, col0 + g * HALF:col0 + (g + 1) * HALF], p_[:, SEQ:UC],
                       start=False, stop=branch == 1)
                pT_reader[u["s"]] = (m,)
                if h % 2 and branch:
                    head_out(b, pair, m)
            return [logits, probabilities, lambda: unit_transpose(u), values]

        b = banks.take()
        for g in range(2):
            for t in range(QT):
                m = turned(b.t[:, g * SEQ + t * P:g * SEQ + (t + 1) * P],
                           pc[:, t * 8 + g * 4:t * 8 + g * 4 + 4, :].rearrange("p a b -> p (a b)"), ident, t_pc, *b.after)
        t_pcT = copy("scalar", pcT.rearrange("p a b -> p (a b)"), b.t[:, :], m)
        banks.give(b, t_pcT)
        run_units([nsa_unit(h, br) for h in range(8) for br in range(2)], (0, 1, FILL, 2, 3),
                  chain(latent_queries(), background))

        w_uv = pc.rearrange("p a b -> p (a b)")
        in_uv = q.load("w_uv", w_uv, I["dsa_w_uv"][0].rearrange("r h d -> r (h d)"), t_pcT)
        dbias = over_relu.take(2, UC)
        db_reader = [(), ()]
        olat_reader = [(), ()]

        def dsa_unit(h):
            u = {}

            def logits():
                s = h % 2
                tt("gpsimd", dbias[:, s, 0:P], bias[:, 8 + h, P:SEQ], taken[:, 0:P], ALU.add, selected["mask"], *db_reader[s])
                g_ = tt("gpsimd", dbias[:, s, P:UC], bias[:, 8 + h, :], taken[:, P:UC], ALU.add)
                unit_logits(u, lambda t: qlatT[:, h, t * P:(t + 1) * P], lambda k: ckvT[:, k], SCALE,
                            lambda: ((dbias[:, s, 0:P], dbias[:, s, P:UC]), g_), (t_ql[h], t_ckvT))
                db_reader[s] = (u["v"],)

            def probabilities():
                unit_coefficients(u)
                unit_scale(u)

            def values():
                s = h % 2
                b = banks.take()
                p_ = pT[:, u["s"], :]
                mm(b.t[:, 0:SEQ], ckv[:, 0, :], p_[:, 0:SEQ], u["pT"], t_ckv, *b.after, stop=False)
                m = mm(b.t[:, P:SEQ], ckv[:, 1, :], p_[:, SEQ:UC], start=False)
                pT_reader[u["s"]] = (m,)
                c = copy("scalar", olat[:, s, :], b.t[:, 0:SEQ], m, *olat_reader[s])
                banks.give(b, c)
                u["olat"] = c

            def project():
                s, lo, pair = h % 2, h % 2 * HALF, h // 2
                if h % 2 == 0:
                    head_bank[pair] = banks.take()
                b = head_bank[pair]
                m = mm(b.t[lo:lo + HALF, 0:SEQ], w_uv[:, h * HALF:(h + 1) * HALF], olat[:, s, :], in_uv,
                       u["olat"], *b.after)
                olat_reader[s] = (m,)
                if h % 2:
                    head_out(b, 4 + pair, m)
            return [logits, probabilities, lambda: unit_transpose(u), values, project]

        ln_sem = [ctx.enter_context(nc.semaphore(f"ln_rows_in{i}")) for i in range(2)]
        ln_reader = [()]
        ln_uses = [0]
        x_state = {"x": (in_x[0], in_x[1])}

        class OutProduct:

            def __init__(self, n_chunks, eager=False):
                self.n, self.i, self.tail, self.eager = n_chunks, 0, [], eager
                self.ys = None
                self.m = [None] * QT

            def multiply(self, chunk, src, t, first, last):
                w, w_ready, _ = chunk
                for kk, (h_, l_, src_ready) in enumerate(src):
                    for half in range(2):
                        b = self.ys[t][half]
                        cs = slice(half * 512, (half + 1) * 512)
                        self.m[t] = split_mm(
                            b.t[:, :], (h_[:, t * P:(t + 1) * P], l_[:, t * P:(t + 1) * P]),
                            (w[0][:, kk, cs], w[1][:, kk, cs]), w_ready, src_ready,
                            *(b.after if first and kk == 0 else ()),
                            start=first and kk == 0, stop=last and kk == KW - 1)

            def step(self, src):
                if self.ys is None:
                    self.ys = [[banks.take() for _ in range(2)] for _ in range(QT)]
                chunk = weights.take()
                i = self.i
                self.i += 1
                if i < self.n - 2:
                    for t in range(QT):
                        self.multiply(chunk, src, t, i == 0, False)
                    weights.done(chunk[2], self.m[QT - 1])
                    if self.eager:
                        weights.ahead()
                    return
                self.tail.append((chunk, src, i))
                if len(self.tail) == 2:
                    for t in range(QT):
                        for c_, src_, i_ in self.tail:
                            self.multiply(c_, src_, t, i_ == 0, i_ == self.n - 1)
                            if t == QT - 1:
                                weights.done(c_[2], self.m[t])

        head_halves = lambda i: [(oH[:, k, :], oL[:, k, :], t_oT[k]) for k in range(KW * i, KW * i + KW)]

        def out_steps(op, order):
            for i in order:
                while any(t_oT[k] is None for k in range(KW * i, KW * i + KW)):
                    yield
                op.step(head_halves(i))
                yield

        def residual_norm(op, sub, ln, next_mod):
            rows_in = []
            ln_uses[0] += 1
            for i, name in enumerate(("ln_g", "ln_b")):
                rows_in.append(q.dma(lambda e, i=i, name=name: e.dma_start(
                    ln_rows[:, i, :], I[name][ln // 2, ln % 2].partition_broadcast(P)), ln_sem[i],
                    16 * ln_uses[0], *ln_reader[0]))
            t_mod = next_mod() if next_mod else None
            done, xs, normed = [], [], []

            def statistics(t):
                y = y_tmp[:, t, :]
                for half in range(2):
                    b = op.ys[t][half]
                    v = tt("vector", y[:, half * 512:(half + 1) * 512], b.t[:, :], gate_rows[:, sub, half * 512:(half + 1) * 512],
                           ALU.mult, op.m[t], t_gate[sub], loose=True)
                    banks.give(b, v)
                gate_read[0] = v
                stt(y, x_tok[:, t, :], ALPHA, y, ALU.mult, ALU.add, x_state["x"][t])
                st = stats[:, t, :]
                for half in range(2):
                    V(lambda e, o=st[:, 6 * half:6 * half + 6], i_=y[:, half * 512:(half + 1) * 512]: e.bn_stats(o, i_),
                      loose=half > 0)
                V(lambda e, o=st[:, 12:14], i_=st[:, 0:12]: e.bn_aggr(o, i_))
                mean, var, tmp, rstd, shift = (st[:, 12 + i:13 + i] for i in range(5))
                rsqrt_col(rstd, var, tmp, 1e-5)
                v = stt(shift, mean, -1.0, rstd, ALU.mult, ALU.mult)
                normed.append((act(n_tok[:, t, 0:512], y[:, 0:512], ACT.Identity, v, scale=rstd, bias=shift),
                               ts("vector", n_tok[:, t, 512:D], y[:, 512:D], rstd, shift, ALU.mult, ALU.add)))

            def outputs(t):
                if next_mod:
                    done.extend(to_features(n_tok[:, t, :], normed[t], hT, (hH, hL), mod_cols[:, 0, :], mod_cols[:, 1, :],
                                            t_mod, (op.m[QT - 1],), t * P))
                free_engine = "gpsimd" if next_mod else "vector"
                tt(free_engine, x_tok[:, t, :], n_tok[:, t, :], ln_rows[:, 0, :], ALU.mult, *normed[t], *rows_in)
                xs.append(tt(free_engine, x_tok[:, t, :], x_tok[:, t, :], ln_rows[:, 1, :], ALU.add))

            gate_read = [None]
            statistics(0)
            for _ in range(SPLIT_SLOTS):
                weights.ahead("gpsimd")
            statistics(1)
            outputs(0)
            outputs(1)
            gate_reader[sub] = (gate_read[0],)
            ln_reader[0] = (xs[-1],)
            x_state["x"] = xs
            return done

        US = 4
        uH, uL = hi_lo.at(KT * L2, US * KW, SEQ)

        def mlp(t_src, between=None):
            n = DFF // CW
            op = OutProduct(n, eager=True)
            made, used = {}, {}
            for step in range(n + MLP_LAG):
                if step < n:
                    w, ready, slot = weights.take()
                    b = banks.take()
                    for i in range(KW):
                        m = feature_product3(w, i * P, (hH, hL), all_toks, b.t[:, i * SEQ:(i + 1) * SEQ], ready, *t_src, *b.after)
                    weights.done(slot, m)
                    weights.ahead()
                    r_ = relu_tmp[:, step % 2, :]
                    s1 = act(r_, b.t[:, :], ACT.Relu, m, made.get(step - 2))
                    banks.give(b, s1)
                    g1 = tt("gpsimd", r_, r_, r_, ALU.mult, s1)
                    s_ = step % US
                    grp = (slice(None), slice(s_ * KW, (s_ + 1) * KW))
                    made[step] = split_into(uH[grp], uL[grp], r_.rearrange("p (a b) -> p a b", a=KW), g1, used.get(step - US))
                if step >= MLP_LAG:
                    i = step - MLP_LAG
                    s_ = i % US
                    op.step([(uH[:, s_ * KW + k, :], uL[:, s_ * KW + k, :], made[i]) for k in range(KW)])
                    used[i] = op.m[QT - 1]
                if between is not None:
                    between(step)
            return op

        op = OutProduct(KT // KW)
        run_units([dsa_unit(h) for h in range(8)], (0, 1, FILL, 2, 3, 4),
                  out_steps(op, range(KT // KW)))
        ln_reader[0] = (t_oT[7],)
        while pending:
            ada_finish()
        t_h = residual_norm(op, 0, 0, lambda: modulation(1, 0))

        def ada_between(step):
            if pending:
                ada_finish()
            if 1 <= step <= 2:
                ada_start(0, 9 + step)
            elif 3 <= step <= 12:
                ada_start(1, step - 3)

        op = mlp(t_h, ada_between)
        t_h = residual_norm(op, 1, 1, lambda: modulation(0, 1))

        ar.at = phase_base
        spare = ar.over(spare_at, 2 * QT * D)
        x_done = x_state["x"]
        PAIRS = 3
        q2T = ar.take(2 * PAIRS, SEQ)
        k2T = ar.take(2 * PAIRS, SEQ)
        v2 = ar.take(2 * PAIRS, SEQ)
        zb = spare.take(NB, UC)
        pT = spare.take(NB, UC)
        ust = ar.take(NB, 8)
        o_tok = spare.take(2, 2 * SEQ)
        o_st = ar.take(2, 3, 4)
        lam = ar.take(4 * 64)
        lam_p = ar.take(2 * 64)
        lam_c = ar.take(4)
        m = op.m[QT - 1]
        z_reader, pT_reader = [(m, *x_done)] * NB, [(m, *x_done)] * NB
        in_lam = q.load("lam", lam, I["diff_lam"][0].rearrange("a d -> (a d)").partition_broadcast(P), m)
        l4 = lam.rearrange("p (a b d) -> p a b d", a=2, b=2)
        tt("vector", lam_p.rearrange("p (a d) -> p a d", a=2), l4[:, :, 0, :], l4[:, :, 1, :], ALU.mult, in_lam)
        v1 = reduce_(lam_c[:, 0:2], lam_p.rearrange("p (a d) -> p a d", a=2), ALU.add)
        s1 = act(lam_c[:, 0:2], lam_c[:, 0:2], ACT.Exp, v1)
        tt("vector", lam_c[:, 2:3], lam_c[:, 1:2], lam_c[:, 0:1], ALU.subtract, s1)
        t_lam = ts("vector", lam_c[:, 2:3], lam_c[:, 2:3], -LAMBDA_INIT, None, ALU.add, None)
        subln = ar.take(1)
        t_subln = ts("vector", subln, col("subln"), 1.0 - LAMBDA_INIT, None, ALU.mult, None)

        t_oT = [None] * KT
        pair_in, pair_read = {}, {}

        def pair_projection(i):
            s = i % PAIRS
            while i >= PAIRS and i - PAIRS not in pair_read:
                yield
            free = pair_read.get(i - PAIRS, ())
            for part, dst in ((0, q2T), (1, k2T)):
                w, ready, slot = weights.take()
                b = banks.take()
                for j in range(2):
                    m = feature_product3(w, j * P, (hH, hL), all_toks, b.t[:, j * SEQ:(j + 1) * SEQ], ready, *t_h, *b.after)
                weights.done(slot, m)
                t_qk = copy("scalar", dst[:, 2 * s:2 * s + 2, :], b.t[:, :].rearrange("p (a b) -> p a b", a=2), m, *free)
                banks.give(b, t_qk)
                yield
            w, ready, slot = weights.take()
            b = banks.take()
            for t in range(QT):
                m = token_product3(w, CW, (hH, hL), tok_tile(t), b.t[:, t * CW:(t + 1) * CW], ready, *b.after)
            weights.done(slot, m)
            t_v2 = copy("scalar", v2[:, 2 * s:2 * s + 2, :], b.t[:, :].rearrange("p (a b) -> p a b", a=2), m, *free)
            banks.give(b, t_v2)
            pair_in[i] = (t_qk, t_v2)
            yield

        def diff_unit(h):
            ua, ub = {}, {}
            i, tile = h // 2, 2 * (h // 2 % PAIRS) + h % 2

            def logits():
                for mp, u in ((0, ua), (1, ub)):
                    lo = mp * HALF
                    unit_logits(u, lambda t: q2T[lo:lo + HALF, tile, t * P:(t + 1) * P],
                                lambda k: k2T[lo:lo + HALF, tile, k], SCALE, lambda: bias_pair(2 * h + mp), (pair_in[i][0],))

            def probabilities():
                unit_coefficients(ua)
                act(ua["z"][:, 0:P], ua["z"][:, 0:P], ACT.Copy, ua["v"], scale=ua["st"][:, 4:5], loose=True)
                ua["p"] = act(ua["z"][:, P:UC], ua["z"][:, P:UC], ACT.Copy, scale=ua["st"][:, 5:6], loose=True)
                unit_coefficients(ub, lambda st, v: ts("vector", st[:, 4:6], st[:, 4:6], lam_c[:, 2:3], None, ALU.mult, None,
                                                       t_lam))
                stt(ua["z"][:, 0:P], ub["z"][:, 0:P], ub["st"][:, 4:5], ua["z"][:, 0:P], ALU.mult, ALU.add, ua["p"])
                v = stt(ua["z"][:, P:UC], ub["z"][:, P:UC], ub["st"][:, 5:6], ua["z"][:, P:UC], ALU.mult, ALU.add)
                ua["p"] = v
                z_reader[ub["s"]] = (v,)

            def values():
                p_ = pT[:, ua["s"], :]
                t_v2 = pair_in[i][1]
                vh = slice((h % 2) * P, (h % 2 + 1) * P)
                v0, v1_ = v2[:, 2 * (i % PAIRS), vh], v2[:, 2 * (i % PAIRS) + 1, vh]
                if h % 2 == 0:
                    pair_bank[i] = banks.take()
                b = pair_bank[i]
                o = b.t[:, h % 2 * SEQ:(h % 2 + 1) * SEQ]
                mm(o[:, 0:P], p_[:, 0:P], v0, ua["pT"], t_v2, *b.after)
                mm(o[:, P:SEQ], p_[:, P:SEQ], v0, stop=False)
                m = mm(o[:, P:SEQ], p_[:, SEQ:UC], v1_, start=False)
                pT_reader[ua["s"]] = (m,)
                if h % 2:
                    pair_read[i] = (m,)

            def pair_norm():
                b, st, s = pair_bank[i], o_st[:, i % 2], i % 2
                for j in range(4):
                    c = slice(j * P, (j + 1) * P)
                    s1 = act(o_tok[:, s, c], b.t[:, c], ACT.Square, *pair_read[i], *o_free[s], accum=st[:, 0, j:j + 1],
                             loose=j > 0)
                ts("vector", st[:, 0], st[:, 0], 1.0 / P, None, ALU.mult, None, s1)
                rsqrt_col(st[:, 1], st[:, 0], st[:, 2], 1e-5)
                v = tt("vector", o_tok[:, s].rearrange("p (a b) -> p a b", a=4), b.t[:, :].rearrange("p (a b) -> p a b", a=4),
                       st[:, 1].unsqueeze(2).broadcast_to([P, 4, P]), ALU.mult)
                banks.give(b, v)
                pair_normed[i] = v

            def pair_turn():
                s = i % 2
                b = banks.take()
                for j in range(4):
                    m = turned(b.t[:, j * P:(j + 1) * P], o_tok[:, s, j * P:(j + 1) * P], ident, pair_normed[i], *b.after)
                o_free[s] = (m,)
                c = split_into(oH[:, 2 * i:2 * i + 2, :], oL[:, 2 * i:2 * i + 2, :],
                               b.t[:, :].rearrange("p (a b) -> p a b", a=2), m, t_subln, scale=subln[:, 0:1])
                t_oT[2 * i] = t_oT[2 * i + 1] = c
                banks.give(b, c)
            nothing = lambda: None
            return [logits, probabilities, lambda: unit_transpose(ua), values, pair_norm if h % 2 else nothing,
                    pair_turn if h % 2 else nothing]

        pair_bank, pair_normed = {}, {}
        o_free = [x_done, x_done]
        op = OutProduct(KT // KW)

        def layer_two_fill():
            for i in range(1, 4):
                yield from pair_projection(i)
            yield from out_steps(op, range(KT // KW))

        for _ in pair_projection(0):
            pass
        run_units([diff_unit(h) for h in range(8)], (2, 0, FILL, 3, 1, 4, FILL, 5), layer_two_fill())
        t_h = residual_norm(op, 0, 2, lambda: modulation(1, 2))

        def last_gate(step):
            if pending:
                ada_finish()
            if 1 <= step <= 2:
                ada_start(1, 9 + step)

        op = mlp(t_h, last_gate)
        residual_norm(op, 1, 3, None)
        m = op.m[QT - 1]

        ar.at = after_cols
        TT_ROWS = (P, P, META)
        TOK_AT = (META, META + P, 0)
        masks = ar.take(4 + 2 * LEVELS, P)
        a_log_row, dtb_row = ar.take(8), ar.take(8)
        qk_norm_row = ar.take(2, 64)
        rope = ar.take(3, 64)
        cT = ar.take(12, L2)
        kv_tok = ar.take(3, 2, 512)
        z_tok = ar.take(QT, 512)
        av = ar.take(3, P)
        ba = ar.take(3, 16)
        o_acc = ar.take(QT, 512)
        st2 = ar.take(3, 24)
        ex_row = ar.take(8)
        aqk_at = ar.at
        aqk = ar.take(3, 10, 64)
        delta_at = ar.at
        n2 = ar.take(2, D)
        u2T = ar.take(KT, L2)
        conv = ar.take(12, L2 + 4)
        end_block_one = [m, *x_state["x"]]
        in_masks = q.load("masks", masks.rearrange("p a b -> p (a b)"), I["square_masks"][:, P:], *end_block_one)
        in_alog = q.load("alog", a_log_row, I["a_log_2"][0].rearrange("a b -> (a b)").partition_broadcast(P), *end_block_one)
        in_dtb = q.load("dtb", dtb_row, I["dt_bias_2"][0].rearrange("a b -> (a b)").partition_broadcast(P), *end_block_one)
        in_qn = q.load("qn", qk_norm_row[:, 0, :], I["q_norm_2"][0].partition_broadcast(P), *end_block_one)
        in_kn = q.load("kn", qk_norm_row[:, 1, :], I["k_norm_2"][0].partition_broadcast(P), *end_block_one)
        over_conv = ar.over(delta_at + 2 * D + KT * L2, 2 * D)
        meta_x, nm = over_conv.take(D, rows=META), over_conv.take(D, rows=META)
        in_meta = q.load("meta", meta_x, I["meta_tokens_2"][:, :], *end_block_one)
        in_rope = [q.load(f"rope{t}", rope[0:TT_ROWS[t], t, :], I["rope_tables"][t * P:t * P + TT_ROWS[t], :], *end_block_one)
                   for t in range(3)]
        uH, uL = hi_lo.at(0, KT, L2)

        def rms_rows(src, t_src, dst, rows, st, width, eps, *after):
            s1 = act(dst, src, ACT.Square, t_src, *after, accum=st[0:rows, 0:1])
            ts("vector", st[0:rows, 1:2], st[0:rows, 0:1], 1.0 / width, None, ALU.mult, None, s1)
            v = rsqrt_col(st[0:rows, 2:3], st[0:rows, 1:2], st[0:rows, 3:4], eps)
            return (act(dst[:, 0:width // 2], src[:, 0:width // 2], ACT.Copy, v, scale=st[0:rows, 2:3]),
                    ts("vector", dst[:, width // 2:], src[:, width // 2:], st[0:rows, 2:3], None, ALU.mult, None))

        t_u = []
        srcs, dsts = (x_tok[:, 0, :], x_tok[:, 1, :], meta_x), (n2[:, 0, :], n2[:, 1, :], nm)
        ss, rs, tmp_ = st2[:, 0, 0:3], st2[:, 1, 0:3], st2[:, 2, 0:3]
        m_ss = memset("vector", ss, 1.0, *end_block_one)
        for t in range(3):
            r = TT_ROWS[t]
            s1 = act(dsts[t], srcs[t], ACT.Square, m_ss, x_state["x"][t] if t < 2 else in_meta, *end_block_one,
                     accum=ss[0:r, t:t + 1])
        ts("vector", ss, ss, 1.0 / D, None, ALU.mult, None, s1)
        v = rsqrt_col(rs, ss, tmp_, 1e-6)
        normed = []
        for t in range(3):
            scale_ = rs[0:TT_ROWS[t], t:t + 1]
            normed.append((act(dsts[t][:, 0:512], srcs[t][:, 0:512], ACT.Copy, v, scale=scale_),
                           ts("vector", dsts[t][:, 512:], srcs[t][:, 512:], scale_, None, ALU.mult, None)))
        for t in range(3):
            t_u += to_features(dsts[t], normed[t], u2T, (uH, uL), col("mix_pre", 0, KT), None, t_cols_ln, (m,), TOK_AT[t],
                               TT_ROWS[t])

        every = slice(0, L2)
        memset("gpsimd", conv[:, :, 0:2], 0.0, *t_u)
        t_pad = memset("gpsimd", conv[:, :, L2 + 2:L2 + 4], 0.0)
        t_conv_in = [None] * 12

        def conv_projection(i0):
            w, ready, slot = weights.take()
            for i in range(2):
                b = banks.take()
                m = feature_product3(w, i * P, (uH, uL), every, b.t[:, 0:L2], ready, *t_u, *b.after)
                t_conv_in[i0 + i] = copy("scalar", conv[:, i0 + i, 2:L2 + 2], b.t[:, 0:L2], m)
                banks.give(b, t_conv_in[i0 + i])
            weights.done(slot, m)

        def conv_group(g4):
            for i in range(4 * g4, 4 * g4 + 4):
                tap = lambda j: col("conv", j * 12 + i)
                v = ts("vector", cT[:, i, :], conv[:, i, 0:L2], tap(0), None, ALU.mult, None, t_conv_in[i], t_pad, t_cols_b)
                for j in range(1, 5):
                    v = stt(cT[:, i, :], conv[:, i, j:j + L2], tap(j), cT[:, i, :], ALU.mult, ALU.add)
            grp = slice(4 * g4, 4 * g4 + 4)
            return act(cT[:, grp, :], cT[:, grp, :], ACT.Silu, v)

        def l2_group(g4, t_silu):
            for i in range(4 * g4, 4 * g4 + 4):
                g_ = tt("gpsimd", conv[:, i, 0:L2], cT[:, i, :], cT[:, i, :], ALU.mult, t_silu, *t_convs[g4])
                sq_t[i] = g_

        sq_t = [None] * 12
        t_convs = [()] * 3
        t_cT = [None] * 12

        def l2_finish(g4):
            for i in range(4 * g4, 4 * g4 + 4):
                b = banks.take()
                m1 = mm(b.t[:, 0:L2], ones, conv[:, i, 0:L2], sq_t[i], *b.after)
                s_ = act(conv[:, i, 0:L2], b.t[:, 0:L2], ACT.Ln, m1, m_eps, bias=eps6[:, 0:1])
                banks.give(b, s_)
            grp = slice(4 * g4, 4 * g4 + 4)
            s_ = act(conv[:, grp, 0:L2], conv[:, grp, 0:L2], ACT.Exp, scale=-0.5)
            if g4 == 0:
                v = stt(cT[:, grp, :], conv[:, grp, 0:L2], P ** -0.5, cT[:, grp, :], ALU.mult, ALU.mult, s_)
            else:
                v = tt("vector", cT[:, grp, :], conv[:, grp, 0:L2], cT[:, grp, :], ALU.mult, s_)
            for i in range(4 * g4, 4 * g4 + 4):
                t_cT[i] = v

        for g4 in (1, 0):
            for half in range(2):
                conv_projection(4 * g4 + 2 * half)
            l2_group(g4, conv_group(g4))
        w, landed, slot = ring.load(w_in[:, :, 2048:2064])
        b = banks.take()
        for t in range(3):
            r = TT_ROWS[t]
            m = token_product(w, 0, 16, u2T, slice(TOK_AT[t], TOK_AT[t] + r), b.t[0:r, t * 16:t * 16 + 16], landed, *b.after)
        ring.done(slot, m)
        memset("vector", ba[:, 2, :], 0.0)
        for t in range(3):
            r = TT_ROWS[t]
            t_ba = copy("vector", ba[0:r, t, :], b.t[0:r, t * 16:t * 16 + 16], m)
        banks.give(b, t_ba)
        for half in range(2):
            conv_projection(8 + 2 * half)
        w, ready, slot = weights.take()
        for t in range(3):
            r = TT_ROWS[t]
            b = banks.take()
            m = token_product3(w, CW, (uH, uL), slice(TOK_AT[t], TOK_AT[t] + P), b.t[:, 0:CW], ready, *b.after)
            copy("scalar", aqk[0:r, t, 8:10, :], b.t[0:r, 0:P].rearrange("p (h d) -> p h d", d=64), m)
            t_av = copy("scalar", av[0:r, t, :], b.t[0:r, P:CW])
            banks.give(b, t_av)
        weights.done(slot, m)
        for half in range(2):
            w, ready, slot = weights.take()
            b = banks.take()
            for t in range(QT):
                m = token_product3(w, CW, (uH, uL), slice(TOK_AT[t], TOK_AT[t] + P), b.t[:, t * CW:(t + 1) * CW],
                                   ready, *b.after)
            weights.done(slot, m)
            t_aq = copy("scalar", aqk[:, 0:2, 4 * half:4 * half + 4, :],
                        b.t[:, :].rearrange("p (t h d) -> p t h d", t=2, d=64), m)
            banks.give(b, t_aq)

        for half in range(2):
            w, ready, slot = weights.take()
            b = banks.take()
            for t in range(QT):
                m = token_product3(w, CW, (uH, uL), slice(TOK_AT[t], TOK_AT[t] + P), b.t[:, t * CW:(t + 1) * CW],
                                   ready, *b.after)
            weights.done(slot, m)
            t_z = act(z_tok[:, :, half * CW:(half + 1) * CW], b.t[:, :].rearrange("p (t n) -> p t n", t=2), ACT.Silu, m)
            banks.give(b, t_z)
        t_silu_v = conv_group(2)
        for i in range(8, 12):
            t_cT[i] = t_silu_v
        l2_finish(1)
        l2_finish(0)

        s1 = act(ex_row, a_log_row, ACT.Exp, in_alog)
        ts("vector", ex_row, ex_row, -1.0, None, ALU.mult, None, s1)
        b_, g_, tmp, tmp2 = ba[:, :, 0:8], ba[:, :, 8:16], st2[:, :, 8:16], st2[:, :, 16:24]
        v = ts("vector", tmp, b_, -EXP_MAX, None, ALU.max, None, t_ba)
        s1 = act(tmp, tmp, ACT.Exp, v, scale=-1.0)
        tt("vector", g_, g_, dtb_row.unsqueeze(1).broadcast_to([P, 3, 8]), ALU.add, in_dtb)
        ts("vector", tmp2, g_, -1.0, None, ALU.mult, None)
        v = tt("vector", tmp2, g_, tmp2, ALU.max)
        act(tmp2, tmp2, ACT.Exp, v, scale=-1.0)
        ts("vector", tmp, tmp, 1.0, None, ALU.add, None, s1)
        recip(b_, tmp)
        s1 = act(tmp2, tmp2, ACT.Ln, bias=ones[:, 0:1])
        stt(g_, g_, 0.0, tmp2, ALU.max, ALU.add, s1)
        t_bg = tt("vector", g_, g_, ex_row.unsqueeze(1).broadcast_to([P, 3, 8]), ALU.mult)

        for kv in (1, 0):
            for t in (2, 0, 1):
                r = TT_ROWS[t]
                b = banks.take()
                for h in range(4):
                    m = turned(b.t[0:r, h * P:(h + 1) * P], cT[:, 4 + 4 * kv + h, TOK_AT[t]:TOK_AT[t] + r], ident,
                               *(t_cT[8:] if kv else t_cT), *b.after)
                t_kv = copy("scalar", kv_tok[0:r, t, kv, :], b.t[0:r, :], m)
                banks.give(b, t_kv)

        ar.at = delta_at
        aT = ar.take(4, SEQ)
        akT = ar.take(2, L2)
        buf_at = ar.at
        rot = ar.take(10, 64)
        rst = ar.take(3, 10)
        sqk = ar.take(10, 64)
        after_rot = ar.at
        NA = 3
        over_aqk = ar.over(aqk_at, 3 * 640)
        za = over_aqk.take(NA, L2)
        over_rot = ar.over(buf_at, after_rot - buf_at)
        paT = over_rot.take(NA, 3 * P)
        ast = over_rot.take(NA, 4)
        ready_of = {}

        def rotate(t):
            r, h0 = TT_ROWS[t], 0 if t < 2 else 8
            x_ = aqk[0:r, t, h0:10, :]
            n = 10 - h0
            sq_ = sqk[0:r, h0:10, :]
            s0_, s1_, s2_ = (rst[0:r, i, h0:10] for i in range(3))
            tt("vector", sq_, x_, x_, ALU.mult, t_av, t_aq, t_kv)
            reduce_(s0_, sq_, ALU.add)
            ts("vector", s0_, s0_, 1.0 / 64, None, ALU.mult, None)
            rsqrt_col(s1_, s0_, s2_, 1e-6)
            tt("vector", x_, x_, s1_.unsqueeze(2).broadcast_to([r, n, 64]), ALU.mult)
            if t < 2:
                tt("vector", x_[:, 0:8, :], x_[:, 0:8, :],
                   qk_norm_row[0:r, 0:1, :].broadcast_to([r, 8, 64]), ALU.mult, in_qn)
            tt("vector", x_[:, n - 2:n, :], x_[:, n - 2:n, :],
               qk_norm_row[0:r, 1:2, :].broadcast_to([r, 2, 64]), ALU.mult, in_kn)
            for ax in range(2):
                lo_, hi_ = x_[:, :, 32 * ax:32 * ax + 16], x_[:, :, 32 * ax + 16:32 * ax + 32]
                cos = rope[0:r, t, 16 * ax:16 * ax + 16].unsqueeze(1).broadcast_to([r, n, 16])
                sin = rope[0:r, t, 32 + 16 * ax:48 + 16 * ax].unsqueeze(1).broadcast_to([r, n, 16])
                o_lo = rot[0:r, h0:10, 32 * ax:32 * ax + 16]
                o_hi = rot[0:r, h0:10, 32 * ax + 16:32 * ax + 32]
                tmp = sq_[:, :, 0:16]
                tt("vector", o_lo, lo_, cos, ALU.mult, in_rope[t], ready_of.get("turned"))
                tt("vector", tmp, hi_, sin, ALU.mult)
                tt("vector", o_lo, o_lo, tmp, ALU.subtract)
                tt("vector", o_hi, hi_, cos, ALU.mult)
                tt("vector", tmp, lo_, sin, ALU.mult)
                v = tt("vector", o_hi, o_hi, tmp, ALU.add)
            for _ in range(3):
                yield
            if t < 2:
                b = banks.take()
                for i in range(4):
                    m = turned(b.t[:, i * P:(i + 1) * P], rot[:, 2 * i:2 * i + 2, :].rearrange("p a b -> p (a b)"), ident,
                               v, *b.after)
                t_aT = copy("scalar", aT[:, :, t * P:(t + 1) * P], b.t[:, :].rearrange("p (a b) -> p a b", a=4), m)
                banks.give(b, t_aT)
                ready_of["aT"] = t_aT
            b = banks.take()
            m = turned(b.t[:, 0:r], rot[0:r, 8:10, :].rearrange("p a b -> p (a b)"), ident[0:r, 0:r], v, *b.after)
            for g in range(2):
                for half in range(2):
                    t_ak = copy("scalar", akT[half * HALF:(half + 1) * HALF, g, t * P:t * P + r], b.t[g * HALF:(g + 1) * HALF, 0:r], m)
            banks.give(b, t_ak)
            ready_of["turned"], ready_of["akT"] = m, t_ak
            yield

        za_reader, paT_reader = [None] * NA, [None] * NA
        a_n = [0]
        a_bank = {}
        t_oT = [None] * KT

        def axial_unit(h, t):
            u = {}
            lo, pair, g = h % 2 * HALF, h // 2, h // 4

            def logits():
                s = u["s"] = a_n[0] % NA
                a_n[0] += 1
                b = banks.take()
                m = mm(b.t[:, 0:L2], aT[lo:lo + HALF, pair, t * P:(t + 1) * P], akT[lo:lo + HALF, g, :], ready_of["aT"], ready_of["akT"],
                       *b.after)
                st = ast[:, s, :]
                reduce_(st[:, 0:1], b.t[:, 0:L2], ALU.max, m, ready_of["turned"], negate=True)
                v = ts("vector", st[:, 0:1], st[:, 0:1], SCALE, None, ALU.mult, None)
                a = act(za[:, s, :], b.t[:, 0:L2], ACT.Exp, v, za_reader[s], bias=st[:, 0:1], scale=SCALE,
                        accum=st[:, 1:2], loose=True)
                banks.give(b, a)
                v = recip(st[:, 2:3], st[:, 1:2], a)
                u["p"] = act(za[:, s, :], za[:, s, :], ACT.Copy, v, scale=st[:, 2:3])

            def turn():
                s = u["s"]
                b = banks.take()
                turned(b.t[:, 0:P], za[:, s, 0:P], ident, u["p"], *b.after)
                turned(b.t[:, P:2 * P], za[:, s, P:2 * P], ident)
                m = turned(b.t[0:META, 2 * P:3 * P], za[:, s, SEQ:L2], ident)
                za_reader[s] = m
                copy("scalar", paT[:, s, 0:SEQ], b.t[:, 0:SEQ], m, paT_reader[s], loose=True)
                u["pT"] = copy("scalar", paT[0:META, s, SEQ:3 * P], b.t[0:META, SEQ:3 * P])
                banks.give(b, u["pT"])

            def values():
                s = u["s"]
                if h % 2 == 0 and t == 0:
                    a_bank[pair] = banks.take()
                b = a_bank[pair]
                o = b.t[lo:lo + HALF, t * P:(t + 1) * P]
                for kt in range(3):
                    r = TT_ROWS[kt]
                    m = mm(o, av[0:r, kt, g * HALF:(g + 1) * HALF], paT[0:r, s, kt * P:(kt + 1) * P], u["pT"], t_av,
                           *b.after, start=kt == 0, stop=kt == 2)
                paT_reader[s] = m
                if h % 2 and t == 1:
                    head_out(b, 4 + pair, m)
            return [logits, turn, values]

        def axial_steps():
            for t in range(3):
                yield from rotate(t)
            units = [axial_unit(2 * pair + i, t) for pair in range(4) for t in range(QT) for i in range(2)]
            lags = (0, 1, 2)
            for step in range(len(units) + lags[-1]):
                for stage, lag in reversed(list(enumerate(lags))):
                    if 0 <= step - lag < len(units):
                        units[step - lag][stage]()
                        yield

        names = ("a", "qk", "aT", "lT", "x", "xT", "w", "bv", "bek", "kdec", "qdec", "s")
        lent = [ring.lend() for _ in range(2)]
        slot_buf = [s_[:, i * 512:(i + 1) * 512].rearrange("p (a b) -> p a b", a=4) for s_, _ in lent for i in range(4)]
        buf = [{n: ar.take(4, P) for n in names}, {n: slot_buf[i] if i < 8 else ar.take(4, P) for i, n in enumerate(names)}]
        dst_ = [ar.take(6, 4) for _ in range(2)]
        t_o = [None] * QT
        t_s = [None, None]

        def chunk(d, t, first):
            B, st = buf[d], dst_[d]
            C, at = TT_ROWS[t], TOK_AT[t]
            back = d if t < 2 else 0
            real = t < 2
            M1, strict = masks[0:C, back, 0:C], masks[0:C, 2 + back, 0:C]
            level = lambda l, back_: masks[0:C, 4 + LEVELS * back_ + l, 0:C]
            beta, g = ba[0:C, t, 4 * d:4 * d + 4], ba[0:C, t, 8 + 4 * d:12 + 4 * d]
            wide = lambda a: a.unsqueeze(1).broadcast_to([C, 4, C])
            per = lambda c: c.unsqueeze(2).broadcast_to([C, 4, P])
            v_ = lambda n, w_=C: B[n][0:C, :, 0:w_]
            gc, e_tot, e_gc, e_last, bg = (st[:, i, :] for i in range(5))
            cols_ = slice(at, at + C)

            b = banks.take()
            mm(b.t[0:C, 0:4], M1, g, t_bg, in_masks, t_kv, *b.after)
            m = mm(b.t[:, 4:8], ones[0:C, :], g)
            copy("scalar", gc[0:C], b.t[0:C, 0:4], m, t_s[d])
            act(e_last, b.t[:, 4:8], ACT.Exp)
            c = copy("scalar", e_tot[0:C], b.t[0:C, 4:8])
            banks.give(b, c)
            v = tt("vector", e_tot[0:C], e_tot[0:C], gc[0:C], ALU.subtract, c)
            act(e_tot[0:C], e_tot[0:C], ACT.Exp, v)
            s_ = act(e_gc[0:C], gc[0:C], ACT.Exp)
            v = tt("vector", bg[0:C], e_gc[0:C], beta, ALU.mult, s_)
            gw = copy("gpsimd", B["w"][0:C], per(g), t_bg, m, t_s[d])
            yield
            R = banks.take()
            for h in range(4):
                m = mm(R.t[0:P if real else C, h * P:h * P + C], B["w"][0:C, h, 0:P if real else C], M1, gw, *R.after)
            Rv = R.t[:, :].rearrange("p (h c) -> p h c", h=4)
            K = banks.take()
            for h in range(4):
                kT_ = cT[:, 4 + h, cols_]
                mk = mm(K.t[0:C, h * P:h * P + C], kT_, kT_, *t_cT, *K.after)
            for h in range(4):
                v = ts("vector", B["a"][0:C, h, 0:C], Rv[0:C, h, 0:C], gc[0:C, h:h + 1], 0.0, ALU.subtract, ALU.max, m)
                if real:
                    v = ts("vector", B["qk"][0:C, h, 0:C], Rv[0:C, h, 0:C], gc[0:C, h:h + 1], 0.0, ALU.subtract, ALU.min)
            if real:
                act(B["qdec"], Rv, ACT.Exp, v)
            s_ = act(v_("a"), v_("a"), ACT.Exp, v, scale=-1.0)
            banks.give(R, s_)
            yield
            v = tt("vector", v_("a"), v_("a"), wide(strict), ALU.mult, s_)
            for h in range(4):
                v = stt(B["a"][0:C, h, 0:C], K.t[0:C, h * P:h * P + C], beta[:, h:h + 1], B["a"][0:C, h, 0:C], ALU.mult, ALU.mult, mk)
            banks.give(K, v)
            b = banks.take()
            for h in range(4):
                m = turned(b.t[0:C, h * P:h * P + C], B["a"][0:C, h, 0:C], ident[0:C, 0:C], v, *b.after)
            c = copy("scalar", v_("aT"), b.t[0:C, :].rearrange("p (h c) -> p h c", h=4)[:, :, 0:C], m)
            banks.give(b, c)
            tt("gpsimd", v_("x"), v_("a"), wide(level(0, 1 - back)), ALU.mult, v)
            gx = tt("gpsimd", v_("xT"), v_("aT"), wide(level(0, back)), ALU.mult, c)
            tt("gpsimd", B["bv"][0:C], kv_tok[0:C, t, 1, :].rearrange("p (h c) -> p h c", h=4), per(beta), ALU.mult, t_kv)
            if real:
                act(B["qk"], B["qk"], ACT.Exp)
                tt("gpsimd", B["qdec"], B["qdec"], cT[:, 0:4, cols_], ALU.mult)
            yield
            idn = wide(ident[0:C, 0:C])
            tt("vector", v_("x"), idn, v_("x"), ALU.subtract, gx)
            v = tt("vector", v_("xT"), idn, v_("xT"), ALU.subtract)
            n_levels = LEVELS if real else 4
            joined = lambda l: v_("lT" if l % 2 else "a")
            join = lambda l, *after: tt("gpsimd", joined(l), v_("aT"), wide(level(l, back)), ALU.mult, *after)
            heads_of = lambda bank: bank.t[0:C, :].rearrange("p (h c) -> p h c", h=4)[:, :, 0:C]
            t_x = t_xT = v
            g_join = join(1, v)
            mw = None
            for l in range(1, n_levels):
                last = l == n_levels - 1
                b = banks.take()
                for h in range(4):
                    mw_next = mm(b.t[0:C, h * P:h * P + C], joined(l)[:, h, :], B["x"][0:C, h, 0:C], g_join, t_x, *b.after)
                c = copy("scalar", v_("w"), heads_of(b), mw_next)
                banks.give(b, c)
                if not last:
                    g_join = join(l + 1, mw)
                mw = mw_next
                if l == 1:
                    tt("gpsimd", B["bek"][0:C], kv_tok[0:C, t, 0, :].rearrange("p (h c) -> p h c", h=4), per(bg[0:C]), ALU.mult, t_kv)
                    gk = tt("gpsimd", B["kdec"][0:C], kv_tok[0:C, t, 0, :].rearrange("p (h c) -> p h c", h=4), per(e_tot[0:C]), ALU.mult)
                yield
                if not last:
                    b = banks.take()
                    for h in range(4):
                        m = mm(b.t[0:C, h * P:h * P + C], B["xT"][0:C, h, 0:C], B["w"][0:C, h, 0:C], c, t_xT, *b.after)
                    t_x = tt("vector", v_("x"), v_("x"), heads_of(b), ALU.subtract, m)
                    banks.give(b, t_x)
                b = banks.take()
                for h in range(4):
                    m = mm(b.t[0:C, h * P:h * P + C], B["w"][0:C, h, 0:C], B["xT"][0:C, h, 0:C], c, t_xT, *b.after)
                v = t_xT = tt("vector", v_("xT"), v_("xT"), heads_of(b), ALU.subtract, m)
                banks.give(b, t_xT)
                yield
            if real:
                b = banks.take()
                for h in range(4):
                    m = mm(b.t[:, h * P:(h + 1) * P], cT[:, 4 + h, cols_], cT[:, h, cols_], *b.after)
                vq = tt("vector", B["qk"], B["qk"], wide(M1), ALU.mult)
                vq = tt("vector", B["qk"], B["qk"], b.t[:, :].rearrange("p (h c) -> p h c", h=4), ALU.mult, m)
                banks.give(b, vq)
                b = banks.take()
                for h in range(4):
                    m = mm(b.t[:, h * P:(h + 1) * P], B["bek"][:, h, :], B["xT"][:, h, :], gk, v, *b.after)
                nw = act(B["x"], b.t[:, :].rearrange("p (h c) -> p h c", h=4), ACT.Copy, m, scale=-1.0)
                banks.give(b, nw)
                yield
            b = banks.take()
            for h in range(4):
                m = mm(b.t[0:C, h * P:(h + 1) * P], B["xT"][0:C, h, 0:C], B["bv"][0:C, h, :], v, gk, *b.after, stop=not real)
                if real:
                    m = mm(b.t[0:C, h * P:(h + 1) * P], B["x"][:, h, :], B["s"][:, h, :], nw, t_s[d], start=False)
            vn = copy("scalar", B["bek"][0:C], b.t[0:C, :].rearrange("p (h c) -> p h c", h=4), m)
            banks.give(b, vn)
            yield
            if real:
                b = banks.take()
                for h in range(4):
                    mm(b.t[:, h * P:(h + 1) * P], B["qdec"][:, h, :], B["s"][:, h, :], *b.after, stop=False)
                    m = mm(b.t[:, h * P:(h + 1) * P], B["qk"][:, h, :], B["bek"][:, h, :], vn, vq, start=False)
                if t_o[t] is None:
                    t_o[t] = copy("vector", o_acc[:, t, :], b.t[:, :], m)
                else:
                    t_o[t] = tt("vector", o_acc[:, t, :], o_acc[:, t, :], b.t[:, :], ALU.add, m)
                banks.give(b, t_o[t])
                if not first:
                    return
            b = banks.take()
            for h in range(4):
                m = mm(b.t[:, h * P:(h + 1) * P], B["kdec"][0:C, h, :], B["bek"][0:C, h, :], gk, vn, *b.after)
            if not real:
                v = copy("vector", B["s"], b.t[:, :].rearrange("p (h c) -> p h c", h=4), m)
            else:
                for h in range(4):
                    v = stt(B["s"][:, h, :], B["s"][:, h, :], e_last[:, h:h + 1], b.t[:, h * P:(h + 1) * P], ALU.mult, ALU.add, m)
            banks.give(b, v)
            t_s[d] = v
            yield

        def delta_rule():
            for order in ((2, 2), (0, 1), (1, 0)):
                live = [chunk(d, order[d], order == (0, 1)) for d in range(2)]
                while live:
                    live = [c for c in live if next(c, "end") != "end"]
                    yield

        op = OutProduct(KT // KW)
        axial = axial_steps()
        for n_round, _ in enumerate(delta_rule()):
            for _ in range(1 if n_round < 12 else 2):
                next(axial, None)
        for _ in axial:
            pass
        delta_end = ("vector", q.sem["vector"], q.count["vector"])
        for _, slot in lent:
            ring.done(slot, delta_end)
        for i in (2, 3):
            op.step(head_halves(i))

        osq = buf[0]["qk"]
        hb = [banks.take() for _ in range(QT)]
        for t in range(QT):
            z_ = z_tok[:, t, :]
            o4 = o_acc[:, t, :].rearrange("p (h c) -> p h c", h=4)
            tt("vector", osq, o4, o4, ALU.mult, t_o[t], t_z)
            s0_, s1_, s2_ = (st2[:, t, 4 * i:4 * i + 4] for i in range(3))
            reduce_(s0_, osq, ALU.add)
            ts("vector", s0_, s0_, 1.0 / P, None, ALU.mult, None)
            rsqrt_col(s1_, s0_, s2_, 1e-6)
            tt("vector", o4, o4, s1_.unsqueeze(2).broadcast_to([P, 4, P]), ALU.mult)
            v = tt("vector", o_acc[:, t, :], o_acc[:, t, :], z_, ALU.mult)
            b = hb[t]
            for h in range(4):
                m2 = turned(b.t[:, h * P:(h + 1) * P], o_acc[:, t, h * P:(h + 1) * P], ident, v, *b.after)
            grp = (slice(None), slice(0, 4), slice(t * P, (t + 1) * P))
            c = split_into(oH[grp], oL[grp], b.t[:, :].rearrange("p (a b) -> p a b", a=4), m2, t_cols_ln,
                           scale=col("dn_norm"))
            banks.give(b, c)
        for i in range(4):
            t_oT[i] = c
        delta_done = c

        ar.at = after_cols
        n_tok = ar.take(QT, D)
        hT = ar.take(KT, SEQ)
        post = ar.take(2, D)
        st3 = ar.take(QT, 16)
        relu_tmp = ar.take(2, 512)
        in_post = [q.load(f"post{i}", post[:, i, :], I[name][0].partition_broadcast(P), delta_done)
                   for i, name in enumerate(("norm_mix_post_2", "norm_mlp_post_2"))]

        def post_norm_residual(op, which, t):
            st = st3[:, t, :]
            for half in range(2):
                s1 = act(n_tok[:, t, half * 512:(half + 1) * 512], op.ys[t][half].t[:, :], ACT.Square, op.m[t],
                         delta_done, accum=st[:, half:half + 1])
            tt("vector", st[:, 2:3], st[:, 0:1], st[:, 1:2], ALU.add, s1)
            ts("vector", st[:, 2:3], st[:, 2:3], 1.0 / D, None, ALU.mult, None)
            rsqrt_col(st[:, 3:4], st[:, 2:3], st[:, 4:5], 1e-6)
            for half in range(2):
                c = slice(half * 512, (half + 1) * 512)
                v = stt(n_tok[:, t, c], op.ys[t][half].t[:, :], st[:, 3:4], post[:, which, c], ALU.mult, ALU.mult,
                        in_post[which])
                banks.give(op.ys[t][half], v)
            return tt("vector", x_tok[:, t, :], x_tok[:, t, :], n_tok[:, t, :], ALU.add)

        for i in (0, 1):
            op.step(head_halves(i))
        t_x, t_n, t_h = [], [], []
        for t in range(QT):
            t_x.append(post_norm_residual(op, 0, t))
            t_n.append(rms_rows(x_tok[:, t, :], t_x[t], n_tok[:, t, :], P, st3[:, t, 8:16], D, 1e-6))
            if t == 0:
                for _ in range(SPLIT_SLOTS):
                    weights.ahead("gpsimd")
        for t in range(QT):
            t_h += to_features(n_tok[:, t, :], t_n[t], hT, (hH, hL), col("mlp_pre", 0, KT), None, t_cols_ln, (delta_done,), t * P)
        uH, uL = hi_lo.at(KT * L2, US * KW, SEQ)
        op = mlp(t_h)
        t_x = [post_norm_residual(op, 1, t) for t in range(QT)]
        out_sem = ctx.enter_context(nc.semaphore("out_stored"))
        for t in range(QT):
            stored = q.dma(lambda e, o=out[0, t * P:(t + 1) * P, :], i_=x_tok[:, t, :]: e.dma_start(o, i_),
                           out_sem, 16 * QT, t_x[t])
        q.stores.append(stored)
        finish(nc, q, ctx)


def finish(nc, q, ctx):
    block = ctx.enter_context(nc.Block())

    @block.sync
    def _(eng):
        q.emit("sync", eng)
        for name, sem, value in q.stores:
            eng.wait_ge(sem, value)

    @block.tensor
    def _(eng):
        q.emit("tensor", eng)

    @block.vector
    def _(eng):
        q.emit("vector", eng)

    @block.scalar
    def _(eng):
        q.emit("scalar", eng)

    @block.gpsimd
    def _(eng):
        q.emit("gpsimd", eng)


INPUTS = [
    "x", "c", "rel_bias", "ada_w", "ada_b", "ln_g", "ln_b", "ev_w_in", "ev_w_out", "nsa_pe_k", "nsa_pe_v",
    "nsa_w1_k", "nsa_w2_k", "nsa_w1_v", "nsa_w2_v", "dsa_kv_norm", "dsa_w_uk", "dsa_w_uv", "od_w_in", "od_w_out",
    "diff_lam", "diff_subln", "mlp_w1", "mlp_w2", "meta_tokens_2", "w_in_2", "conv_w_2", "a_log_2", "dt_bias_2",
    "dn_out_norm_2", "q_norm_2", "k_norm_2", "w_out_2", "norm_mix_pre_2", "norm_mix_post_2", "w_up_2",
    "w_down_2", "norm_mlp_pre_2", "norm_mlp_post_2",
]


def prepare(inputs):
    arrays = {n: np.ascontiguousarray(inputs[n]) for n in INPUTS}
    arrays["bucket_rows"] = bucket_rows()
    arrays["square_masks"] = square_masks()
    arrays["rope_tables"] = rope_tables()
    return arrays


def kernel(**inputs):
    import concourse.bacc as bacc
    from concourse.bass_utils import run_bass_kernel_spmd

    nc = bacc.Bacc("TRN2", target_bir_lowering=False, num_devices=1)
    arrays = prepare(inputs)
    aps = {n: nc.dram_tensor(n, a.shape, mybir.dt.from_np(a.dtype), kind="ExternalInput").ap()
           for n, a in arrays.items()}
    out = nc.dram_tensor("out", (1, SEQ, D), F32, kind="ExternalOutput").ap()
    program(nc, aps, out)
    r = run_bass_kernel_spmd(nc, [arrays], core_ids=[0])
    return r.results[0]["out"]
```
